# Optimizing a Trainium2 kernel written in Bass

```python
import math
import jax, jax.numpy as jnp
from jax import lax
import numpy as np

D_MODEL = 1024
BATCH = 1
SEQ = 256
DEPTH = 2

GRID_W = 64
CTX_LEN = 256

CONV_W = 256
CONV_K = 31
RET_HEADS = 6
RET_DK = 32
RET_DV = 64
RET_W = RET_HEADS * RET_DV
RET_CHUNK = 128
RET_GN_EPS = 1e-5
MLA_HEADS = 6
MLA_Q_RANK = 192
MLA_KV_RANK = 128
MLA_D_NOPE = 64
MLA_D_ROPE = 32
MLA_D_V = 64
MLA_W = MLA_HEADS * MLA_D_V
MLA_SCALE = (MLA_D_NOPE + MLA_D_ROPE) ** -0.5
Q_BLOCK = 128
MIX_W = CONV_W + RET_W + MLA_W
ROPE_DIM = 32
ROPE_PAIRS = ROPE_DIM // 4
ROPE_BASE = 10000.0
N_EXPERTS = 16
N_GROUPS = 4
EXPERTS_PER_GROUP = N_EXPERTS // N_GROUPS
TOP_K = 2
D_EXPERT = 256
EPS = 1e-6

IN_SIZES = (2 * CONV_W, RET_HEADS * RET_DK, RET_HEADS * RET_DK, RET_W, RET_W, RET_W,
            MLA_Q_RANK, MLA_KV_RANK, MLA_D_ROPE)
IN_COLS = 2 * CONV_W + 2 * RET_HEADS * RET_DK + 3 * RET_W + MLA_Q_RANK + MLA_KV_RANK + MLA_D_ROPE

kernel_name = "hymba_conv_retnet_mla_groupmoe_dit"

def rmsnorm(x, w):
    xf = x.astype(jnp.float32)
    y = xf * lax.rsqrt(jnp.mean(xf * xf, axis=-1, keepdims=True) + EPS)
    return (y * w.astype(jnp.float32)).astype(x.dtype)

def layernorm(x, w, b):
    xf = x.astype(jnp.float32)
    mu = jnp.mean(xf, axis=-1, keepdims=True)
    var = jnp.mean(jnp.square(xf - mu), axis=-1, keepdims=True)
    y = (xf - mu) * lax.rsqrt(var + EPS)
    return (y * w.astype(jnp.float32) + b.astype(jnp.float32)).astype(x.dtype)

def modulate(h, shift, scale):
    return h * (1.0 + scale) + shift

def split_cols(p, sizes):
    offs = np.cumsum(sizes)[:-1].tolist()
    return jnp.split(p, offs, axis=-1)

def rope_tables(rows):
    r, cl = jnp.meshgrid(jnp.arange(rows, dtype=jnp.float32),
                         jnp.arange(GRID_W, dtype=jnp.float32), indexing="ij")
    r = r.reshape(-1)
    cl = cl.reshape(-1)
    inv = ROPE_BASE ** (-jnp.arange(ROPE_PAIRS, dtype=jnp.float32) / ROPE_PAIRS)
    ar = r[:, None, None] * inv
    ac = cl[:, None, None] * inv
    return (jnp.cos(ar), jnp.sin(ar), jnp.cos(ac), jnp.sin(ac))

def apply_rope(x, tabs):
    cos_r, sin_r, cos_c, sin_c = tabs
    m = x.shape[-1] // 4

    def rot(seg, cos, sin):
        a, b = seg[..., :m], seg[..., m:]
        return jnp.concatenate([a * cos - b * sin, a * sin + b * cos], axis=-1)

    y = jnp.concatenate([rot(x[..., :2 * m], cos_r, sin_r), rot(x[..., 2 * m:], cos_c, sin_c)], axis=-1)
    return y.astype(x.dtype)

def conformer_conv(u2, dw, db, ln_w, ln_b):
    a, g = jnp.split(u2, 2, axis=-1)
    u = a * jax.nn.sigmoid(g)
    y = lax.conv_general_dilated(
        u, dw[:, None, :], window_strides=(1,),
        padding=[(CONV_K // 2, CONV_K // 2)],
        dimension_numbers=("NWC", "WIO", "NWC"),
        feature_group_count=CONV_W) + db
    y = layernorm(y, ln_w, ln_b)
    return jax.nn.silu(y)

def retention_chunked(q, k, v, gamma, r0, with_output):
    B_, L, H, dk = q.shape
    dv = v.shape[-1]
    n = L // RET_CHUNK
    qb = q.reshape(B_, n, RET_CHUNK, H, dk)
    kb = k.reshape(B_, n, RET_CHUNK, H, dk)
    vb = v.reshape(B_, n, RET_CHUNK, H, dv)
    log_g = jnp.log(gamma.astype(jnp.float32))
    idx = jnp.arange(RET_CHUNK, dtype=jnp.float32)
    zeta = jnp.exp((RET_CHUNK - 1 - idx)[:, None] * log_g[None, :])
    d_state = jnp.einsum("bnjhd,bnjhe,jh->bnhde", kb, vb, zeta).astype(jnp.float32)
    g_chunk = jnp.exp(RET_CHUNK * log_g)[None, :, None, None]

    def step(r, dr):
        return g_chunk * r + dr, r

    r_final, r_prev = lax.scan(step, r0, jnp.moveaxis(d_state, 1, 0))
    if not with_output:
        return None, r_final
    r_prev = jnp.moveaxis(r_prev, 0, 1)
    diff = idx[:, None] - idx[None, :]
    dmask = jnp.where(diff[None] >= 0,
                      jnp.exp(jnp.maximum(diff, 0.0)[None] * log_g[:, None, None]), 0.0)
    scores = jnp.einsum("bnihd,bnjhd->bnhij", qb, kb) * dmask
    inner = jnp.einsum("bnhij,bnjhe->bnihe", scores, vb)
    xi = jnp.exp((idx + 1.0)[:, None] * log_g[None, :])
    cross = jnp.einsum("bnihd,bnhde->bnihe", qb, r_prev) * xi[None, None, :, :, None]
    return (inner + cross).reshape(B_, L, H, dv), r_final

def retention_dir(q, k, v, gamma, r0, reverse, with_output):
    if reverse:
        q, k, v = jnp.flip(q, 1), jnp.flip(k, 1), jnp.flip(v, 1)
    out, r = retention_chunked(q, k, v, gamma, r0, with_output)
    if reverse and out is not None:
        out = jnp.flip(out, 1)
    return out, r

def head_groupnorm(y):
    yf = y.astype(jnp.float32)
    mu = jnp.mean(yf, axis=-1, keepdims=True)
    var = jnp.mean(jnp.square(yf - mu), axis=-1, keepdims=True)
    return (yf - mu) * lax.rsqrt(var + RET_GN_EPS)

def retention_mixer(pc, pl, tabs, need_ctx):
    def heads(parts, rotate):
        q, k, v, gf, gb = parts
        B_, L, _ = q.shape
        q = q.reshape(B_, L, RET_HEADS, RET_DK)
        k = k.reshape(B_, L, RET_HEADS, RET_DK) * (RET_DK ** -0.5)
        v = v.reshape(B_, L, RET_HEADS, RET_DV)
        gf = gf.reshape(B_, L, RET_HEADS, RET_DV)
        gb = gb.reshape(B_, L, RET_HEADS, RET_DV)
        if rotate:
            q = apply_rope(q, tabs)
            k = apply_rope(k, tabs)
        return q, k, v, gf, gb

    qc, kc, vc, gfc, gbc = heads(pc, False)
    ql, kl, vl, gfl, gbl = heads(pl, True)
    B_, L = ql.shape[0], ql.shape[1]
    gamma_f = 1.0 - 2.0 ** (-5.0 - jnp.arange(RET_HEADS, dtype=jnp.float32))
    gamma_b = gamma_f[::-1]
    r0 = jnp.zeros((B_, RET_HEADS, RET_DK, RET_DV), jnp.float32)
    outs_l, outs_c = [], []
    for reverse, gamma, gate_l, gate_c in ((False, gamma_f, gfl, gfc), (True, gamma_b, gbl, gbc)):
        oc, rc = retention_dir(qc, kc, vc, gamma, r0, reverse, need_ctx)
        ol, _ = retention_dir(ql, kl, vl, gamma, rc, reverse, True)
        outs_l.append(jax.nn.silu(gate_l) * head_groupnorm(ol).astype(gate_l.dtype))
        if need_ctx:
            outs_c.append(jax.nn.silu(gate_c) * head_groupnorm(oc).astype(gate_c.dtype))
    out_l = (outs_l[0] + outs_l[1]).reshape(B_, L, RET_W)
    if not need_ctx:
        return None, out_l
    out_c = (outs_c[0] + outs_c[1]).reshape(B_, qc.shape[1], RET_W)
    return out_c, out_l

def mla_attend(qn, qr, kn, kr, v):
    s = jnp.einsum("bqhd,bkhd->bhqk", qn, kn) + jnp.einsum("bqhd,bkd->bhqk", qr, kr)
    p = jax.nn.softmax(s.astype(jnp.float32) * MLA_SCALE, axis=-1).astype(v.dtype)
    return jnp.einsum("bhqk,bkhd->bqhd", p, v)

def mla_mixer(pc, pl, q_norm_w, w_uq, kv_norm_w, w_ukv, tabs, need_ctx):
    def project(parts, rotate, with_q):
        cq, ckv, kr = parts
        B_, L, _ = ckv.shape
        kv = (rmsnorm(ckv, kv_norm_w) @ w_ukv).reshape(B_, L, MLA_HEADS, MLA_D_NOPE + MLA_D_V)
        kn, v = kv[..., :MLA_D_NOPE], kv[..., MLA_D_NOPE:]
        kr = kr[:, :, None, :]
        if rotate:
            kr = apply_rope(kr, tabs)
        kr = kr[:, :, 0, :]
        if not with_q:
            return None, None, kn, kr, v
        q = (rmsnorm(cq, q_norm_w) @ w_uq).reshape(B_, L, MLA_HEADS, MLA_D_NOPE + MLA_D_ROPE)
        qn, qr = q[..., :MLA_D_NOPE], q[..., MLA_D_NOPE:]
        if rotate:
            qr = apply_rope(qr, tabs)
        return qn, qr, kn, kr, v

    qn_c, qr_c, kn_c, kr_c, v_c = project(pc, False, need_ctx)
    qn_l, qr_l, kn_l, kr_l, v_l = project(pl, True, True)
    kn_all = jnp.concatenate([kn_c, kn_l], axis=1)
    kr_all = jnp.concatenate([kr_c, kr_l], axis=1)
    v_all = jnp.concatenate([v_c, v_l], axis=1)
    B_, L = qn_l.shape[0], qn_l.shape[1]
    nb = L // Q_BLOCK

    def to_blocks(t):
        return jnp.moveaxis(t.reshape(B_, nb, Q_BLOCK, *t.shape[2:]), 1, 0)

    out_l = lax.map(lambda qb: mla_attend(qb[0], qb[1], kn_all, kr_all, v_all),
                    (to_blocks(qn_l), to_blocks(qr_l)))
    out_l = jnp.moveaxis(out_l, 0, 1).reshape(B_, L, MLA_W)
    if not need_ctx:
        return None, out_l
    out_c = mla_attend(qn_c, qr_c, kn_c, kr_c, v_c).reshape(B_, qn_c.shape[1], MLA_W)
    return out_c, out_l

def mixing_sublayer(h_c, h_l, w_in, conv_dw, conv_b, conv_ln_w, conv_ln_b,
                    q_norm_w, w_uq, kv_norm_w, w_ukv, w_out, tabs, need_ctx):
    parts_l = split_cols(h_l @ w_in, IN_SIZES)
    parts_c = split_cols(h_c @ w_in, IN_SIZES)
    conv_l = conformer_conv(parts_l[0], conv_dw, conv_b, conv_ln_w, conv_ln_b)
    ret_c, ret_l = retention_mixer(parts_c[1:6], parts_l[1:6], tabs, need_ctx)
    mla_c, mla_l = mla_mixer(parts_c[6:], parts_l[6:], q_norm_w, w_uq, kv_norm_w, w_ukv, tabs, need_ctx)
    o_l = jnp.concatenate([conv_l, ret_l.astype(h_l.dtype), mla_l], axis=-1) @ w_out
    if not need_ctx:
        return None, o_l
    conv_c = conformer_conv(parts_c[0], conv_dw, conv_b, conv_ln_w, conv_ln_b)
    o_c = jnp.concatenate([conv_c, ret_c.astype(h_c.dtype), mla_c], axis=-1) @ w_out
    return o_c, o_l

def grouped_moe(h, router_w, router_bias, w_gate, w_up, w_down):
    B_, L, D = h.shape
    t = h.reshape(B_ * L, D)
    aff = jax.nn.sigmoid((t @ router_w).astype(jnp.float32))
    sel = aff + router_bias.astype(jnp.float32)
    grp = sel.reshape(-1, N_GROUPS, EXPERTS_PER_GROUP)
    group_score = jnp.sum(lax.top_k(grp, 2)[0], axis=-1)
    best_group = jnp.argmax(group_score, axis=-1)
    in_group = (jnp.arange(N_EXPERTS) // EXPERTS_PER_GROUP)[None, :] == best_group[:, None]
    _, idx = lax.top_k(jnp.where(in_group, sel, -jnp.inf), TOP_K)
    w = jnp.take_along_axis(aff, idx, axis=-1)
    w = w / jnp.sum(w, axis=-1, keepdims=True)
    gates = jnp.sum(jax.nn.one_hot(idx, N_EXPERTS, dtype=jnp.float32) * w[..., None], axis=1)
    out = jnp.zeros((t.shape[0], D), jnp.float32)
    for e in range(N_EXPERTS):
        he = jax.nn.silu(t @ w_gate[e]) * (t @ w_up[e])
        out = out + gates[:, e:e + 1] * (he @ w_down[e])
    return out.astype(h.dtype).reshape(B_, L, D)

def setup_inputs(seed: int = 0) -> dict:
    key = jax.random.key(seed)
    ks = jax.random.split(key, 24)
    f32 = jnp.float32

    def nrm(k, shape, scale):
        return jax.random.normal(k, shape, f32) * scale

    D = D_MODEL
    return {
        "x": nrm(ks[0], (BATCH, SEQ, D), 1.0),
        "c": nrm(ks[1], (BATCH, D), 1.0),
        "ctx": nrm(ks[2], (BATCH, CTX_LEN, D), 1.0),
        "c_ctx": nrm(ks[3], (D,), 1.0),
        "ada_w": nrm(ks[4], (DEPTH, D, 6 * D), 0.5 * D ** -0.5),
        "ada_b": nrm(ks[5], (DEPTH, 6 * D), 0.02),
        "norm1_w": 1.0 + nrm(ks[6], (DEPTH, D), 0.05),
        "norm2_w": 1.0 + nrm(ks[7], (DEPTH, D), 0.05),
        "w_in": nrm(ks[8], (DEPTH, D, IN_COLS), D ** -0.5),
        "conv_dw": nrm(ks[9], (DEPTH, CONV_K, CONV_W), CONV_K ** -0.5),
        "conv_b": nrm(ks[10], (DEPTH, CONV_W), 0.02),
        "conv_ln_w": 1.0 + nrm(ks[11], (DEPTH, CONV_W), 0.05),
        "conv_ln_b": nrm(ks[12], (DEPTH, CONV_W), 0.02),
        "mla_q_norm_w": 1.0 + nrm(ks[13], (DEPTH, MLA_Q_RANK), 0.05),
        "mla_w_uq": nrm(ks[14], (DEPTH, MLA_Q_RANK, MLA_HEADS * (MLA_D_NOPE + MLA_D_ROPE)), MLA_Q_RANK ** -0.5),
        "mla_kv_norm_w": 1.0 + nrm(ks[15], (DEPTH, MLA_KV_RANK), 0.05),
        "mla_w_ukv": nrm(ks[16], (DEPTH, MLA_KV_RANK, MLA_HEADS * (MLA_D_NOPE + MLA_D_V)), MLA_KV_RANK ** -0.5),
        "w_out": nrm(ks[17], (DEPTH, MIX_W, D), MIX_W ** -0.5),
        "router_w": nrm(ks[18], (D, N_EXPERTS), D ** -0.5),
        "router_bias": nrm(ks[19], (N_EXPERTS,), 0.01),
        "moe_w_gate": nrm(ks[20], (DEPTH, N_EXPERTS, D, D_EXPERT), D ** -0.5),
        "moe_w_up": nrm(ks[21], (DEPTH, N_EXPERTS, D, D_EXPERT), D ** -0.5),
        "moe_w_down": nrm(ks[22], (DEPTH, N_EXPERTS, D_EXPERT, D), D_EXPERT ** -0.5),
        "final_norm_w": 1.0 + nrm(ks[23], (D,), 0.05),
    }

def reference(x, c, ctx, c_ctx, ada_w, ada_b, norm1_w, norm2_w, w_in, conv_dw, conv_b,
              conv_ln_w, conv_ln_b, mla_q_norm_w, mla_w_uq, mla_kv_norm_w, mla_w_ukv, w_out,
              router_w, router_bias, moe_w_gate, moe_w_up, moe_w_down, final_norm_w):
    L = x.shape[1]
    ROWS = L // GRID_W
    tabs = rope_tables(ROWS)
    silu_c = jax.nn.silu(c)
    silu_cc = jax.nn.silu(c_ctx)
    xc = ctx
    for l in range(DEPTH):
        need_ctx = l < DEPTH - 1
        mod_l = (silu_c @ ada_w[l] + ada_b[l])[:, None, :]
        mod_c = (silu_cc @ ada_w[l] + ada_b[l])[None, None, :]
        sh1, sc1, g1, sh2, sc2, g2 = jnp.split(mod_l, 6, axis=-1)
        csh1, csc1, cg1, csh2, csc2, cg2 = jnp.split(mod_c, 6, axis=-1)

        h_l = modulate(rmsnorm(x, norm1_w[l]), sh1, sc1)
        h_c = modulate(rmsnorm(xc, norm1_w[l]), csh1, csc1)
        o_c, o_l = mixing_sublayer(h_c, h_l, w_in[l], conv_dw[l], conv_b[l], conv_ln_w[l], conv_ln_b[l],
                                   mla_q_norm_w[l], mla_w_uq[l], mla_kv_norm_w[l], mla_w_ukv[l],
                                   w_out[l], tabs, need_ctx)
        x = x + g1 * o_l
        h_l = modulate(rmsnorm(x, norm2_w[l]), sh2, sc2)
        x = x + g2 * grouped_moe(h_l, router_w, router_bias, moe_w_gate[l], moe_w_up[l], moe_w_down[l])
        if need_ctx:
            xc = xc + cg1 * o_c
            h_c = modulate(rmsnorm(xc, norm2_w[l]), csh2, csc2)
            xc = xc + cg2 * grouped_moe(h_c, router_w, router_bias, moe_w_gate[l], moe_w_up[l], moe_w_down[l])
    return rmsnorm(x, final_norm_w)


_drawn_inputs = setup_inputs


def setup_inputs(seed=0):
    import zlib

    import numpy as np

    out = dict(_drawn_inputs(seed))
    spreads = {}
    factors = {'conv_b': 8.0,
     'conv_ln_w': 2.747,
     'conv_ln_b': 5.76,
     'mla_q_norm_w': 8.0,
     'mla_kv_norm_w': 8.0}
    for name, (base, spread) in spreads.items():
        noise = np.random.default_rng([zlib.crc32(name.encode()), seed]).standard_normal(out[name].shape)
        drawn = base * np.exp(spread * noise) if base else spread * noise
        out[name] = __import__('jax').numpy.asarray(drawn.astype(out[name].dtype))
    for name, factor in factors.items():
        out[name] = (out[name] * factor).astype(out[name].dtype)
    return out
```

```python
from contextlib import ExitStack

import concourse.bass as bass
from concourse import mybir

P = 128
D = 1024
DEPTH = 2
SEQ = 256
NT = 4
KD = D // P
CONV_W, CONV_K = 256, 31
HEADS, RET_DK, RET_DV = 6, 32, 64
CHUNK_PAD = SEQ + CONV_K - 1
Q_RANK, KV_RANK, D_NOPE, D_ROPE, D_V = 192, 128, 64, 32, 64
D_QK = D_NOPE + D_ROPE
MLA_SCALE = float(D_QK) ** -0.5
N_EXPERTS, EPG, D_EXPERT = 16, 4, 256
N_GROUPS = N_EXPERTS // EPG
EPS, GN_EPS = 1e-6, 1e-5
QKW, VW = 2 * HEADS * RET_DK, HEADS * RET_DV
LATW = Q_RANK + KV_RANK + D_ROPE
BIG = 1e30
F32 = mybir.dt.float32
BF16 = mybir.dt.bfloat16
ACT = mybir.ActivationFunctionType
ALU = mybir.AluOpType
AX_X = mybir.AxisListType.X

NQ = [4, 2]
CONV_U, QK_U, V_U, LAT_U, GF_U, GB_U = range(6)
UNIT_COLS = [(0, 512), (512, QKW), (896, VW), (2048, LATW), (1280, VW), (1664, VW)]
N_WSLOT = 3
SCALE_Q, SHIFT_Q, GATE_Q = 0, 1, 2
MOD_UNITS = [(SHIFT_Q, 0), (SHIFT_Q, 1), (SCALE_Q, 0), (SCALE_Q, 1), (GATE_Q, 0), (GATE_Q, 1)]


def gamma(h):
    return 1.0 - 2.0 ** (-5.0 - h)


def plan():
    units, mods = [], []
    for l in range(DEPTH):
        for a in range(2):
            if a:
                units += [("in", l, u) for u in range(6)] + [("out", l, c) for c in range(2)]
            units += [("ada", l, a, u) for u in range(6)]
            for u, (q, half) in enumerate(MOD_UNITS):
                both = l == 0 or (a == 0 and q != GATE_Q)
                mods += [(l, a, u, s) for s in range(2 if both else 1)]
    return units, mods


def build(nc, dram, out):
    units, mods = plan()
    unit_at = {u: n for n, u in enumerate(units)}
    mod_at = {m: n for n, m in enumerate(mods)}
    units_per_layer = len(units) // DEPTH
    ada_per_layer = 12
    moe = [(l, r, e) for l in range(DEPTH) for r in range(NQ[l] // 2) for e in range(N_EXPERTS)]
    moe_at = {m: n for n, m in enumerate(moe)}
    moe_before = [0, NQ[0] // 2 * N_EXPERTS, len(moe)]

    def before(l, per):
        return sum(per[:l])

    with ExitStack() as ctx:
        def sb(name, shape, dt=F32):
            return ctx.enter_context(nc.sbuf_tensor(name, shape, dt))

        def sem(name):
            return ctx.enter_context(nc.semaphore(name))

        ps = ctx.enter_context(nc.psum_tensor("ps", [P, 8, 512], F32))

        wring = sb("wring", [P, N_WSLOT, 4096])
        x = sb("x", [P, NT, D])
        hT_buf = sb("hT_buf", [P, 4096])
        mod = sb("mod", [P, 3, 2, D])
        work1 = sb("work1", [P, 4096])
        decay = sb("decay", [P, 2, HEADS, 384])
        work2 = sb("work2", [P, 2176])
        convT = sb("convT", [P, 2, 512])
        v_ret = sb("v_ret", [P, NT, VW])
        gate_act = sb("gate_act", [P, 2, NT, VW])
        v_mla = sb("v_mla", [P, NT, HEADS * D_V])
        o_mla = sb("o_mla", [P, NT, HEADS * D_V])
        stage = sb("stage", [P, 1536])
        tmp = sb("tmp", [P, 768])
        w_uq = sb("w_uq", [P, 2, HEADS * D_QK])
        w_ukv = sb("w_ukv", [P, HEADS * P])
        cqT = sb("cqT", [P, 2, 512])
        ckvT = sb("ckvT", [P, 512])
        sel = sb("sel", [P, 2, P])
        ident = sb("ident", [P, P])
        ones_mean = sb("ones_mean", [P, P])
        rope = sb("rope", [P, 2, 2, D_ROPE])
        router_w = sb("router_w", [P, KD, N_EXPERTS])
        junk = sb("junk", [P, Q_RANK], BF16)
        c_raw = sb("c_raw", [P, 2, KD])
        c_pad = sb("c_pad", [P, KD, 32])
        conv_vec = sb("conv_vec", [P, 2, CONV_K + 3])
        dw = conv_vec[:, :, 0:CONV_K]
        q_norm = sb("q_norm", [P, 2])
        kv_norm = sb("kv_norm", [P, 1])
        eps_col = sb("eps_col", [P, 1])
        half_neg = sb("half_neg", [P, 12])
        rstd = sb("rstd", [P, NT])
        lat_sumsq = sb("lat_sumsq", [P, NT, 2])
        lat_rstd = sb("lat_rstd", [P, NT, 2])
        gn_mean = sb("gn_mean", [P, 2, 12])
        gn_rstd = sb("gn_rstd", [P, 2, 12])
        neg_max = sb("neg_max", [P, 2])
        prob_sum = sb("prob_sum", [P, NT, HEADS])
        aff = sb("aff", [P, NT, N_EXPERTS])
        r_bias = sb("r_bias", [P, N_EXPERTS])
        rank16 = sb("rank16", [P, N_EXPERTS])
        gates = sb("gates", [P, NT, N_EXPERTS])

        hT = hT_buf[:, :].rearrange("p (k n) -> p k n", k=KD)
        oT = hT_buf[:, 0:6 * 512].rearrange("p (k n) -> p k n", k=6)
        norm_w = work1[:, 0:D]
        mod_rows = work1[:, D:2 * D].rearrange("p (b n) -> p b n", b=2)
        h_tok = work1[:, 2 * D:4 * D].rearrange("p (b n) -> p b n", b=2)
        conv_sig = h_tok[:, :, 0:512]
        qkT = work1[:, 0:2048].rearrange("p (f n) -> p f n", f=4)
        masked = work1[:, 2048:4096].rearrange("p (f j n) -> p f j n", f=2, j=4)
        qT = work1[0:D_QK, 0:HEADS * 512].rearrange("p (h n) -> p h n", h=HEADS)
        KT = mod[0:D_QK, 0:2, :, :].rearrange("p a b n -> p (a b n)")[:, 0:HEADS * 512].rearrange(
            "p (h n) -> p h n", h=HEADS)
        conv_in = work2[:, 0:2 * 2 * CHUNK_PAD].rearrange("p (c s n) -> p c s n", c=2, s=2)
        conv_sq = work2[:, 0:1024].rearrange("p (c n) -> p c n", c=2)
        conv_std = work2[:, 0:512]
        acc = work2[:, 1144:2168].rearrange("p (c n) -> p c n", c=2)
        q_stage = work2[:, 0:1152].rearrange("p (b n) -> p b n", b=2)
        probs = work2[:, 0:1024].rearrange("p (b n) -> p b n", b=2)
        probsT = work2[:, 1024:2048].rearrange("p (b n) -> p b n", b=2)
        y_moe = work2[:, 0:2048].rearrange("p (c n) -> p c n", c=2)
        ada_bias = stage[:, 0:1024].rearrange("p (b n) -> p b n", b=2)
        qk_tok = stage[:, 0:NT * QKW].rearrange("p (t n) -> p t n", t=NT)
        lat_tok = stage[:, 0:NT * LATW].rearrange("p (t n) -> p t n", t=NT)
        gn_y = stage[:, 0:1536].rearrange("p (i g n) -> p i g n", i=2, g=12)
        square_junk = tmp[:, 0:512].bitcast(BF16)
        silu_buf = v_ret[:, :, :].rearrange("p t n -> p (t n)")[:, 0:512].rearrange("p (b n) -> p b n", b=2)
        he_buf = v_ret[:, :, :].rearrange("p t n -> p (t n)")[:, 512:1024].rearrange("p (b n) -> p b n", b=2)
        heT_buf = v_ret[:, :, :].rearrange("p t n -> p (t n)")[:, 1024:1536].rearrange("p (b n) -> p b n", b=2)
        gu = [wring[:, j, :].rearrange("p (k n) -> p k n", k=KD) for j in range(2)]
        dn = [wring[:, 2, j * 2048:(j + 1) * 2048].rearrange("p (f n) -> p f n", f=2) for j in range(2)]

        def unit_view(n):
            kind = units[n][0]
            cols = UNIT_COLS[units[n][2]][1] if kind == "in" else 512
            return wring[:, n % N_WSLOT, 0:KD * cols].rearrange("p (k n) -> p k n", k=KD)

        s_const = sem("s_const")
        s_small = sem("s_small")
        s_wslot = [sem(f"s_wslot{j}") for j in range(N_WSLOT)]
        s_bias = [sem(f"s_bias{j}") for j in range(2)]
        s_normw = sem("s_normw")
        s_gu = [sem(f"s_gu{j}") for j in range(2)]
        s_dn = [sem(f"s_dn{j}") for j in range(2)]
        s_ones = sem("s_ones")
        s_cpad = sem("s_cpad")
        s_bias_zero = sem("s_bias_zero")
        s_ada_part = sem("s_ada_part")
        s_ada_rows = sem("s_ada_rows")
        s_ada_bc = sem("s_ada_bc")
        s_mod = sem("s_mod")
        s_sumsq = sem("s_sumsq")
        s_rstd = sem("s_rstd")
        s_scaled = sem("s_scaled")
        s_h = sem("s_h")
        s_hT_ps = sem("s_hT_ps")
        s_hT = sem("s_hT")
        s_conv_ps = sem("s_conv_ps")
        s_sig = sem("s_sig")
        s_glu = sem("s_glu")
        s_pad = sem("s_pad")
        s_proj_ps = sem("s_proj_ps")
        s_proj = sem("s_proj")
        s_qk_rope = sem("s_qk_rope")
        s_qkT_ps = sem("s_qkT_ps")
        s_qkT = sem("s_qkT")
        s_lat_sq = sem("s_lat_sq")
        s_lat_rstd = sem("s_lat_rstd")
        s_lat_norm = sem("s_lat_norm")
        s_latT_ps = sem("s_latT_ps")
        s_latT = sem("s_latT")
        s_kr = sem("s_kr")
        s_taps = sem("s_taps")
        s_cmean_ps = sem("s_cmean_ps")
        s_ccent = sem("s_ccent")
        s_csq = sem("s_csq")
        s_cvar_ps = sem("s_cvar_ps")
        s_cstd = sem("s_cstd")
        s_cnorm = sem("s_cnorm")
        s_convT = sem("s_convT")
        s_ret_ps = sem("s_ret_ps")
        s_mask = [sem("s_mask_f"), sem("s_mask_b")]
        s_ret_pv = [sem("s_ret_pv_f"), sem("s_ret_pv_b")]
        s_gn_y = sem("s_gn_y")
        s_gn_cent = sem("s_gn_cent")
        s_gn_sq = sem("s_gn_sq")
        s_gn_var = sem("s_gn_var")
        s_gn_rstd = sem("s_gn_rstd")
        s_gn_norm = sem("s_gn_norm")
        s_ret_out = sem("s_ret_out")
        s_mla_ps = sem("s_mla_ps")
        s_mla_sb = sem("s_mla_sb")
        s_q_rope = sem("s_q_rope")
        s_qT_ps = sem("s_qT_ps")
        s_qT = sem("s_qT")
        s_score_ps = sem("s_score_ps")
        s_max = sem("s_max")
        s_exp = sem("s_exp")
        s_pT_ps = sem("s_pT_ps")
        s_pT = sem("s_pT")
        s_pv = sem("s_pv")
        s_mla_out = sem("s_mla_out")
        s_oT_ps = sem("s_oT_ps")
        s_oT = sem("s_oT")
        s_out_ps = sem("s_out_ps")
        s_x1 = sem("s_x1")
        s_logit_ps = sem("s_logit_ps")
        s_aff = sem("s_aff")
        s_gates = sem("s_gates")
        s_up_ps = sem("s_up_ps")
        s_silu = sem("s_silu")
        s_he = sem("s_he")
        s_heT_ps = sem("s_heT_ps")
        s_heT = sem("s_heT")
        s_y_ps = sem("s_y_ps")
        s_y = sem("s_y")
        s_x2 = sem("s_x2")
        s_final = sem("s_final")
        s_out = sem("s_out")
        s_dve = sem("s_dve")
        s_pool = sem("s_pool")
        s_act = sem("s_act")

        N_CONST = 12
        N_SMALL = 5
        NORM_TILES = [4 + NQ[0], 4 + NQ[1]]

        def norm_base(l, a):
            return sum(NORM_TILES[:l]) + (0, 4, 4 + NQ[l])[a] if l < DEPTH else sum(NORM_TILES)

        PROJ_JOBS = [[(u, t) for u in (QK_U, V_U, LAT_U, GF_U, GB_U) for t in range(NT if u < GF_U else NQ[l])]
                     for l in range(DEPTH)]
        per_proj = [len(j) for j in PROJ_JOBS]
        MLA_JOBS = [[("k", h) for h in range(HEADS)] + [("v", t) for t in range(NT)] +
                    [("q", t, half) for t in range(NQ[l]) for half in range(2)] for l in range(DEPTH)]
        per_mla = [len(j) for j in MLA_JOBS]
        ATTN = [[(t, h) for t in range(NQ[l]) for h in range(HEADS)] for l in range(DEPTH)]
        per_attn = [len(j) for j in ATTN]
        RET_PASSES = [NQ[l] // 2 for l in range(DEPTH)]
        per_ret = [HEADS * r for r in RET_PASSES]
        SMALL_LOADS = 16 * N_SMALL

        def w_wait(eng, n):
            eng.wait_ge(s_wslot[n % N_WSLOT], 16 * (n // N_WSLOT + 1))

        block = ctx.enter_context(nc.Block())

        def freed(n):
            kind, l = units[n][:2]
            if kind == "ada":
                return s_ada_part, l * ada_per_layer + units[n][2] * 6 + units[n][3] + 1
            if kind == "out":
                return s_out_ps, before(l, [2 * q for q in NQ]) + (units[n][2] + 1) * NQ[l]
            if units[n][2] == CONV_U:
                return s_conv_ps, 4 * (l + 1)
            done = [i for i, (u, t) in enumerate(PROJ_JOBS[l]) if u == units[n][2]][-1] + 1
            return s_proj_ps, before(l, per_proj) + done

        @block.sync
        def _(sp):
            def load_unit(n):
                u = units[n]
                l = u[1]
                if n - N_WSLOT >= units_per_layer * l or (l == 0 and n >= N_WSLOT):
                    sp.wait_ge(*freed(n - N_WSLOT))
                elif l > 0:
                    sp.wait_ge(s_y_ps, 2 * moe_before[l])
                if u[0] == "ada":
                    a, j = u[2], u[3]
                    q, half = MOD_UNITS[j]
                    col = (a * 3 + (1, 0, 2)[q]) * D + half * 512
                    src = dram["ada_w"][l].rearrange("(p k) n -> p k n", k=KD)[:, :, col:col + 512]
                    b = l * ada_per_layer + a * 6 + j
                    if j == 0:
                        sp.wait_ge(s_bias_zero, 2 * l + a + 1)
                    if j == 2:
                        if l or a:
                            sp.wait_ge(s_mod, mod_at[(l, a, 0, 0)])
                        if a:
                            sp.wait_ge(s_score_ps, before(l + 1, per_attn))
                        sp.dma_start(norm_w, dram[("norm1_w", "norm2_w")[a]][l:l + 1, :].to_broadcast([P, D])).then_inc(s_normw, 16)
                    if b >= 2:
                        sp.wait_ge(s_ada_rows, b - 1)
                    sp.dma_start(ada_bias[0:2, b % 2, :],
                                 dram["ada_b"][l:l + 1, col:col + 512].to_broadcast([2, 512])).then_inc(s_bias[b % 2], 16)
                elif u[0] == "in":
                    c0, w = UNIT_COLS[u[2]]
                    src = dram["w_in"][l].rearrange("(p k) n -> p k n", k=KD)[:, :, c0:c0 + w]
                else:
                    src = dram["w_out"][l].rearrange("(k p) n -> p k n", p=P)[:, :, u[2] * 512:u[2] * 512 + 512]
                sp.dma_start(unit_view(n), src).then_inc(s_wslot[n % N_WSLOT], 16)

            def load_expert(m):
                l, r, e = moe[m]
                j = m % 2
                if m - moe_before[l] < 2:
                    sp.wait_ge(s_ada_part, ada_per_layer * (l + 1))
                else:
                    sp.wait_ge(s_up_ps, 2 * (m - 1))
                for i, name in enumerate(("moe_w_gate", "moe_w_up")):
                    sp.dma_start(gu[j][:, :, i * D_EXPERT:(i + 1) * D_EXPERT],
                                 dram[name][l, e].rearrange("(p k) n -> p k n", k=KD)).then_inc(s_gu[j], 16)
                if m - moe_before[l] >= 2:
                    sp.wait_ge(s_y_ps, 2 * (m - 1))
                sp.dma_start(dn[j], dram["moe_w_down"][l, e].rearrange("(p f) n -> p f n", f=2)).then_inc(s_dn[j], 16)

            for l in range(DEPTH):
                if l:
                    sp.wait_ge(s_convT, 2 * l)
                    sp.wait_ge(s_mla_ps, before(l, per_mla))
                for dst, src in (
                    (w_uq[0:96, :, :], dram["mla_w_uq"][l].rearrange("(k p) n -> p k n", p=96)),
                    (w_ukv[:, :], dram["mla_w_ukv"][l]),
                    (conv_vec[:, :, :], dram["conv_cols"][l]),
                    (q_norm[0:96, :], dram["q_norm_cols"][l]),
                    (kv_norm[:, :], dram["mla_kv_norm_w"][l].rearrange("(p k) -> p k", k=1)),
                ):
                    sp.dma_start(dst, src).then_inc(s_small, 16)
                for n in range(units_per_layer * l, units_per_layer * (l + 1)):
                    load_unit(n)
                for m in range(moe_before[l], moe_before[l + 1]):
                    load_expert(m)
            sp.wait_ge(s_mod, len(mods))
            sp.dma_start(norm_w, dram["final_norm_w"].rearrange("(a n) -> a n", a=1).to_broadcast([P, D])).then_inc(s_normw, 16)
            for t in range(2):
                sp.wait_ge(s_final, t + 1)
                sp.dma_start(out[0, t * P:(t + 1) * P, :], h_tok[:, (norm_base(DEPTH, 0) + t) % 2, :]).then_inc(s_out, 16)
            sp.wait_ge(s_out, 32)

        def tok(t):
            return slice(t * P, (t + 1) * P)

        def key_tile(s, slot):
            return 2 + slot if slot < 2 else 2 * s + slot - 2

        def lat_evacs(l, t):
            per = lambda a, b: sum(4 if i < NQ[a] else 2 for i in range(b))
            return sum(per(a, NT) for a in range(l)) + per(l, t)

        @block.tensor
        def _(pe):
            T = nc.tensor

            def modulation(l, a):
                def broadcast(u):
                    n = l * ada_per_layer + a * 6 + u
                    pe.wait_ge(s_ada_rows, n + 1)
                    for s in range(2):
                        if (l, a, u, s) in mod_at:
                            b = mod_at[(l, a, u, s)]
                            if b >= 2:
                                pe.wait_ge(s_mod, b - 1)
                            T.matmul(ps[:, 2 + b % 2, :], sel[:, s, :], mod_rows[:, n % 2, :],
                                     start=True, stop=True).then_inc(s_ada_bc, 1)

                if a:
                    pe.wait_ge(s_exp, before(l + 1, per_attn))
                    pe.wait_ge(s_oT, 2 * before(l + 1, NQ))
                elif l:
                    pe.wait_ge(s_he, 2 * moe_before[l])
                    pe.wait_ge(s_heT, 2 * moe_before[l])
                for u in range(6):
                    n = l * ada_per_layer + a * 6 + u
                    w_wait(pe, unit_at[("ada", l, a, u)])
                    w = unit_view(unit_at[("ada", l, a, u)])
                    if n >= 2:
                        pe.wait_ge(s_ada_rows, n - 1)
                    for step in range(2):
                        for strip in range(4):
                            k = 2 * strip + step
                            last = T.matmul(ps[32 * strip:32 * strip + 32, n % 2, :], c_pad[:, k, :], w[:, k, :],
                                            start=(step == 0), stop=(step == 1),
                                            tile_position=(0, 32 * strip))
                    last.then_inc(s_ada_part, 1)
                    if u >= 1:
                        broadcast(u - 1)
                broadcast(5)

            def transpose_h(l, a, tiles):
                for t in range(tiles):
                    i = norm_base(l, a) + t
                    pe.wait_ge(s_h, i + 1)
                    h = h_tok[:, i % 2, :].rearrange("q (p k) -> q k p", k=KD)
                    for b in range(2):
                        if i >= 1:
                            pe.wait_ge(s_hT, 2 * (i - 1) + b + 1)
                        for j in range(4):
                            last = T.transpose(ps[:, 6 + b, j * P:(j + 1) * P], h[:, 4 * b + j, :], ident[:, :])
                        last.then_inc(s_hT_ps, 1)

            def project_conv(l):
                n = unit_at[("in", l, CONV_U)]
                w_wait(pe, n)
                w = unit_view(n)
                pe.wait_ge(s_hT, 2 * (norm_base(l, 0) + 4))
                pe.wait_ge(s_ada_rows, l * ada_per_layer + 6)
                pe.wait_ge(s_mod, mod_at[(l, 1, 0, 0)])
                width = NQ[l] * P
                for m in (2, 3, 0, 1):
                    for k in range(KD):
                        last = T.matmul(ps[:, m, 0:width], w[:, k, tok(m)], hT[:, k, 0:width],
                                        start=(k == 0), stop=(k == KD - 1))
                    last.then_inc(s_conv_ps, 1)

            def project(l, us):
                for i, (u, t) in enumerate(PROJ_JOBS[l]):
                    if u not in us:
                        continue
                    j = before(l, per_proj) + i
                    n = unit_at[("in", l, u)]
                    if t == 0:
                        w_wait(pe, n)
                    w = unit_view(n)
                    if i >= 2:
                        pe.wait_ge(s_proj, j - 1)
                    for k in range(KD):
                        last = T.matmul(ps[:, 4 + j % 2, 0:UNIT_COLS[u][1]], hT[:, k, tok(t)], w[:, k, :],
                                        start=(k == 0), stop=(k == KD - 1))
                    last.then_inc(s_proj_ps, 1)

            def transpose_qk(l):
                for t in range(NT):
                    if t < 2:
                        pe.wait_ge(s_qk_rope, 2 * l + t + 1)
                    else:
                        pe.wait_ge(s_proj, before(l, per_proj) + t + 1)
                        pe.wait_ge(s_qkT, 2 * (NT * l + t - 1))
                    for f, (c0, w) in enumerate(((0, 128), (128, 64), (192, 128), (320, 64))):
                        if f < 2 and t >= NQ[l]:
                            continue
                        last = T.transpose(ps[0:w, 6 + t % 2, f * P:(f + 1) * P], qk_tok[:, t, c0:c0 + w], ident[:, :])
                    last.then_inc(s_qkT_ps, 1)

            def transpose_latents(l):
                pe.wait_ge(s_qkT, 2 * NT * (l + 1))
                for t in range(NT):
                    pe.wait_ge(s_lat_norm, NT * l + t + 1)
                    if t >= 2:
                        pe.wait_ge(s_latT, lat_evacs(l, t - 1))
                    for f, (c0, w) in enumerate(((0, 96), (96, 96), (192, 128), (320, 32))):
                        if f < 2 and t >= NQ[l]:
                            continue
                        last = T.transpose(ps[0:w, 6 + t % 2, f * P:(f + 1) * P], lat_tok[:, t, c0:c0 + w], ident[:, :])
                    last.then_inc(s_latT_ps, 1)

            def retention(l, s):
                r0 = before(l, per_ret) + s * HEADS

                def scores(h):
                    r = r0 + h
                    if s == 0 and h < 2:
                        pe.wait_ge((s_glu, s_sig)[h], 2 * (l + 1))
                    elif s == 1 and h < 2:
                        pe.wait_ge((s_ccent, s_cstd)[h], (2 * (l + 1), l + 1)[h])
                    else:
                        pe.wait_ge(s_mask[0], r - 1)
                        pe.wait_ge(s_mask[1], r - 1)
                    q0, side = 32 * (h % 4), h // 4
                    qs = qkT[q0:q0 + 32, side, s * SEQ:(s + 1) * SEQ]
                    for slot in (range(4) if s == 0 else (2, 3)):
                        bank = 2 * (h % 2) + slot // 2 if s == 0 else h % 2
                        last = T.matmul(ps[:, bank, slot % 2 * SEQ:(slot % 2 + 1) * SEQ],
                                        qkT[q0:q0 + 32, 2 + side, tok(key_tile(s, slot))], qs, start=True, stop=True,
                                        tile_position=(q0, 0))
                    last.then_inc(s_ret_ps, 1)

                def sums(h, f):
                    r = r0 + h
                    pe.wait_ge(s_mask[f], r + 1)
                    for i in range(2):
                        slots = ([0, 1] if s == 0 else []) + [j for j in (2, 3) if (j - 2 <= i if f == 0 else j - 2 >= i)]
                        for j in slots:
                            last = T.matmul(ps[:, 4 + 2 * i + f, h * RET_DV:(h + 1) * RET_DV],
                                            masked[:, f, j, tok(i)], v_ret[:, key_tile(s, j), h * RET_DV:(h + 1) * RET_DV],
                                            start=(j == slots[0]), stop=(j == slots[-1]))
                    last.then_inc(s_ret_pv[f], 1)

                scores(0)
                if s == 0:
                    pe.wait_ge(s_proj, before(l + 1, per_proj))
                    pe.wait_ge(s_latT, lat_evacs(l, NT))
                else:
                    pe.wait_ge(s_gn_y, 4 * (before(l, RET_PASSES) + s))
                for h in range(HEADS):
                    if h + 1 < HEADS:
                        scores(h + 1)
                    sums(h, 0)
                    sums(h, 1)

            def conv_mean(l):
                for f in range(2):
                    pe.wait_ge(s_mask[f], before(l, per_ret) + HEADS)
                pe.wait_ge(s_taps, 2 * CONV_K * (l + 1))
                for c in range(2):
                    last = T.matmul(ps[:, 0, 0:NQ[l] * P], ones_mean[:, :], acc[:, c, 0:NQ[l] * P],
                                    start=(c == 0), stop=(c == 1))
                last.then_inc(s_cmean_ps, 1)

            def conv_var(l):
                pe.wait_ge(s_csq, 2 * (l + 1))
                for c in range(2):
                    last = T.matmul(ps[:, 1, 0:NQ[l] * P], ones_mean[:, :], conv_sq[:, c, 0:NQ[l] * P],
                                    start=(c == 0), stop=(c == 1))
                last.then_inc(s_cvar_ps, 1)

            def mla_job(l, i):
                job = MLA_JOBS[l][i]
                j = before(l, per_mla) + i
                bank = 2 + j % 2
                if i >= 2:
                    pe.wait_ge(s_mla_sb, j - 1)
                if job[0] == "k":
                    h = job[1]
                    last = T.matmul(ps[0:D_NOPE, bank, :], w_ukv[:, h * P:h * P + D_NOPE], ckvT[:, :],
                                    start=True, stop=True)
                elif job[0] == "v":
                    vs = w_ukv[:, :].rearrange("p (h n) -> p h n", h=HEADS)[:, :, D_NOPE:]
                    last = T.matmul(ps[:, bank, 0:HEADS * D_V], ckvT[:, tok(job[1])], vs, start=True, stop=True)
                else:
                    _, t, half = job
                    for k in range(2):
                        last = T.matmul(ps[:, bank, 0:288], cqT[0:96, k, tok(t)],
                                        w_uq[0:96, k, half * 288:(half + 1) * 288], start=(k == 0), stop=(k == 1))
                last.then_inc(s_mla_ps, 1)

            def transpose_q(l, t):
                i = before(l, NQ) + t
                if t < 2:
                    pe.wait_ge(s_q_rope, 2 * l + t + 1)
                else:
                    pe.wait_ge(s_mla_sb, before(l, per_mla) + 10 + 2 * (t + 1))
                if t == 0:
                    pe.wait_ge(s_gn_y, 4 * before(l + 1, RET_PASSES))
                else:
                    pe.wait_ge(s_qT, 2 * i)
                for h in range(HEADS):
                    last = T.transpose(ps[0:D_QK, 6 + h // 4, h % 4 * P:(h % 4 + 1) * P],
                                       q_stage[:, t % 2, h * D_QK:(h + 1) * D_QK], ident[:, :])
                last.then_inc(s_qT_ps, 1)

            def attention(l):
                items = ATTN[l]
                n0 = before(l, per_attn)
                pe.wait_ge(s_kr, l + 1)
                pe.wait_ge(s_mla_sb, before(l + 1, per_mla))
                pe.wait_ge(s_cstd, l + 1)
                for f in range(2):
                    pe.wait_ge(s_mask[f], before(l + 1, per_ret))
                pe.wait_ge(s_qT, 2 * before(l + 1, NQ))

                def scores(i):
                    t, h = items[i]
                    if i >= 2:
                        pe.wait_ge(s_exp, n0 + i - 1)
                    keys = slice(0, 512) if t < 2 else slice(SEQ, 512)
                    T.matmul(ps[:, (n0 + i) % 2, 0:keys.stop - keys.start], qT[:, h, tok(t)], KT[:, h, keys],
                             start=True, stop=True).then_inc(s_score_ps, 1)

                def turn(i):
                    t, h = items[i]
                    n = n0 + i
                    pe.wait_ge(s_exp, n + 1)
                    if i >= 2:
                        pe.wait_ge(s_pT, n - 1)
                    for j in range(4 if t < 2 else 2):
                        last = T.transpose(ps[:, 2 + n % 2, tok(j)], probs[:, n % 2, tok(j)], ident[:, :])
                    last.then_inc(s_pT_ps, 1)

                def values(i):
                    t, h = items[i]
                    n = n0 + i
                    pe.wait_ge(s_pT, n + 1)
                    tiles = range(4) if t < 2 else range(2, 4)
                    for j, kt in enumerate(tiles):
                        last = T.matmul(ps[:, 4 + t, h * D_V:(h + 1) * D_V], probsT[:, n % 2, tok(j)],
                                        v_mla[:, kt, h * D_V:(h + 1) * D_V], start=(j == 0), stop=(kt == 3))
                    last.then_inc(s_pv, 1)

                scores(0)
                for i in range(len(items)):
                    if i + 1 < len(items):
                        scores(i + 1)
                    turn(i)
                    if i:
                        values(i - 1)
                values(len(items) - 1)

            def project_out(l):
                i0 = before(l, NQ)
                pe.wait_ge(s_pT, before(l + 1, per_attn))
                for t in range(NQ[l]):
                    for b in range(2):
                        if b == 0:
                            pe.wait_ge(s_ret_out, i0 + t + 1)
                        else:
                            pe.wait_ge(s_mla_out, i0 + t + 1)
                        if t:
                            pe.wait_ge(s_oT, 2 * (i0 + t - 1) + b + 1)
                        o = o_mla[:, t, :] if b else gate_act[:, 0, t, :]
                        for j in range(3):
                            last = T.transpose(ps[:, 2 + b, tok(j)], o[:, tok(j)], ident[:, :])
                        last.then_inc(s_oT_ps, 1)
                pe.wait_ge(s_convT, 2 * (l + 1))
                for c in range(2):
                    n = unit_at[("out", l, c)]
                    w_wait(pe, n)
                    w = unit_view(n)
                    for t in range(NQ[l]):
                        i = c * NQ[l] + t
                        j = 2 * i0 + i
                        if c == 0:
                            pe.wait_ge(s_oT, 2 * (i0 + t + 1))
                        if i >= 4:
                            pe.wait_ge(s_x1, j - 3)
                        for k in range(KD):
                            lhs = convT[:, k, tok(t)] if k < 2 else oT[:, k - 2, tok(t)]
                            last = T.matmul(ps[:, 4 + i % 4, :], lhs, w[:, k, :], start=(k == 0), stop=(k == KD - 1))
                        last.then_inc(s_out_ps, 1)

            def route(l):
                pe.wait_ge(s_hT, 2 * (norm_base(l, 1) + NQ[l]))
                for t in range(NQ[l]):
                    for k in range(KD):
                        last = T.matmul(ps[:, 4, t * N_EXPERTS:(t + 1) * N_EXPERTS], hT[:, k, tok(t)], router_w[:, k, :],
                                        start=(k == 0), stop=(k == KD - 1))
                last.then_inc(s_logit_ps, 1)

            def experts(l):
                first, end = 2 * moe_before[l], 2 * moe_before[l + 1]

                def up(i):
                    m, c = i // 2, i % 2
                    _, r, e = moe[m]
                    if c == 0:
                        pe.wait_ge(s_gu[m % 2], 32 * (m // 2 + 1))
                    if i >= first + 2:
                        pe.wait_ge(s_he, i - 1)
                    for k in range(KD):
                        last = T.matmul(ps[:, i % 2, :], hT[:, k, tok(2 * r + c)], gu[m % 2][:, k, :],
                                        start=(k == 0), stop=(k == KD - 1))
                    last.then_inc(s_up_ps, 1)

                def turn(i):
                    pe.wait_ge(s_he, i + 1)
                    if i >= first + 2:
                        pe.wait_ge(s_heT, i - 1)
                    he = he_buf[:, i % 2, :].rearrange("q (p f) -> q f p", f=2)
                    for f in range(2):
                        last = T.transpose(ps[:, 2 + i % 2, tok(f)], he[:, f, :], ident[:, :])
                    last.then_inc(s_heT_ps, 1)

                def down(i):
                    m, c = i // 2, i % 2
                    _, r, e = moe[m]
                    pe.wait_ge(s_heT, i + 1)
                    if c == 0:
                        pe.wait_ge(s_dn[m % 2], 16 * (m // 2 + 1))
                    if e % EPG == 0:
                        g = m // EPG
                        if g:
                            pe.wait_ge(s_y, 2 * (g - 1) + c + 1)
                    for half in range(2):
                        for f in range(2):
                            last = T.matmul(ps[:, 4 + 2 * c + half, :], heT_buf[:, i % 2, tok(f)],
                                            dn[m % 2][:, f, half * 512:(half + 1) * 512],
                                            start=(e % EPG == 0 and f == 0), stop=(e % EPG == EPG - 1 and f == 1))
                    last.then_inc(s_y_ps, 1)

                pe.wait_ge(s_ada_rows, ada_per_layer * (l + 1))
                pe.wait_ge(s_mod, mod_at[(l + 1, 0, 0, 0)] if l + 1 < DEPTH else len(mods))
                pe.wait_ge(s_aff, l + 1)
                for i in range(first, end + 2):
                    if i < end:
                        up(i)
                    if first <= i - 1 < end:
                        turn(i - 1)
                    if i - 2 >= first:
                        down(i - 2)

            pe.wait_ge(s_const, 16 * N_CONST)
            pe.wait_ge(s_cpad, 2)
            pe.wait_ge(s_ones, 1)
            for l in range(DEPTH):
                modulation(l, 0)
                if l:
                    pe.wait_ge(s_y, 2 * moe_before[l] // EPG)
                transpose_h(l, 0, NT)
                project_conv(l)
                project(l, (QK_U, V_U))
                transpose_qk(l)
                project(l, (LAT_U, GF_U, GB_U))
                transpose_latents(l)
                retention(l, 0)
                conv_mean(l)
                pe.wait_ge(s_small, 16 * N_SMALL * (l + 1))
                for i in range(10):
                    mla_job(l, i)
                conv_var(l)
                if RET_PASSES[l] == 2:
                    retention(l, 1)
                for t in range(NQ[l]):
                    mla_job(l, 10 + 2 * t)
                    mla_job(l, 11 + 2 * t)
                    if t:
                        transpose_q(l, t - 1)
                transpose_q(l, NQ[l] - 1)
                attention(l)
                pe.wait_ge(s_mla_out, before(l + 1, NQ))
                project_out(l)
                modulation(l, 1)
                pe.wait_ge(s_x1, 2 * before(l + 1, NQ))
                transpose_h(l, 1, NQ[l])
                route(l)
                experts(l)

        @block.scalar
        def _(act):
            S = nc.scalar
            steps = [0]

            def chain(ins):
                steps[0] += 1
                ins.then_inc(s_act, 1)
                act.wait_ge(s_act, steps[0])

            for dst, src in (
                (x[:, 0:2, :], dram["x"][0].rearrange("(t p) n -> p t n", p=P)),
                (x[:, 2:4, :], dram["ctx"][0].rearrange("(t p) n -> p t n", p=P)),
                (c_raw[:, 0, :], dram["c"][0].rearrange("(p k) -> p k", k=KD)),
                (c_raw[:, 1, :], dram["c_ctx"].rearrange("(p k) -> p k", k=KD)),
                (ident[:, :], dram["const_ident"]),
                (sel[:, :, :], dram["const_sel"]),
                (rope[:, :, :, :], dram["const_rope"]),
                (decay[:, 0, :, :], dram["const_decay"][:, 0, :, :]),
                (decay[:, 1, :, :], dram["const_decay"][:, 1, :, :]),
                (rank16[:, :], dram["const_rank"]),
                (router_w[:, :, :], dram["router_w"].rearrange("(p k) n -> p k n", k=KD)),
                (r_bias[:, :], dram["router_bias"].rearrange("(a n) -> a n", a=1).to_broadcast([P, N_EXPERTS])),
            ):
                act.dma_start(dst, src).then_inc(s_const, 16)

            def square_sums(l, a, tiles):
                for t in range(tiles):
                    i = norm_base(l, a) + t
                    if i:
                        act.wait_ge(s_sumsq, i)
                    S.activation(square_junk, x[:, t, :], ACT.Square, accum_out=rstd[:, t:t + 1]).then_inc(s_sumsq, 1)

            def copy_hT(l, a, tiles):
                for t in range(tiles):
                    i = norm_base(l, a) + t
                    for b in range(2):
                        act.wait_ge(s_hT_ps, 2 * i + b + 1)
                        S.activation(hT[:, 4 * b:4 * b + 4, tok(t)], ps[:, 6 + b, :].rearrange("p (k n) -> p k n", k=4),
                                     ACT.Copy).then_inc(s_hT, 1)

            def project(l, us):
                dst = {QK_U: qk_tok, V_U: v_ret, LAT_U: lat_tok}
                for i, (u, t) in enumerate(PROJ_JOBS[l]):
                    if u not in us:
                        continue
                    j = before(l, per_proj) + i
                    act.wait_ge(s_proj_ps, j + 1)
                    got = ps[:, 4 + j % 2, 0:UNIT_COLS[u][1]]
                    if u in dst:
                        S.activation(dst[u][:, t, :], got, ACT.Copy).then_inc(s_proj, 1)
                    else:
                        S.activation(gate_act[:, u - GF_U, t, :], got, ACT.Silu).then_inc(s_proj, 1)
                    if u == LAT_U:
                        act.wait_ge(s_proj, j + 1)
                        if NT * l + t:
                            act.wait_ge(s_lat_sq, NT * l + t)
                        if t < NQ[l]:
                            chain(S.activation(junk[:, :], lat_tok[:, t, 0:Q_RANK], ACT.Square,
                                               accum_out=lat_sumsq[:, t, 0:1]))
                        S.activation(junk[:, 0:KV_RANK], lat_tok[:, t, Q_RANK:Q_RANK + KV_RANK], ACT.Square,
                                     accum_out=lat_sumsq[:, t, 1:2]).then_inc(s_lat_sq, 1)

            def copy_qkT(l):
                for t in range(NT):
                    act.wait_ge(s_qkT_ps, NT * l + t + 1)
                    f0 = 0 if t < NQ[l] else 2
                    got = ps[:, 6 + t % 2, :].rearrange("p (f n) -> p f n", f=4)
                    S.activation(qkT[:, f0::2, tok(t)], got[:, f0::2, :], ACT.Copy).then_inc(s_qkT, 1)
                    S.activation(qkT[0:64, f0 + 1::2, tok(t)], got[0:64, f0 + 1::2, :], ACT.Copy).then_inc(s_qkT, 1)

            def copy_latT(l):
                act.wait_ge(s_small, 16 * N_SMALL * (l + 1))
                for t in range(NT):
                    act.wait_ge(s_latT_ps, NT * l + t + 1)
                    bank = 6 + t % 2
                    if t < NQ[l]:
                        for k in range(2):
                            S.activation(cqT[0:96, k, tok(t)], ps[0:96, bank, k * P:(k + 1) * P], ACT.Copy,
                                         scale=q_norm[0:96, k:k + 1]).then_inc(s_latT, 1)
                    S.activation(ckvT[:, tok(t)], ps[:, bank, 2 * P:3 * P], ACT.Copy,
                                 scale=kv_norm[:, 0:1]).then_inc(s_latT, 1)
                    S.activation(KT[D_NOPE:D_QK, 0, tok(t)], ps[0:D_ROPE, bank, 3 * P:4 * P], ACT.Copy).then_inc(s_latT, 1)

            def groupnorm_in(l, s):
                g = before(l, RET_PASSES) + s
                for f in range(2):
                    act.wait_ge(s_ret_pv[f], HEADS * (g + 1))
                for i in range(2):
                    if g:
                        act.wait_ge(s_ret_out, 2 * (g - 1) + i + 1)
                    for f in range(2):
                        S.activation(gn_y[:, i, 6 * f:6 * f + 6, :],
                                     ps[:, 4 + 2 * i + f, 0:VW].rearrange("p (h n) -> p h n", h=HEADS),
                                     ACT.Copy).then_inc(s_gn_y, 1)

            def groupnorm_sq(l, s):
                for i in range(2):
                    g = 2 * (before(l, RET_PASSES) + s) + i
                    act.wait_ge(s_gn_cent, g + 1)
                    if g:
                        act.wait_ge(s_gn_var, g)
                    S.activation(tmp[:, :].rearrange("p (g n) -> p g n", g=12), gn_y[:, i, :, :],
                                 ACT.Square).then_inc(s_gn_sq, 1)

            def conv_sq_act(l):
                for c in range(2):
                    act.wait_ge(s_ccent, 2 * l + c + 1)
                    S.activation(conv_sq[:, c, 0:NQ[l] * P], acc[:, c, 0:NQ[l] * P], ACT.Square).then_inc(s_csq, 1)

            def conv_std_act(l):
                act.wait_ge(s_cvar_ps, l + 1)
                S.activation(conv_std[:, 0:NQ[l] * P], ps[:, 1, 0:NQ[l] * P], ACT.Sqrt, bias=eps_col[:, 0:1]).then_inc(s_cstd, 1)

            def conv_out(l):
                for c in range(2):
                    act.wait_ge(s_cnorm, 2 * l + c + 1)
                    S.activation(convT[:, c, 0:NQ[l] * P], acc[:, c, 0:NQ[l] * P], ACT.Silu,
                                 scale=conv_vec[:, c, CONV_K + 1:CONV_K + 2], bias=conv_vec[:, c, CONV_K + 2:CONV_K + 3]).then_inc(s_convT, 1)

            def mla_copy(l, i):
                job = MLA_JOBS[l][i]
                j = before(l, per_mla) + i
                bank = 2 + j % 2
                act.wait_ge(s_mla_ps, j + 1)
                if job[0] == "k":
                    S.activation(KT[0:D_NOPE, job[1], :], ps[0:D_NOPE, bank, :], ACT.Copy).then_inc(s_mla_sb, 1)
                elif job[0] == "v":
                    S.activation(v_mla[:, job[1], :], ps[:, bank, 0:HEADS * D_V], ACT.Copy).then_inc(s_mla_sb, 1)
                else:
                    _, t, half = job
                    if t >= 2:
                        act.wait_ge(s_qT_ps, before(l, NQ) + t - 1)
                    if t == 0:
                        act.wait_ge(s_cnorm, 2 * (l + 1))
                    S.activation(q_stage[:, t % 2, half * 288:(half + 1) * 288], ps[:, bank, 0:288],
                                 ACT.Copy).then_inc(s_mla_sb, 1)

            def copy_qT(l, t):
                act.wait_ge(s_qT_ps, before(l, NQ) + t + 1)
                for b, n in ((0, 4), (1, 2)):
                    S.activation(qT[:, 4 * b:4 * b + n, tok(t)],
                                 ps[0:D_QK, 6 + b, 0:n * P].rearrange("p (h n) -> p h n", h=n),
                                 ACT.Copy, scale=MLA_SCALE).then_inc(s_qT, 1)

            def softmax(l):
                n0 = before(l, per_attn)
                for i, (t, h) in enumerate(ATTN[l]):
                    n = n0 + i
                    w = 512 if t < 2 else SEQ
                    act.wait_ge(s_max, n + 1)
                    if i >= 2:
                        act.wait_ge(s_pT_ps, n - 1)
                    S.activation(probs[:, n % 2, 0:w], ps[:, n % 2, 0:w], ACT.Exp, bias=neg_max[:, n % 2:n % 2 + 1],
                                 accum_out=prob_sum[:, t, h:h + 1]).then_inc(s_exp, 1)

            def copy_oT(l):
                for t in range(NQ[l]):
                    for b in range(2):
                        i = 2 * (before(l, NQ) + t) + b
                        act.wait_ge(s_oT_ps, i + 1)
                        S.activation(oT[:, 3 * b:3 * b + 3, tok(t)],
                                     ps[:, 2 + b, 0:3 * P].rearrange("p (k n) -> p k n", k=3), ACT.Copy).then_inc(s_oT, 1)

            def experts(l):
                first, end = 2 * moe_before[l], 2 * moe_before[l + 1]
                for i in range(first, end + 1):
                    if i < end:
                        act.wait_ge(s_up_ps, i + 1)
                        if i >= first + 2:
                            act.wait_ge(s_he, i - 1)
                        S.activation(silu_buf[:, i % 2, :], ps[:, i % 2, 0:D_EXPERT], ACT.Silu).then_inc(s_silu, 1)
                    if i - 1 >= first:
                        j = i - 1
                        act.wait_ge(s_heT_ps, j + 1)
                        if j >= first + 2:
                            act.wait_ge(s_y_ps, j - 1)
                        S.activation(heT_buf[:, j % 2, :], ps[:, 2 + j % 2, 0:D_EXPERT], ACT.Copy).then_inc(s_heT, 1)

            act.wait_ge(s_const, 16 * N_CONST)
            act.wait_ge(s_ones, 1)
            for s in range(2):
                S.activation(c_pad[:, :, s], c_raw[:, s, :], ACT.Silu).then_inc(s_cpad, 1)
            for l in range(DEPTH):
                if l:
                    act.wait_ge(s_x2, before(l, NQ))
                square_sums(l, 0, NT)
                copy_hT(l, 0, NT)
                for j in range(2):
                    act.wait_ge(s_conv_ps, 4 * l + j + 1)
                    S.activation(conv_sig[:, j, 0:NQ[l] * P], ps[:, 2 + j, 0:NQ[l] * P], ACT.Sigmoid).then_inc(s_sig, 1)
                project(l, (QK_U, V_U))
                copy_qkT(l)
                project(l, (LAT_U, GF_U, GB_U))
                copy_latT(l)
                groupnorm_in(l, 0)
                conv_sq_act(l)
                for i in range(10):
                    mla_copy(l, i)
                conv_std_act(l)
                groupnorm_sq(l, 0)
                conv_out(l)
                if RET_PASSES[l] == 2:
                    groupnorm_in(l, 1)
                    groupnorm_sq(l, 1)
                for t in range(NQ[l]):
                    mla_copy(l, 10 + 2 * t)
                    mla_copy(l, 11 + 2 * t)
                    if t:
                        copy_qT(l, t - 1)
                copy_qT(l, NQ[l] - 1)
                softmax(l)
                copy_oT(l)
                act.wait_ge(s_x1, 2 * before(l + 1, NQ))
                square_sums(l, 1, NQ[l])
                copy_hT(l, 1, NQ[l])
                act.wait_ge(s_logit_ps, l + 1)
                S.activation(aff[:, 0:NQ[l], :], ps[:, 4, 0:NQ[l] * N_EXPERTS].rearrange("p (t n) -> p t n", n=N_EXPERTS),
                             ACT.Sigmoid).then_inc(s_aff, 1)
                experts(l)
            act.wait_ge(s_x2, before(DEPTH, NQ))
            square_sums(DEPTH, 0, 2)

        @block.vector
        def _(dve):
            V = nc.vector
            steps = [0]

            def chain(ins):
                steps[0] += 1
                ins.then_inc(s_dve, 1)
                dve.wait_ge(s_dve, steps[0])

            def modulation(l, a):
                def bcast(u):
                    q, half = MOD_UNITS[u]
                    for s in range(2):
                        if (l, a, u, s) not in mod_at:
                            continue
                        b = mod_at[(l, a, u, s)]
                        dve.wait_ge(s_ada_bc, b + 1)
                        dst = mod[:, q, s, half * 512:(half + 1) * 512]
                        if q == SCALE_Q:
                            dve.wait_ge(s_normw, 16 * (2 * l + a + 1))
                            V.scalar_tensor_tensor(out=dst, in0=ps[:, 2 + b % 2, :], scalar=1.0,
                                                   in1=norm_w[:, half * 512:(half + 1) * 512],
                                                   op0=ALU.add, op1=ALU.mult).then_inc(s_mod, 1)
                        else:
                            V.tensor_copy(dst, ps[:, 2 + b % 2, :]).then_inc(s_mod, 1)

                for u in range(6):
                    n = l * ada_per_layer + a * 6 + u
                    dve.wait_ge(s_ada_part, n + 1)
                    dve.wait_ge(s_bias[n % 2], 16 * (n // 2 + 1))
                    if u >= 2:
                        dve.wait_ge(s_ada_bc, mod_at[(l, a, u - 1, 0)])
                    V.tensor_tensor(mod_rows[:, n % 2, :], ps[:, n % 2, :], ada_bias[:, n % 2, :],
                                    ALU.add).then_inc(s_ada_rows, 1)
                    if u >= 1:
                        bcast(u - 1)
                bcast(5)

            def scale_tiles(l, a, tiles):
                dve.wait_ge(s_mod, mod_at[(l, a, 4, 0)])
                for t in range(tiles):
                    i = norm_base(l, a) + t
                    dve.wait_ge(s_rstd, i + 1)
                    if i >= 2:
                        dve.wait_ge(s_hT_ps, 2 * (i - 1))
                    V.scalar_tensor_tensor(out=h_tok[:, i % 2, :], in0=x[:, t, :], scalar=rstd[:, t:t + 1],
                                           in1=mod[:, SCALE_Q, t // 2, :], op0=ALU.mult, op1=ALU.mult).then_inc(s_scaled, 1)

            def glu(l):
                dve.wait_ge(s_pad, l + 1)
                dve.wait_ge(s_conv_ps, 4 * (l + 1))
                dve.wait_ge(s_sig, 2 * (l + 1))
                n = NQ[l] // 2
                for c in range(2):
                    V.tensor_tensor(conv_in[:, c, 0:n, CONV_K // 2:CONV_K // 2 + SEQ],
                                    ps[:, c, 0:n * SEQ].rearrange("p (s n) -> p s n", s=n),
                                    conv_sig[:, c, 0:n * SEQ].rearrange("p (s n) -> p s n", s=n),
                                    ALU.mult).then_inc(s_glu, 1)

            def rotate(view, t, heads, done, value):
                n = heads * D_ROPE
                straight = tmp[:, 0:n].rearrange("p (h r) -> p h r", h=heads)
                swapped = tmp[:, 384:384 + n].rearrange("p (h g b r) -> p h g b r", h=heads, g=2, b=2)
                src = view.rearrange("p h (g b r) -> p h g b r", g=2, b=2)
                sin = rope[:, t, 1, :].rearrange("p (h g b r) -> p h g b r", h=1, g=2, b=2)
                cos = rope[:, t, 0, :].rearrange("p (h r) -> p h r", h=1)
                V.tensor_tensor(straight, view, cos.to_broadcast([P, heads, D_ROPE]), ALU.mult)
                for b in range(2):
                    last = V.tensor_tensor(swapped[:, :, :, b, :], src[:, :, :, 1 - b, :],
                                           sin[:, :, :, b, :].to_broadcast([P, heads, 2, 8]), ALU.mult)
                chain(last)
                V.tensor_tensor(view, straight, tmp[:, 384:384 + n].rearrange("p (h r) -> p h r", h=heads),
                                ALU.add).then_inc(done, 1)
                dve.wait_ge(done, value)

            def rope_qk(l):
                for t in range(2):
                    dve.wait_ge(s_proj, before(l, per_proj) + t + 1)
                    rotate(qk_tok[:, t, :].rearrange("p (h r) -> p h r", h=12), t, 12, s_qk_rope, 2 * l + t + 1)

            def norm_latents(l):
                for t in range(NT):
                    dve.wait_ge(s_lat_rstd, NT * l + t + 1)
                    if t < NQ[l]:
                        V.tensor_scalar(lat_tok[:, t, 0:Q_RANK], lat_tok[:, t, 0:Q_RANK], lat_rstd[:, t, 0:1], None, ALU.mult)
                    ckv = lat_tok[:, t, Q_RANK:Q_RANK + KV_RANK]
                    last = V.tensor_scalar(ckv, ckv, lat_rstd[:, t, 1:2], None, ALU.mult)
                    if t < 2:
                        rotate(lat_tok[:, t, Q_RANK + KV_RANK:LATW].rearrange("p (h r) -> p h r", h=1), t, 1,
                               s_lat_norm, NT * l + t + 1)
                    else:
                        last.then_inc(s_lat_norm, 1)

            def taps(l):
                n = NQ[l] // 2
                dve.wait_ge(s_glu, 2 * (l + 1))
                dve.wait_ge(s_small, 16 * N_SMALL * (l + 1))
                for k in range(CONV_K):
                    for c in range(2):
                        i = 2 * (CONV_K * l + k) + c
                        src = conv_in[:, c, 0:n, k:k + SEQ]
                        dst = acc[:, c, 0:n * SEQ].rearrange("p (s n) -> p s n", s=n)
                        if k == 0:
                            V.tensor_scalar(dst, src, dw[:, c, 0:1], conv_vec[:, c, CONV_K:CONV_K + 1], ALU.mult, ALU.add).then_inc(s_taps, 1)
                        else:
                            dve.wait_ge(s_taps, i - 1)
                            V.scalar_tensor_tensor(out=dst, in0=src, scalar=dw[:, c, k:k + 1], in1=dst,
                                                   op0=ALU.mult, op1=ALU.add).then_inc(s_taps, 1)

            def masks(l, s):
                k = RET_DK ** -0.5
                for h in range(HEADS):
                    r = before(l, per_ret) + s * HEADS + h
                    dve.wait_ge(s_ret_ps, r + 1)
                    far = [gamma(h) ** P, gamma(HEADS - 1 - h) ** P]

                    def own(slot):
                        bank = 2 * (h % 2) + slot // 2 if s == 0 else h % 2
                        return ps[:, bank, slot % 2 * SEQ:(slot % 2 + 1) * SEQ]

                    def decayed(f, slot, cols, t0, scale):
                        n = cols.stop - cols.start
                        return V.scalar_tensor_tensor(out=masked[:, f, slot, cols], in0=own(slot)[:, cols],
                                                      scalar=float(scale * k), in1=decay[:, f, h, t0:t0 + n],
                                                      op0=ALU.mult, op1=ALU.mult)

                    whole = slice(0, SEQ)
                    if r:
                        dve.wait_ge(s_ret_pv[0], r)
                    if s == 0:
                        decayed(0, 0, whole, P, far[0])
                        decayed(0, 1, whole, P, 1.0)
                    decayed(0, 2, whole, 0, 1.0)
                    decayed(0, 3, slice(P, SEQ), 0, 1.0).then_inc(s_mask[0], 1)
                    if r:
                        dve.wait_ge(s_ret_pv[1], r)
                    if s == 0:
                        decayed(1, 0, whole, 0, 1.0)
                        decayed(1, 1, whole, 0, far[1])
                    decayed(1, 3, whole, P, 1.0)
                    decayed(1, 2, slice(0, P), SEQ, 1.0).then_inc(s_mask[1], 1)

            def groupnorm(l, s):
                g0 = 2 * (before(l, RET_PASSES) + s)
                for i in range(2):
                    dve.wait_ge(s_gn_y, 2 * (g0 + i + 1))
                    chain(V.tensor_reduce(gn_mean[:, i, :], gn_y[:, i, :, :], AX_X, ALU.add))
                    chain(V.tensor_scalar(gn_mean[:, i, :], gn_mean[:, i, :], 1.0 / RET_DV, None, ALU.mult))
                    V.tensor_tensor(gn_y[:, i, :, :], gn_y[:, i, :, :],
                                    gn_mean[:, i, :].rearrange("p (g n) -> p g n", n=1).to_broadcast([P, 12, RET_DV]),
                                    ALU.subtract).then_inc(s_gn_cent, 1)
                for i in range(2):
                    dve.wait_ge(s_gn_sq, g0 + i + 1)
                    V.tensor_reduce(gn_rstd[:, i, :], tmp[:, :].rearrange("p (g n) -> p g n", g=12), AX_X,
                                    ALU.add).then_inc(s_gn_var, 1)
                for i in range(2):
                    dve.wait_ge(s_gn_rstd, g0 + i + 1)
                    V.tensor_tensor(gn_y[:, i, :, :], gn_y[:, i, :, :],
                                    gn_rstd[:, i, :].rearrange("p (g n) -> p g n", n=1).to_broadcast([P, 12, RET_DV]),
                                    ALU.mult).then_inc(s_gn_norm, 1)

            def conv_centre(l):
                n = NQ[l] * P
                dve.wait_ge(s_cmean_ps, l + 1)
                for c in range(2):
                    V.tensor_tensor(acc[:, c, 0:n], acc[:, c, 0:n], ps[:, 0, 0:n], ALU.subtract).then_inc(s_ccent, 1)

            def conv_scale(l):
                n = NQ[l] * P
                dve.wait_ge(s_cstd, l + 1)
                chain(V.reciprocal(conv_std[:, 0:n], conv_std[:, 0:n]))
                for c in range(2):
                    V.tensor_tensor(acc[:, c, 0:n], acc[:, c, 0:n], conv_std[:, 0:n], ALU.mult).then_inc(s_cnorm, 1)

            def rope_q(l, t):
                dve.wait_ge(s_mla_sb, before(l, per_mla) + 10 + 2 * (t + 1))
                rotate(q_stage[:, t, :].rearrange("p (h r) -> p h r", h=HEADS)[:, :, D_NOPE:], t, HEADS,
                       s_q_rope, 2 * l + t + 1)

            def attention(l):
                n0 = before(l, per_attn)
                items = ATTN[l]

                def row_max(i):
                    t, h = items[i]
                    n = n0 + i
                    dve.wait_ge(s_score_ps, n + 1)
                    V.tensor_reduce(neg_max[:, n % 2:n % 2 + 1], ps[:, n % 2, 0:512 if t < 2 else SEQ], AX_X, ALU.max,
                                    negate=True).then_inc(s_max, 1)

                def copy_pT(i):
                    t, h = items[i]
                    n = n0 + i
                    w = 512 if t < 2 else SEQ
                    dve.wait_ge(s_pT_ps, n + 1)
                    if i >= 2:
                        dve.wait_ge(s_pv, n - 1)
                    V.tensor_copy(probsT[:, n % 2, 0:w], ps[:, 2 + n % 2, 0:w]).then_inc(s_pT, 1)

                def finish(i):
                    t, h = items[i]
                    if h < HEADS - 1:
                        return
                    dve.wait_ge(s_pv, n0 + i + 1)
                    chain(V.reciprocal(prob_sum[:, t, :], prob_sum[:, t, :]))
                    V.tensor_tensor(o_mla[:, t, :].rearrange("p (h n) -> p h n", h=HEADS),
                                    ps[:, 4 + t, 0:HEADS * D_V].rearrange("p (h n) -> p h n", h=HEADS),
                                    prob_sum[:, t, :].rearrange("p (h n) -> p h n", n=1).to_broadcast([P, HEADS, D_V]),
                                    ALU.mult).then_inc(s_mla_out, 1)

                row_max(0)
                for i in range(len(items)):
                    if i + 1 < len(items):
                        row_max(i + 1)
                    copy_pT(i)
                    if i:
                        finish(i - 1)
                finish(len(items) - 1)

            def residual(l):
                for c in range(2):
                    for t in range(NQ[l]):
                        i = c * NQ[l] + t
                        j = 2 * before(l, NQ) + i
                        cols = slice(c * 512, (c + 1) * 512)
                        dve.wait_ge(s_out_ps, j + 1)
                        if j:
                            dve.wait_ge(s_x1, j)
                        chain(V.tensor_tensor(tmp[:, 0:512], ps[:, 4 + i % 4, :], mod[:, GATE_Q, t // 2, cols], ALU.mult))
                        V.tensor_tensor(x[:, t, cols], x[:, t, cols], tmp[:, 0:512], ALU.add).then_inc(s_x1, 1)

            def route(l):
                n = NQ[l]
                scr = tmp[:, :]
                at = [0]

                def take(shape):
                    size = 1
                    for d in shape:
                        size *= d
                    v = scr[:, at[0]:at[0] + size]
                    at[0] += size
                    names = "abcd"[:len(shape)]
                    kw = dict(zip(names, shape))
                    return v.rearrange(f"p ({' '.join(names)}) -> p {' '.join(names)}", **kw)

                grp = n * N_GROUPS
                dve.wait_ge(s_aff, l + 1)
                choice = take([n, N_EXPERTS])
                c4 = choice.rearrange("p t (g e) -> p (t g) e", g=N_GROUPS)
                chain(V.tensor_tensor(choice, aff[:, 0:n, :],
                                      r_bias[:, :].rearrange("p (t n) -> p t n", t=1).to_broadcast([P, n, N_EXPERTS]), ALU.add))
                pairs = take([grp, 6])
                V.tensor_tensor(pairs[:, :, 0:3], c4[:, :, 0:3], c4[:, :, 1:4], ALU.add)
                V.tensor_tensor(pairs[:, :, 3:5], c4[:, :, 0:2], c4[:, :, 2:4], ALU.add)
                chain(V.tensor_tensor(pairs[:, :, 5:6], c4[:, :, 0:1], c4[:, :, 3:4], ALU.add))
                score = take([grp])
                chain(V.tensor_reduce(score, pairs, AX_X, ALU.max))
                s4 = score.rearrange("p (t g) -> p t g", g=N_GROUPS)
                best = take([n])
                chain(V.tensor_reduce(best, s4, AX_X, ALU.max))

                def spread(v, k):
                    return v.rearrange("p (t n) -> p t n", n=1).to_broadcast([P, n, k])

                ranks = rank16[:, :].rearrange("p (t n) -> p t n", t=1)

                def first_best(values, top, k, out_mask):
                    chain(V.tensor_tensor(out_mask, values, spread(top, k), ALU.is_ge))
                    chain(V.tensor_tensor(out_mask, out_mask, ranks[:, :, 0:k].to_broadcast([P, n, k]), ALU.mult))
                    chain(V.tensor_reduce(top, out_mask, AX_X, ALU.max))
                    chain(V.tensor_tensor(out_mask, out_mask, spread(top, k), ALU.is_equal))

                in_group = take([n, N_GROUPS])
                first_best(s4, best, N_GROUPS, in_group)
                outside = take([n, N_GROUPS])
                chain(V.tensor_scalar(outside, in_group, BIG, -BIG, ALU.mult, ALU.add))
                ig = in_group.rearrange("p t g -> p (t g)").rearrange("p (g e) -> p g e", e=1).to_broadcast([P, grp, EPG])
                og = outside.rearrange("p t g -> p (t g)").rearrange("p (g e) -> p g e", e=1).to_broadcast([P, grp, EPG])
                chain(V.tensor_tensor(c4, c4, ig, ALU.mult))
                chain(V.tensor_tensor(c4, c4, og, ALU.add))
                chosen = []
                for j in range(2):
                    mask = take([n, N_EXPERTS])
                    chain(V.tensor_reduce(best, choice, AX_X, ALU.max))
                    first_best(choice, best, N_EXPERTS, mask)
                    chosen.append(mask)
                    if j == 0:
                        chain(V.scalar_tensor_tensor(out=choice, in0=mask, scalar=-4.0 * BIG, in1=choice,
                                                     op0=ALU.mult, op1=ALU.add))
                chain(V.tensor_tensor(chosen[0], chosen[0], chosen[1], ALU.add))
                chain(V.tensor_tensor(chosen[0], chosen[0], aff[:, 0:n, :], ALU.mult))
                chain(V.tensor_reduce(best, chosen[0], AX_X, ALU.add))
                chain(V.reciprocal(best, best))
                V.tensor_tensor(gates[:, 0:n, :], chosen[0], spread(best, N_EXPERTS), ALU.mult).then_inc(s_gates, 1)

            def experts(l):
                first, end = 2 * moe_before[l], 2 * moe_before[l + 1]
                dve.wait_ge(s_gates, l + 1)

                def combine(i):
                    m, c = i // 2, i % 2
                    _, r, e = moe[m]
                    if e % EPG < EPG - 1:
                        return
                    dve.wait_ge(s_y_ps, i + 1)
                    got = ps[:, 4 + 2 * c:6 + 2 * c, :].rearrange("p b n -> p (b n)")
                    if e == EPG - 1:
                        if r:
                            dve.wait_ge(s_x2, before(l, NQ) + 2 * (r - 1) + c + 1)
                        V.tensor_copy(y_moe[:, c, :], got).then_inc(s_y, 1)
                    else:
                        dve.wait_ge(s_y, 2 * (m // EPG - 1) + c + 1)
                        V.tensor_tensor(y_moe[:, c, :], y_moe[:, c, :], got, ALU.add).then_inc(s_y, 1)
                    if e == N_EXPERTS - 1:
                        t = 2 * r + c
                        dve.wait_ge(s_y, 2 * (m // EPG) + c + 1)
                        chain(V.tensor_tensor(y_moe[:, c, :], y_moe[:, c, :], mod[:, GATE_Q, r, :], ALU.mult))
                        V.tensor_tensor(x[:, t, :], x[:, t, :], y_moe[:, c, :], ALU.add).then_inc(s_x2, 1)

                for i in range(first, end + 2):
                    if i < end:
                        m, c = i // 2, i % 2
                        _, r, e = moe[m]
                        t = 2 * r + c
                        dve.wait_ge(s_silu, i + 1)
                        if i >= first + 2:
                            dve.wait_ge(s_heT_ps, i - 1)
                        V.scalar_tensor_tensor(out=he_buf[:, i % 2, :], in0=silu_buf[:, i % 2, :],
                                               scalar=gates[:, t, e:e + 1], in1=ps[:, i % 2, D_EXPERT:2 * D_EXPERT],
                                               op0=ALU.mult, op1=ALU.mult).then_inc(s_he, 1)
                    if i - 2 >= first:
                        combine(i - 2)

            dve.wait_ge(s_const, 16 * N_CONST)
            for l in range(DEPTH):
                modulation(l, 0)
                scale_tiles(l, 0, NT)
                glu(l)
                rope_qk(l)
                norm_latents(l)
                taps(l)
                masks(l, 0)
                conv_centre(l)
                groupnorm(l, 0)
                conv_scale(l)
                if RET_PASSES[l] == 2:
                    masks(l, 1)
                    groupnorm(l, 1)
                for t in range(2):
                    rope_q(l, t)
                attention(l)
                residual(l)
                modulation(l, 1)
                scale_tiles(l, 1, NQ[l])
                route(l)
                experts(l)
            dve.wait_ge(s_normw, 16 * (2 * DEPTH + 1))
            for t in range(2):
                i = norm_base(DEPTH, 0) + t
                dve.wait_ge(s_rstd, i + 1)
                V.scalar_tensor_tensor(out=h_tok[:, i % 2, :], in0=x[:, t, :], scalar=rstd[:, t:t + 1],
                                       in1=norm_w, op0=ALU.mult, op1=ALU.mult).then_inc(s_final, 1)

        @block.gpsimd
        def _(pool):
            G = nc.gpsimd
            steps = [0]

            def chain(ins):
                steps[0] += 1
                ins.then_inc(s_pool, 1)
                pool.wait_ge(s_pool, steps[0])

            def inverse_root(v, n, eps):
                w = v.shape[-1]
                chain(G.tensor_scalar(v, v, 1.0 / n, eps, ALU.mult, ALU.add))
                return G.tensor_tensor(v, v, half_neg[:, 0:w], ALU.pow)

            def zero_bias(l, a):
                G.memset(ada_bias, 0.0).then_inc(s_bias_zero, 1)

            def norm(l, a, tiles, shift=True):
                for t in range(tiles):
                    i = norm_base(l, a) + t
                    pool.wait_ge(s_sumsq, i + 1)
                    inverse_root(rstd[:, t:t + 1], D, EPS).then_inc(s_rstd, 1)
                if shift:
                    for t in range(tiles):
                        i = norm_base(l, a) + t
                        pool.wait_ge(s_scaled, i + 1)
                        G.tensor_tensor(h_tok[:, i % 2, :], h_tok[:, i % 2, :], mod[:, SHIFT_Q, t // 2, :],
                                        ALU.add).then_inc(s_h, 1)

            G.memset(ones_mean[:, :], 1.0 / CONV_W)
            G.memset(eps_col[:, :], EPS)
            G.memset(half_neg[:, :], -0.5)
            G.memset(c_pad[:, :, :], 0.0).then_inc(s_ones, 1)
            pool.wait_ge(s_ones, 1)
            pool.wait_ge(s_const, 16 * N_CONST)
            for l in range(DEPTH):
                if l:
                    pool.wait_ge(s_ada_rows, l * ada_per_layer)
                    pool.wait_ge(s_x2, before(l, NQ))
                zero_bias(l, 0)
                for e0 in (0, CONV_K // 2 + SEQ):
                    last = G.memset(conv_in[:, :, :, e0:e0 + CONV_K // 2], 0.0)
                last.then_inc(s_pad, 1)
                norm(l, 0, NT)
                for t in range(NT):
                    pool.wait_ge(s_lat_sq, NT * l + t + 1)
                    if t < NQ[l]:
                        chain(G.tensor_scalar(lat_rstd[:, t, 0:1], lat_sumsq[:, t, 0:1], 1.0 / Q_RANK, EPS, ALU.mult, ALU.add))
                    chain(G.tensor_scalar(lat_rstd[:, t, 1:2], lat_sumsq[:, t, 1:2], 1.0 / KV_RANK, EPS, ALU.mult, ALU.add))
                    v = lat_rstd[:, t, 0 if t < NQ[l] else 1:2]
                    G.tensor_tensor(v, v, half_neg[:, 0:v.shape[-1]], ALU.pow).then_inc(s_lat_rstd, 1)
                pool.wait_ge(s_latT, lat_evacs(l, NT))
                for h in range(1, HEADS):
                    last = G.tensor_copy(KT[D_NOPE:D_QK, h, :], KT[D_NOPE:D_QK, 0, :])
                last.then_inc(s_kr, 1)
                pool.wait_ge(s_kr, l + 1)
                for s in range(RET_PASSES[l]):
                    g0 = 2 * (before(l, RET_PASSES) + s)
                    for i in range(2):
                        pool.wait_ge(s_gn_var, g0 + i + 1)
                        inverse_root(gn_rstd[:, i, :], RET_DV, GN_EPS).then_inc(s_gn_rstd, 1)
                    for i in range(2):
                        t = 2 * s + i
                        pool.wait_ge(s_gn_norm, g0 + i + 1)
                        for f in range(2):
                            last = G.tensor_tensor(gate_act[:, f, t, :], gate_act[:, f, t, :],
                                                   gn_y[:, i, 6 * f:6 * f + 6, :].rearrange("p h n -> p (h n)"), ALU.mult)
                        chain(last)
                        G.tensor_tensor(gate_act[:, 0, t, :], gate_act[:, 0, t, :], gate_act[:, 1, t, :],
                                        ALU.add).then_inc(s_ret_out, 1)
                zero_bias(l, 1)
                norm(l, 1, NQ[l])
            norm(DEPTH, 0, 2, shift=False)


def _constants():
    import numpy as np

    ident = np.eye(P, dtype=np.float32)
    sel = np.zeros((P, 2, P), np.float32)
    for s in range(2):
        sel[s::32, s, :] = 1.0
    p = np.arange(P)[:, None, None].astype(np.float64)
    n = np.arange(384)[None, None, :]
    g = gamma(np.arange(HEADS, dtype=np.float64))[None, :, None]
    fwd, bwd = n - p, p + SEQ - n
    decay = np.stack([np.where(fwd >= 0, g ** np.maximum(fwd, 0), 0.0),
                      np.where(bwd >= 0, g[:, ::-1] ** np.maximum(bwd, 0), 0.0)], axis=1).astype(np.float32)
    t = np.arange(SEQ).reshape(2, P)
    inv = 10000.0 ** (-np.arange(8, dtype=np.float64) / 8)
    rope = np.zeros((P, 2, 2, D_ROPE), np.float32)
    for i in range(2):
        for g2, pos in enumerate((t[i] // 64, t[i] % 64)):
            ang = pos[:, None] * inv
            for b in range(2):
                cols = slice(16 * g2 + 8 * b, 16 * g2 + 8 * b + 8)
                rope[:, i, 0, cols] = np.cos(ang)
                rope[:, i, 1, cols] = np.sin(ang) * (1 if b else -1)
    rank = np.broadcast_to(np.arange(N_EXPERTS, 0, -1, dtype=np.float32), (P, N_EXPERTS)).copy()
    return {"const_ident": ident, "const_sel": sel, "const_decay": decay, "const_rope": rope, "const_rank": rank}


_INS = ["x", "c", "ctx", "c_ctx", "ada_w", "ada_b", "norm1_w", "norm2_w", "w_in", 
        "mla_w_uq", "mla_kv_norm_w", "mla_w_ukv", "w_out", "router_w", "router_bias", "moe_w_gate",
        "moe_w_up", "moe_w_down", "final_norm_w"]


def kernel(**inputs):
    import numpy as np
    import concourse.bacc as bacc
    from concourse.bass_utils import run_bass_kernel_spmd

    nc = bacc.Bacc("TRN2", target_bir_lowering=False, num_devices=1, dynamic_dma_scratch_size=1024)
    arrays = {name: np.ascontiguousarray(inputs[name]) for name in _INS}
    cols = np.concatenate([np.asarray(inputs["conv_dw"])] +
                          [np.asarray(inputs[name])[:, None] for name in ("conv_b", "conv_ln_w", "conv_ln_b")], axis=1)
    arrays["conv_cols"] = np.ascontiguousarray(cols.reshape(DEPTH, CONV_K + 3, 2, P).transpose(0, 3, 2, 1))
    arrays["q_norm_cols"] = np.ascontiguousarray(np.asarray(inputs["mla_q_norm_w"]).reshape(DEPTH, 2, 96).transpose(0, 2, 1))
    arrays.update(_constants())
    dram = {name: nc.dram_tensor(f"in_{name}", a.shape, mybir.dt.from_np(a.dtype), kind="ExternalInput").ap()
            for name, a in arrays.items()}
    out = nc.dram_tensor("out_0", (1, SEQ, D), F32, kind="ExternalOutput").ap()
    build(nc, dram, out)
    r = run_bass_kernel_spmd(nc, [{f"in_{name}": a for name, a in arrays.items()}], core_ids=[0])
    return r.results[0]["out_0"]
```

```python
from contextlib import ExitStack

import concourse.bass as bass
from concourse import mybir

P = 128
D = 1024
DEPTH = 2
SEQ = 256
NT = 4
KD = D // P
CONV_W, CONV_K = 256, 31
HEADS, RET_DK, RET_DV = 6, 32, 64
CHUNK_PAD = SEQ + CONV_K - 1
Q_RANK, KV_RANK, D_NOPE, D_ROPE, D_V = 192, 128, 64, 32, 64
D_QK = D_NOPE + D_ROPE
MLA_SCALE = float(D_QK) ** -0.5
N_EXPERTS, EPG, D_EXPERT = 16, 4, 256
N_GROUPS = N_EXPERTS // EPG
EPS, GN_EPS = 1e-6, 1e-5
QKW, VW = 2 * HEADS * RET_DK, HEADS * RET_DV
LATW = Q_RANK + KV_RANK + D_ROPE
BIG = 1e30
GROUP_SLOTS = 2 * P
SLOTS = (N_GROUPS + 1) * GROUP_SLOTS
SLOT_W = D + N_EXPERTS
F32 = mybir.dt.float32
BF16 = mybir.dt.bfloat16
ACT = mybir.ActivationFunctionType
ALU = mybir.AluOpType
AX_X = mybir.AxisListType.X

NQ = [4, 2]
CONV_U, QK_U, V_U, LAT_U, GF_U, GB_U = range(6)
UNIT_COLS = [(0, 512), (512, QKW), (896, VW), (2048, LATW), (1280, VW), (1664, VW)]
N_WSLOT = 3
SCALE_Q, SHIFT_Q, GATE_Q = 0, 1, 2
MOD_UNITS = [(SHIFT_Q, 0), (SHIFT_Q, 1), (SCALE_Q, 0), (SCALE_Q, 1), (GATE_Q, 0), (GATE_Q, 1)]


def gamma(h):
    return 1.0 - 2.0 ** (-5.0 - h)


def plan():
    units, mods = [], []
    for l in range(DEPTH):
        for a in range(2):
            if a:
                units += [("in", l, u) for u in range(6)] + [("out", l, c) for c in range(2)]
            units += [("ada", l, a, u) for u in range(6)]
            for u, (q, half) in enumerate(MOD_UNITS):
                both = l == 0 or (a == 0 and q != GATE_Q)
                mods += [(l, a, u, s) for s in range(2 if both else 1)]
    return units, mods


def build(nc, dram, out):
    units, mods = plan()
    unit_at = {u: n for n, u in enumerate(units)}
    mod_at = {m: n for n, m in enumerate(mods)}
    units_per_layer = len(units) // DEPTH
    ada_per_layer = 12
    group_passes = [N_GROUPS + (NQ[l] * P > 2 * GROUP_SLOTS - 1) for l in range(DEPTH)]

    def before(l, per):
        return sum(per[:l])

    with ExitStack() as ctx:
        def sb(name, shape, dt=F32):
            return ctx.enter_context(nc.sbuf_tensor(name, shape, dt))

        def sem(name):
            return ctx.enter_context(nc.semaphore(name))

        ps = ctx.enter_context(nc.psum_tensor("ps", [P, 8, 512], F32))

        wring = sb("wring", [P, N_WSLOT, 4096])
        x = sb("x", [P, NT, D])
        hT_buf = sb("hT_buf", [P, 4096])
        mod = sb("mod", [P, 3, 2, D])
        work1 = sb("work1", [P, 4096])
        decay = sb("decay", [P, 2, HEADS, 384])
        work2 = sb("work2", [P, 2176])
        convT = sb("convT", [P, 2, 512])
        tokens = sb("tokens", [P, 3 * NT * VW])
        v_mla = sb("v_mla", [P, NT, HEADS * D_V])
        o_mla = sb("o_mla", [P, NT, HEADS * D_V])
        stage = sb("stage", [P, 1536])
        tmp = sb("tmp", [P, 768])
        w_uq = sb("w_uq", [P, 2, HEADS * D_QK])
        w_ukv = sb("w_ukv", [P, HEADS * P])
        cqT = sb("cqT", [P, 2, 512])
        ckvT = sb("ckvT", [P, 512])
        sel = sb("sel", [P, 2, P])
        ident = sb("ident", [P, P])
        ones_mean = sb("ones_mean", [P, P])
        rope = sb("rope", [P, 2, 2, D_ROPE])
        router_w = sb("router_w", [P, KD, N_EXPERTS])
        c_raw = sb("c_raw", [P, 2, KD])
        c_pad = sb("c_pad", [P, KD, 32])
        conv_vec = sb("conv_vec", [P, 2, CONV_K + 3])
        dw = conv_vec[:, :, 0:CONV_K]
        q_norm = sb("q_norm", [P, 2])
        kv_norm = sb("kv_norm", [P, 1])
        eps_col = sb("eps_col", [P, 1])
        half_neg = sb("half_neg", [P, 12])
        rstd = sb("rstd", [P, NT])
        lat_sumsq = sb("lat_sumsq", [P, NT, 2])
        lat_rstd = sb("lat_rstd", [P, NT, 2])
        gn_mean = sb("gn_mean", [P, 2, 12])
        gn_rstd = sb("gn_rstd", [P, 2, 12])
        neg_max = sb("neg_max", [P, 2])
        prob_sum = sb("prob_sum", [P, NT, HEADS])
        aff = sb("aff", [P, NT, N_EXPERTS])
        r_bias = sb("r_bias", [P, N_EXPERTS])
        rank16 = sb("rank16", [P, N_EXPERTS])
        tri = sb("tri", [P, P])
        group_slot = sb("group_slot", [P, 2, N_GROUPS])
        slot_of = sb("slot_of", [P, NT], mybir.dt.uint32)
        flags = sb("flags", [1, 8], mybir.dt.int32)

        hT = hT_buf[:, :].rearrange("p (k n) -> p k n", k=KD)
        oT = hT_buf[:, 0:6 * 512].rearrange("p (k n) -> p k n", k=6)
        norm_w = work1[:, 0:D]
        mod_rows = work1[:, D:2 * D].rearrange("p (b n) -> p b n", b=2)
        v_ret = tokens[:, 0:NT * VW].rearrange("p (t n) -> p t n", t=NT)
        gate_act = tokens[:, NT * VW:3 * NT * VW].rearrange("p (f t n) -> p f t n", f=2, t=NT)
        h2 = tokens[:, 0:NT * SLOT_W].rearrange("p (t n) -> p t n", t=NT)
        slot_tok = tokens[:, 0:4 * SLOT_W].rearrange("p (b c n) -> p b c n", b=2, c=2)
        y_back = tokens[:, 0:NT * D].rearrange("p (t n) -> p t n", t=NT)
        zero_rows = tokens[:, 0:SLOT_W]
        slot_hT = hT_buf[:, :].rearrange("p (b c k n) -> p b c k n", b=2, c=2, k=KD)
        h_tok = work1[:, 2 * D:4 * D].rearrange("p (b n) -> p b n", b=2)
        conv_sig = h_tok[:, :, 0:512]
        qkT = work1[:, 0:2048].rearrange("p (f n) -> p f n", f=4)
        masked = work1[:, 2048:4096].rearrange("p (f j n) -> p f j n", f=2, j=4)
        qT = work1[0:D_QK, 0:HEADS * 512].rearrange("p (h n) -> p h n", h=HEADS)
        KT = mod[0:D_QK, 0:2, :, :].rearrange("p a b n -> p (a b n)")[:, 0:HEADS * 512].rearrange(
            "p (h n) -> p h n", h=HEADS)
        conv_in = work2[:, 0:2 * 2 * CHUNK_PAD].rearrange("p (c s n) -> p c s n", c=2, s=2)
        conv_sq = work2[:, 0:1024].rearrange("p (c n) -> p c n", c=2)
        conv_std = work2[:, 0:512]
        acc = work2[:, 1144:2168].rearrange("p (c n) -> p c n", c=2)
        q_stage = work2[:, 0:1152].rearrange("p (b n) -> p b n", b=2)
        probs = work2[:, 0:1024].rearrange("p (b n) -> p b n", b=2)
        probsT = work2[:, 1024:2048].rearrange("p (b n) -> p b n", b=2)
        y_moe = work2[:, 0:2048].rearrange("p (c n) -> p c n", c=2)
        ada_bias = stage[:, 0:1024].rearrange("p (b n) -> p b n", b=2)
        qk_tok = stage[:, 0:NT * QKW].rearrange("p (t n) -> p t n", t=NT)
        lat_tok = stage[:, 0:NT * LATW].rearrange("p (t n) -> p t n", t=NT)
        gn_y = stage[:, 0:1536].rearrange("p (i g n) -> p i g n", i=2, g=12)
        junk = o_mla[:, 0, 0:Q_RANK]
        square_junk = tmp[:, 0:512].bitcast(BF16)
        silu_buf = work1[:, 0:512].rearrange("p (b n) -> p b n", b=2)
        he_buf = work1[:, 512:1024].rearrange("p (b n) -> p b n", b=2)
        heT_buf = work1[:, 1024:1536].rearrange("p (b n) -> p b n", b=2)
        gu = [wring[:, j, :].rearrange("p (k n) -> p k n", k=KD) for j in range(2)]
        dn = [wring[:, 2, j * 2048:(j + 1) * 2048].rearrange("p (f n) -> p f n", f=2) for j in range(2)]

        def unit_view(n):
            kind = units[n][0]
            cols = UNIT_COLS[units[n][2]][1] if kind == "in" else 512
            return wring[:, n % N_WSLOT, 0:KD * cols].rearrange("p (k n) -> p k n", k=KD)

        s_const = sem("s_const")
        s_small = sem("s_small")
        s_wslot = [sem(f"s_wslot{j}") for j in range(N_WSLOT)]
        s_bias = [sem(f"s_bias{j}") for j in range(2)]
        s_normw = sem("s_normw")
        s_gu = [sem(f"s_gu{j}") for j in range(2)]
        s_dn = [sem(f"s_dn{j}") for j in range(2)]
        s_ones = sem("s_ones")
        s_cpad = sem("s_cpad")
        s_bias_zero = sem("s_bias_zero")
        s_ada_part = sem("s_ada_part")
        s_ada_rows = sem("s_ada_rows")
        s_ada_bc = sem("s_ada_bc")
        s_mod = sem("s_mod")
        s_sumsq = sem("s_sumsq")
        s_rstd = sem("s_rstd")
        s_scaled = sem("s_scaled")
        s_h = sem("s_h")
        s_hT_ps = sem("s_hT_ps")
        s_hT = sem("s_hT")
        s_conv_ps = sem("s_conv_ps")
        s_sig = sem("s_sig")
        s_glu = sem("s_glu")
        s_pad = sem("s_pad")
        s_proj_ps = sem("s_proj_ps")
        s_proj = sem("s_proj")
        s_qk_rope = sem("s_qk_rope")
        s_qkT_ps = sem("s_qkT_ps")
        s_qkT = sem("s_qkT")
        s_lat_sq = sem("s_lat_sq")
        s_lat_rstd = sem("s_lat_rstd")
        s_lat_norm = sem("s_lat_norm")
        s_latT_ps = sem("s_latT_ps")
        s_latT = sem("s_latT")
        s_kr = sem("s_kr")
        s_taps = sem("s_taps")
        s_cmean_ps = sem("s_cmean_ps")
        s_ccent = sem("s_ccent")
        s_csq = sem("s_csq")
        s_cvar_ps = sem("s_cvar_ps")
        s_cstd = sem("s_cstd")
        s_cnorm = sem("s_cnorm")
        s_convT = sem("s_convT")
        s_ret_ps = sem("s_ret_ps")
        s_mask = [sem("s_mask_f"), sem("s_mask_b")]
        s_ret_pv = [sem("s_ret_pv_f"), sem("s_ret_pv_b")]
        s_gn_y = sem("s_gn_y")
        s_gn_cent = sem("s_gn_cent")
        s_gn_sq = sem("s_gn_sq")
        s_gn_var = sem("s_gn_var")
        s_gn_rstd = sem("s_gn_rstd")
        s_gn_norm = sem("s_gn_norm")
        s_ret_out = sem("s_ret_out")
        s_mla_ps = sem("s_mla_ps")
        s_mla_sb = sem("s_mla_sb")
        s_q_rope = sem("s_q_rope")
        s_qT_ps = sem("s_qT_ps")
        s_qT = sem("s_qT")
        s_score_ps = sem("s_score_ps")
        s_max = sem("s_max")
        s_exp = sem("s_exp")
        s_pT_ps = sem("s_pT_ps")
        s_pT = sem("s_pT")
        s_pv = sem("s_pv")
        s_mla_out = sem("s_mla_out")
        s_oT_ps = sem("s_oT_ps")
        s_oT = sem("s_oT")
        s_out_ps = sem("s_out_ps")
        s_x1 = sem("s_x1")
        s_logit_ps = sem("s_logit_ps")
        s_aff = sem("s_aff")
        s_gates = sem("s_gates")
        s_over_gate = sem("s_over_gate")
        s_group = sem("s_group")
        s_rank_ps = sem("s_rank_ps")
        s_flags = sem("s_flags")
        s_fill = sem("s_fill")
        s_filled = sem("s_filled")
        s_scattered = sem("s_scattered")
        s_slot = [sem(f"s_slot{j}") for j in range(2)]
        s_slotT_ps = sem("s_slotT_ps")
        s_slotT = sem("s_slotT")
        s_over_slot = sem("s_over_slot")
        s_over_gu = [sem(f"s_over_gu{j}") for j in range(2)]
        s_over_dn = [sem(f"s_over_dn{j}") for j in range(2)]
        s_gu_used = sem("s_gu_used")
        s_dn_used = sem("s_dn_used")
        s_y_out = [sem(f"s_y_out{c}") for c in range(2)]
        s_back = [sem(f"s_back{t}") for t in range(NT)]
        s_up_ps = sem("s_up_ps")
        s_silu = sem("s_silu")
        s_he = sem("s_he")
        s_heT_ps = sem("s_heT_ps")
        s_heT = sem("s_heT")
        s_y_ps = sem("s_y_ps")
        s_y = [sem(f"s_y{c}") for c in range(2)]
        s_x2 = sem("s_x2")
        s_final = sem("s_final")
        s_out = sem("s_out")
        s_dve = sem("s_dve")
        s_pool = sem("s_pool")
        s_act = sem("s_act")

        slots = nc.dram_tensor("slots", (SLOTS, SLOT_W), F32, kind="Internal").ap()
        y_slots = nc.dram_tensor("y_slots", (SLOTS, D), F32, kind="Internal").ap()

        N_CONST = 13
        N_SMALL = 5
        NORM_TILES = [4 + NQ[0], 4 + NQ[1]]

        def norm_base(l, a):
            return sum(NORM_TILES[:l]) + (0, 4, 4 + NQ[l])[a] if l < DEPTH else sum(NORM_TILES)

        PROJ_JOBS = [[(u, t) for u in (QK_U, V_U, LAT_U, GF_U, GB_U) for t in range(NT if u < GF_U else NQ[l])]
                     for l in range(DEPTH)]
        per_proj = [len(j) for j in PROJ_JOBS]
        MLA_JOBS = [[("k", h) for h in range(HEADS)] + [("v", t) for t in range(NT)] +
                    [("q", t, half) for t in range(NQ[l]) for half in range(2)] for l in range(DEPTH)]
        per_mla = [len(j) for j in MLA_JOBS]
        ATTN = [[(t, h) for t in range(NQ[l]) for h in range(HEADS)] for l in range(DEPTH)]
        per_attn = [len(j) for j in ATTN]
        RET_PASSES = [NQ[l] // 2 for l in range(DEPTH)]
        per_ret = [HEADS * r for r in RET_PASSES]
        SMALL_LOADS = 16 * N_SMALL

        def groups_before(l):
            return sum(group_passes[:l])

        WHOLE = {0: (0, 0), 1: (0, 1), 2: (1, 0), 3: (1, 1), 4: (2, 0), 5: (2, 1), 6: (3, 1), 7: (3, 0)}
        SHORT = {0: (0, 0), 1: (1, 0), 6: (2, 0), 7: (3, 0)}

        def ended(gg, items, k, back):
            place = list(items).index(k) - back
            return 8 * gg + (list(items)[place] + 1 if place >= 0 else place + 1)

        def w_wait(eng, n):
            eng.wait_ge(s_wslot[n % N_WSLOT], 16 * (n // N_WSLOT + 1))

        block = ctx.enter_context(nc.Block())

        def freed(n):
            kind, l = units[n][:2]
            if kind == "ada":
                return s_ada_part, l * ada_per_layer + units[n][2] * 6 + units[n][3] + 1
            if kind == "out":
                return s_out_ps, before(l, [2 * q for q in NQ]) + (units[n][2] + 1) * NQ[l]
            if units[n][2] == CONV_U:
                return s_conv_ps, 4 * (l + 1)
            done = [i for i, (u, t) in enumerate(PROJ_JOBS[l]) if u == units[n][2]][-1] + 1
            return s_proj_ps, before(l, per_proj) + done

        @block.sync
        def _(sp):
            def load_unit(n):
                u = units[n]
                l = u[1]
                if n - N_WSLOT >= units_per_layer * l or (l == 0 and n >= N_WSLOT):
                    sp.wait_ge(*freed(n - N_WSLOT))
                elif l > 0:
                    sp.wait_ge(s_y_ps, 8 * groups_before(l))
                if u[0] == "ada":
                    a, j = u[2], u[3]
                    q, half = MOD_UNITS[j]
                    col = (a * 3 + (1, 0, 2)[q]) * D + half * 512
                    src = dram["ada_w"][l].rearrange("(p k) n -> p k n", k=KD)[:, :, col:col + 512]
                    b = l * ada_per_layer + a * 6 + j
                    if j == 0:
                        sp.wait_ge(s_bias_zero, 2 * l + a + 1)
                    if j == 2:
                        if l or a:
                            sp.wait_ge(s_mod, mod_at[(l, a, 0, 0)])
                        if l and not a:
                            sp.wait_ge(s_y_ps, 8 * groups_before(l))
                        if a:
                            sp.wait_ge(s_score_ps, before(l + 1, per_attn))
                        sp.dma_start(norm_w, dram[("norm1_w", "norm2_w")[a]][l:l + 1, :].to_broadcast([P, D])).then_inc(s_normw, 16)
                    if b >= 2:
                        sp.wait_ge(s_ada_rows, b - 1)
                    sp.dma_start(ada_bias[0:2, b % 2, :],
                                 dram["ada_b"][l:l + 1, col:col + 512].to_broadcast([2, 512])).then_inc(s_bias[b % 2], 16)
                elif u[0] == "in":
                    c0, w = UNIT_COLS[u[2]]
                    src = dram["w_in"][l].rearrange("(p k) n -> p k n", k=KD)[:, :, c0:c0 + w]
                else:
                    src = dram["w_out"][l].rearrange("(k p) n -> p k n", p=P)[:, :, u[2] * 512:u[2] * 512 + 512]
                sp.dma_start(unit_view(n), src).then_inc(s_wslot[n % N_WSLOT], 16)

            def load_expert(l, g, e, gu_sem, dn_sem, which):
                m = EPG * groups_before(l) + e if gu_sem is s_over_gu else EPG * (groups_before(l) + g) + e
                if gu_sem is s_over_gu:
                    m += EPG * N_GROUPS
                j = m % 2
                if m - EPG * groups_before(l) < 2:
                    sp.wait_ge(s_ada_part, ada_per_layer * (l + 1))
                else:
                    sp.wait_ge((s_gu_used, s_dn_used)[which], m - 1)

                def weights(name):
                    w = dram[name][l].rearrange("(g e) k n -> g e k n", e=EPG)
                    return w[bass.ds(g, 1), e].rearrange("g k n -> (g k) n")

                if which == 0:
                    for i, name in enumerate(("moe_w_gate", "moe_w_up")):
                        sp.dma_start(gu[j][:, :, i * D_EXPERT:(i + 1) * D_EXPERT],
                                     weights(name).rearrange("(p k) n -> p k n", k=KD)).then_inc(gu_sem[j], 16)
                else:
                    sp.dma_start(dn[j], weights("moe_w_down").rearrange("(p f) n -> p f n", f=2)).then_inc(dn_sem[j], 16)

            def load_slots(l, g):
                if g >= 2:
                    sp.wait_ge(s_he, 8 * (groups_before(l) + g - 1))
                for c in range(2):
                    r0 = (2 * g + c) * P
                    sp.dma_start(slot_tok[:, g % 2, c, :], slots[r0:r0 + P, :]).then_inc(
                        s_over_slot if g == N_GROUPS else s_slot[g % 2], 16)

            def load_experts(l):
                for e in range(2):
                    load_expert(l, 0, e, s_gu, s_dn, 0)
                load_expert(l, 0, 0, s_gu, s_dn, 1)
                sp.wait_ge(s_scattered, 16 * before(l + 1, NQ))
                load_slots(l, 0)
                load_slots(l, 1)
                for m in range(2, N_EXPERTS):
                    load_expert(l, m // EPG, m % EPG, s_gu, s_dn, 0)
                    load_expert(l, (m - 1) // EPG, (m - 1) % EPG, s_gu, s_dn, 1)
                    if m % EPG == 0 and m // EPG + 1 < N_GROUPS:
                        load_slots(l, m // EPG + 1)
                load_expert(l, N_GROUPS - 1, EPG - 1, s_gu, s_dn, 1)
                if group_passes[l] > N_GROUPS:
                    over = sp.value_load(flags[0:1, 4:5], min_val=0, max_val=1)
                    group = sp.value_load(flags[0:1, 5:6], min_val=0, max_val=N_GROUPS - 1)
                    with sp.If(over > 0):
                        load_slots(l, N_GROUPS)
                        for e in range(EPG):
                            load_expert(l, group, e, s_over_gu, s_over_dn, 0)
                            if e:
                                load_expert(l, group, e - 1, s_over_gu, s_over_dn, 1)
                        load_expert(l, group, EPG - 1, s_over_gu, s_over_dn, 1)

            for l in range(DEPTH):
                if l:
                    sp.wait_ge(s_convT, 2 * l)
                    sp.wait_ge(s_mla_ps, before(l, per_mla))
                for dst, src in (
                    (w_uq[0:96, :, :], dram["mla_w_uq"][l].rearrange("(k p) n -> p k n", p=96)),
                    (w_ukv[:, :], dram["mla_w_ukv"][l]),
                    (conv_vec[:, :, :], dram["conv_cols"][l]),
                    (q_norm[0:96, :], dram["q_norm_cols"][l]),
                    (kv_norm[:, :], dram["mla_kv_norm_w"][l].rearrange("(p k) -> p k", k=1)),
                ):
                    sp.dma_start(dst, src).then_inc(s_small, 16)
                for n in range(units_per_layer * l, units_per_layer * (l + 1)):
                    load_unit(n)
                    if n == 8:
                        sp.wait_ge(s_fill, 1)
                        for j in range(SLOTS // P):
                            sp.dma_start(slots[j * P:(j + 1) * P, :], zero_rows).then_inc(s_filled, 16)
                load_experts(l)
            sp.wait_ge(s_mod, len(mods))
            sp.wait_ge(s_y_ps, 8 * groups_before(DEPTH))
            sp.dma_start(norm_w, dram["final_norm_w"].rearrange("(a n) -> a n", a=1).to_broadcast([P, D])).then_inc(s_normw, 16)
            for t in range(2):
                sp.wait_ge(s_final, t + 1)
                sp.dma_start(out[0, t * P:(t + 1) * P, :], h_tok[:, (norm_base(DEPTH, 0) + t) % 2, :]).then_inc(s_out, 16)
            sp.wait_ge(s_out, 32)

        def tok(t):
            return slice(t * P, (t + 1) * P)

        def key_tile(s, slot):
            return 2 + slot if slot < 2 else 2 * s + slot - 2

        def in_group(n):
            return tmp[:, 700:700 + 4 * n].rearrange("p (t g) -> p t g", t=n)

        def lat_evacs(l, t):
            per = lambda a, b: sum(4 if i < NQ[a] else 2 for i in range(b))
            return sum(per(a, NT) for a in range(l)) + per(l, t)

        @block.tensor
        def _(pe):
            T = nc.tensor

            def modulation(l, a):
                def broadcast(u):
                    n = l * ada_per_layer + a * 6 + u
                    pe.wait_ge(s_ada_rows, n + 1)
                    for s in range(2):
                        if (l, a, u, s) in mod_at:
                            b = mod_at[(l, a, u, s)]
                            if b >= 2:
                                pe.wait_ge(s_mod, b - 1)
                            T.matmul(ps[:, 2 + b % 2, :], sel[:, s, :], mod_rows[:, n % 2, :],
                                     start=True, stop=True).then_inc(s_ada_bc, 1)

                if a:
                    pe.wait_ge(s_exp, before(l + 1, per_attn))
                    pe.wait_ge(s_oT, 2 * before(l + 1, NQ))
                elif l:
                    pe.wait_ge(s_he, 8 * groups_before(l))
                    pe.wait_ge(s_heT, 8 * groups_before(l))
                    pe.wait_ge(s_slotT, 4 * groups_before(l))
                for u in range(6):
                    n = l * ada_per_layer + a * 6 + u
                    w_wait(pe, unit_at[("ada", l, a, u)])
                    w = unit_view(unit_at[("ada", l, a, u)])
                    if n >= 2:
                        pe.wait_ge(s_ada_rows, n - 1)
                    for step in range(2):
                        for strip in range(4):
                            k = 2 * strip + step
                            last = T.matmul(ps[32 * strip:32 * strip + 32, n % 2, :], c_pad[:, k, :], w[:, k, :],
                                            start=(step == 0), stop=(step == 1),
                                            tile_position=(0, 32 * strip))
                    last.then_inc(s_ada_part, 1)
                    if u >= 1:
                        broadcast(u - 1)
                broadcast(5)

            def transpose_h(l, a, tiles):
                for t in range(tiles):
                    i = norm_base(l, a) + t
                    pe.wait_ge(s_h, i + 1)
                    h = (h2[:, t, 0:D] if a else h_tok[:, i % 2, :]).rearrange("q (p k) -> q k p", k=KD)
                    for b in range(2):
                        if i >= 1:
                            pe.wait_ge(s_hT, 2 * (i - 1) + b + 1)
                        for j in range(4):
                            last = T.transpose(ps[:, 6 + b, j * P:(j + 1) * P], h[:, 4 * b + j, :], ident[:, :])
                        last.then_inc(s_hT_ps, 1)

            def project_conv(l):
                n = unit_at[("in", l, CONV_U)]
                w_wait(pe, n)
                w = unit_view(n)
                pe.wait_ge(s_hT, 2 * (norm_base(l, 0) + 4))
                pe.wait_ge(s_ada_rows, l * ada_per_layer + 6)
                pe.wait_ge(s_mod, mod_at[(l, 1, 0, 0)])
                width = NQ[l] * P
                for m in (2, 3, 0, 1):
                    for k in range(KD):
                        last = T.matmul(ps[:, m, 0:width], w[:, k, tok(m)], hT[:, k, 0:width],
                                        start=(k == 0), stop=(k == KD - 1))
                    last.then_inc(s_conv_ps, 1)

            def project(l, us):
                for i, (u, t) in enumerate(PROJ_JOBS[l]):
                    if u not in us:
                        continue
                    j = before(l, per_proj) + i
                    n = unit_at[("in", l, u)]
                    if t == 0:
                        w_wait(pe, n)
                    w = unit_view(n)
                    if i >= 2:
                        pe.wait_ge(s_proj, j - 1)
                    for k in range(KD):
                        last = T.matmul(ps[:, 4 + j % 2, 0:UNIT_COLS[u][1]], hT[:, k, tok(t)], w[:, k, :],
                                        start=(k == 0), stop=(k == KD - 1))
                    last.then_inc(s_proj_ps, 1)

            def transpose_qk(l):
                for t in range(NT):
                    if t < 2:
                        pe.wait_ge(s_qk_rope, 2 * l + t + 1)
                    else:
                        pe.wait_ge(s_proj, before(l, per_proj) + t + 1)
                        pe.wait_ge(s_qkT, 2 * (NT * l + t - 1))
                    for f, (c0, w) in enumerate(((0, 128), (128, 64), (192, 128), (320, 64))):
                        if f < 2 and t >= NQ[l]:
                            continue
                        last = T.transpose(ps[0:w, 6 + t % 2, f * P:(f + 1) * P], qk_tok[:, t, c0:c0 + w], ident[:, :])
                    last.then_inc(s_qkT_ps, 1)

            def transpose_latents(l):
                pe.wait_ge(s_qkT, 2 * NT * (l + 1))
                for t in range(NT):
                    pe.wait_ge(s_lat_norm, NT * l + t + 1)
                    if t >= 2:
                        pe.wait_ge(s_latT, lat_evacs(l, t - 1))
                    for f, (c0, w) in enumerate(((0, 96), (96, 96), (192, 128), (320, 32))):
                        if f < 2 and t >= NQ[l]:
                            continue
                        last = T.transpose(ps[0:w, 6 + t % 2, f * P:(f + 1) * P], lat_tok[:, t, c0:c0 + w], ident[:, :])
                    last.then_inc(s_latT_ps, 1)

            def retention(l, s):
                r0 = before(l, per_ret) + s * HEADS

                def scores(h):
                    r = r0 + h
                    if s == 0 and h < 2:
                        pe.wait_ge((s_glu, s_sig)[h], 2 * (l + 1))
                    elif s == 1 and h < 2:
                        pe.wait_ge((s_ccent, s_cstd)[h], (2 * (l + 1), l + 1)[h])
                    else:
                        pe.wait_ge(s_mask[0], r - 1)
                        pe.wait_ge(s_mask[1], r - 1)
                    q0, side = 32 * (h % 4), h // 4
                    qs = qkT[q0:q0 + 32, side, s * SEQ:(s + 1) * SEQ]
                    for slot in (range(4) if s == 0 else (2, 3)):
                        bank = 2 * (h % 2) + slot // 2 if s == 0 else h % 2
                        last = T.matmul(ps[:, bank, slot % 2 * SEQ:(slot % 2 + 1) * SEQ],
                                        qkT[q0:q0 + 32, 2 + side, tok(key_tile(s, slot))], qs, start=True, stop=True,
                                        tile_position=(q0, 0))
                    last.then_inc(s_ret_ps, 1)

                def sums(h, f):
                    r = r0 + h
                    pe.wait_ge(s_mask[f], r + 1)
                    for i in range(2):
                        slots = ([0, 1] if s == 0 else []) + [j for j in (2, 3) if (j - 2 <= i if f == 0 else j - 2 >= i)]
                        for j in slots:
                            last = T.matmul(ps[:, 4 + 2 * i + f, h * RET_DV:(h + 1) * RET_DV],
                                            masked[:, f, j, tok(i)], v_ret[:, key_tile(s, j), h * RET_DV:(h + 1) * RET_DV],
                                            start=(j == slots[0]), stop=(j == slots[-1]))
                    last.then_inc(s_ret_pv[f], 1)

                scores(0)
                if s == 0:
                    pe.wait_ge(s_proj, before(l + 1, per_proj))
                    pe.wait_ge(s_latT, lat_evacs(l, NT))
                else:
                    pe.wait_ge(s_gn_y, 4 * (before(l, RET_PASSES) + s))
                for h in range(HEADS):
                    if h + 1 < HEADS:
                        scores(h + 1)
                    sums(h, 0)
                    sums(h, 1)

            def conv_mean(l):
                for f in range(2):
                    pe.wait_ge(s_mask[f], before(l, per_ret) + HEADS)
                pe.wait_ge(s_taps, 2 * CONV_K * (l + 1))
                for c in range(2):
                    last = T.matmul(ps[:, 0, 0:NQ[l] * P], ones_mean[:, :], acc[:, c, 0:NQ[l] * P],
                                    start=(c == 0), stop=(c == 1))
                last.then_inc(s_cmean_ps, 1)

            def conv_var(l):
                pe.wait_ge(s_csq, 2 * (l + 1))
                for c in range(2):
                    last = T.matmul(ps[:, 1, 0:NQ[l] * P], ones_mean[:, :], conv_sq[:, c, 0:NQ[l] * P],
                                    start=(c == 0), stop=(c == 1))
                last.then_inc(s_cvar_ps, 1)

            def mla_job(l, i):
                job = MLA_JOBS[l][i]
                j = before(l, per_mla) + i
                bank = 2 + j % 2
                if i >= 2:
                    pe.wait_ge(s_mla_sb, j - 1)
                if job[0] == "k":
                    h = job[1]
                    last = T.matmul(ps[0:D_NOPE, bank, :], w_ukv[:, h * P:h * P + D_NOPE], ckvT[:, :],
                                    start=True, stop=True)
                elif job[0] == "v":
                    vs = w_ukv[:, :].rearrange("p (h n) -> p h n", h=HEADS)[:, :, D_NOPE:]
                    last = T.matmul(ps[:, bank, 0:HEADS * D_V], ckvT[:, tok(job[1])], vs, start=True, stop=True)
                else:
                    _, t, half = job
                    for k in range(2):
                        last = T.matmul(ps[:, bank, 0:288], cqT[0:96, k, tok(t)],
                                        w_uq[0:96, k, half * 288:(half + 1) * 288], start=(k == 0), stop=(k == 1))
                last.then_inc(s_mla_ps, 1)

            def transpose_q(l, t):
                i = before(l, NQ) + t
                if t < 2:
                    pe.wait_ge(s_q_rope, 2 * l + t + 1)
                else:
                    pe.wait_ge(s_mla_sb, before(l, per_mla) + 10 + 2 * (t + 1))
                if t == 0:
                    pe.wait_ge(s_gn_y, 4 * before(l + 1, RET_PASSES))
                else:
                    pe.wait_ge(s_qT, 2 * i)
                for h in range(HEADS):
                    last = T.transpose(ps[0:D_QK, 6 + h // 4, h % 4 * P:(h % 4 + 1) * P],
                                       q_stage[:, t % 2, h * D_QK:(h + 1) * D_QK], ident[:, :])
                last.then_inc(s_qT_ps, 1)

            def attention(l):
                items = ATTN[l]
                n0 = before(l, per_attn)
                pe.wait_ge(s_kr, l + 1)
                pe.wait_ge(s_mla_sb, before(l + 1, per_mla))
                pe.wait_ge(s_cstd, l + 1)
                for f in range(2):
                    pe.wait_ge(s_mask[f], before(l + 1, per_ret))
                pe.wait_ge(s_qT, 2 * before(l + 1, NQ))

                def scores(i):
                    t, h = items[i]
                    if i >= 2:
                        pe.wait_ge(s_exp, n0 + i - 1)
                    keys = slice(0, 512) if t < 2 else slice(SEQ, 512)
                    T.matmul(ps[:, (n0 + i) % 2, 0:keys.stop - keys.start], qT[:, h, tok(t)], KT[:, h, keys],
                             start=True, stop=True).then_inc(s_score_ps, 1)

                def turn(i):
                    t, h = items[i]
                    n = n0 + i
                    pe.wait_ge(s_exp, n + 1)
                    if i >= 2:
                        pe.wait_ge(s_pT, n - 1)
                    for j in range(4 if t < 2 else 2):
                        last = T.transpose(ps[:, 2 + n % 2, tok(j)], probs[:, n % 2, tok(j)], ident[:, :])
                    last.then_inc(s_pT_ps, 1)

                def values(i):
                    t, h = items[i]
                    n = n0 + i
                    pe.wait_ge(s_pT, n + 1)
                    tiles = range(4) if t < 2 else range(2, 4)
                    for j, kt in enumerate(tiles):
                        last = T.matmul(ps[:, 4 + t, h * D_V:(h + 1) * D_V], probsT[:, n % 2, tok(j)],
                                        v_mla[:, kt, h * D_V:(h + 1) * D_V], start=(j == 0), stop=(kt == 3))
                    last.then_inc(s_pv, 1)

                scores(0)
                for i in range(len(items)):
                    if i + 1 < len(items):
                        scores(i + 1)
                    turn(i)
                    if i:
                        values(i - 1)
                values(len(items) - 1)

            def project_out(l):
                i0 = before(l, NQ)
                pe.wait_ge(s_pT, before(l + 1, per_attn))
                for t in range(NQ[l]):
                    for b in range(2):
                        if b == 0:
                            pe.wait_ge(s_ret_out, i0 + t + 1)
                        else:
                            pe.wait_ge(s_mla_out, i0 + t + 1)
                        if t:
                            pe.wait_ge(s_oT, 2 * (i0 + t - 1) + b + 1)
                        o = o_mla[:, t, :] if b else gate_act[:, 0, t, :]
                        for j in range(3):
                            last = T.transpose(ps[:, 2 + b, tok(j)], o[:, tok(j)], ident[:, :])
                        last.then_inc(s_oT_ps, 1)
                pe.wait_ge(s_convT, 2 * (l + 1))
                for c in range(2):
                    n = unit_at[("out", l, c)]
                    w_wait(pe, n)
                    w = unit_view(n)
                    for t in range(NQ[l]):
                        i = c * NQ[l] + t
                        j = 2 * i0 + i
                        if c == 0:
                            pe.wait_ge(s_oT, 2 * (i0 + t + 1))
                        if i >= 4:
                            pe.wait_ge(s_x1, j - 3)
                        for k in range(KD):
                            lhs = convT[:, k, tok(t)] if k < 2 else oT[:, k - 2, tok(t)]
                            last = T.matmul(ps[:, 4 + i % 4, :], lhs, w[:, k, :], start=(k == 0), stop=(k == KD - 1))
                        last.then_inc(s_out_ps, 1)

            def route(l):
                pe.wait_ge(s_hT, 2 * (norm_base(l, 1) + NQ[l]))
                for t in range(NQ[l]):
                    for k in range(KD):
                        last = T.matmul(ps[:, 4, t * N_EXPERTS:(t + 1) * N_EXPERTS], hT[:, k, tok(t)], router_w[:, k, :],
                                        start=(k == 0), stop=(k == KD - 1))
                last.then_inc(s_logit_ps, 1)
                pe.wait_ge(s_group, l + 1)
                n = NQ[l]
                chosen = in_group(n)
                for t in range(n):
                    for u in range(t + 1):
                        T.matmul(ps[:, 4, 64 + 4 * t:68 + 4 * t], tri[:, :] if u == t else ones_mean[:, :], chosen[:, u, :],
                                 start=(u == 0), stop=(u == t))
                for u in range(n):
                    last = T.matmul(ps[:, 4, 96:100], ones_mean[:, :], chosen[:, u, :], start=(u == 0), stop=(u == n - 1))
                last.then_inc(s_rank_ps, 1)

            def experts(l):
                waiting = {"gu": 0, "dn": 0}

                def release(which, ins):
                    if waiting[which]:
                        ins.then_inc({"gu": s_gu_used, "dn": s_dn_used}[which], waiting[which])
                        waiting[which] = 0

                def slot_round(g, r):
                    c, b = r // 2, r % 2
                    n = 4 * (groups_before(l) + g) + r
                    if g == N_GROUPS:
                        pe.wait_ge(s_over_slot, 32)
                    else:
                        pe.wait_ge(s_slot[g % 2], 32 * (2 * l + g // 2 + 1))
                    if n:
                        pe.wait_ge(s_slotT, n)
                    h = slot_tok[:, g % 2, c, 0:D].rearrange("q (p k) -> q k p", k=KD)
                    for j in range(4):
                        last = T.transpose(ps[:, 3, tok(j)], h[:, 4 * b + j, :], ident[:, :])
                        if j == 0:
                            release("gu", last)
                    last.then_inc(s_slotT_ps, 1)

                def landed(g, e, gu_sems, over_sems, each):
                    if g == N_GROUPS:
                        pe.wait_ge(over_sems[e % 2], each * (e // 2 + 1))
                    else:
                        pe.wait_ge(gu_sems[e % 2], each * (2 * (N_GROUPS * l + g) + e // 2 + 1))

                def up(g, items, k):
                    e, c = items[k]
                    gg = groups_before(l) + g
                    i = 8 * gg + k
                    if items is SHORT and k == 6:
                        pe.drain().then_inc(s_up_ps, 4)
                    landed(g, e, s_gu, s_over_gu, 32)
                    pe.wait_ge(s_slotT, 4 * gg + (4 if c else 2))
                    if ended(gg, items, k, 2) > 0:
                        pe.wait_ge(s_he, ended(gg, items, k, 2))
                    for q in range(KD):
                        last = T.matmul(ps[:, i % 2, :], slot_hT[:, g % 2, c, q, :], gu[e % 2][:, q, :],
                                        start=(q == 0), stop=(q == KD - 1))
                        if q == 0:
                            release("dn", last)
                        elif q == 1:
                            release("gu", last)
                    last.then_inc(s_up_ps, 1)
                    if k and (c == 0 if items is SHORT or e == EPG - 1 else c == 1) and k != (6 if items is WHOLE else 8):
                        waiting["gu"] += 1

                def turn(g, items, k):
                    gg = groups_before(l) + g
                    i = 8 * gg + k
                    if items is SHORT and k == 6:
                        pe.drain().then_inc(s_heT_ps, 4)
                    pe.wait_ge(s_he, i + 1)
                    if ended(gg, items, k, 1) > 0:
                        pe.wait_ge(s_heT, ended(gg, items, k, 1))
                    he = he_buf[:, i % 2, :].rearrange("q (p f) -> q f p", f=2)
                    for f in range(2):
                        last = T.transpose(ps[:, 2, tok(f)], he[:, f, :], ident[:, :])
                        if f == 0:
                            release("gu", last)
                    last.then_inc(s_heT_ps, 1)

                def down(g, items, k):
                    e, c = items[k]
                    gg = groups_before(l) + g
                    i = 8 * gg + k
                    if items is SHORT and k == 6:
                        pe.drain().then_inc(s_y_ps, 4)
                    pe.wait_ge(s_heT, i + 1)
                    landed(g, e, s_dn, s_over_dn, 16)
                    if e == 0 and gg:
                        pe.wait_ge(s_y[c], gg)
                    for half in range(2):
                        for f in range(2):
                            last = T.matmul(ps[:, 4 + 2 * c + half, :], heT_buf[:, i % 2, tok(f)],
                                            dn[e % 2][:, f, half * 512:(half + 1) * 512],
                                            start=(e == 0 and f == 0), stop=(e == EPG - 1 and f == 1))
                            if half == 0 and f == 0:
                                release("dn", last)
                    last.then_inc(s_y_ps, 1)
                    if items is SHORT or k in (1, 3, 5, 7):
                        waiting["dn"] += 1

                def body(g, items):
                    order = list(items)
                    if items is SHORT:
                        waiting["gu"] += 1
                    for p in range(1, len(order)):
                        up(g, items, order[p])
                        if p < 4 and g < N_GROUPS - 1:
                            slot_round(g + 1, p)
                        turn(g, items, order[p - 1])
                        if p >= 2:
                            down(g, items, order[p - 2])
                    down(g, items, order[-2])
                    if waiting["dn"]:
                        pe.drain().then_inc(s_dn_used, waiting["dn"])
                        waiting["dn"] = 0
                    assert not waiting["gu"]

                def finish(g):
                    turn(g, WHOLE, 7)
                    down(g, WHOLE, 7)

                def settle():
                    pe.drain().then_inc(s_dn_used, waiting["dn"])
                    waiting["dn"] = 0

                pe.wait_ge(s_ada_rows, ada_per_layer * (l + 1))
                pe.wait_ge(s_mod, mod_at[(l + 1, 0, 0, 0)] if l + 1 < DEPTH else len(mods))
                pe.wait_ge(s_flags, l + 1)
                for r in range(4):
                    slot_round(0, r)
                for g in range(N_GROUPS):
                    up(g, WHOLE, 0)
                    if g < N_GROUPS - 1:
                        slot_round(g + 1, 0)
                    if g:
                        finish(g - 1)
                    second = pe.value_load(flags[0:1, g:g + 1], min_val=0, max_val=1)
                    carried = dict(waiting)
                    with pe.If(second > 0):
                        body(g, WHOLE)
                    waiting.update(carried)
                    with pe.Else():
                        body(g, SHORT)
                finish(N_GROUPS - 1)
                settle()
                if group_passes[l] > N_GROUPS:
                    over = pe.value_load(flags[0:1, 4:5], min_val=0, max_val=1)
                    with pe.If(over > 0):
                        for r in range(4):
                            slot_round(N_GROUPS, r)
                        up(N_GROUPS, WHOLE, 0)
                        body(N_GROUPS, WHOLE)
                        finish(N_GROUPS)
                        settle()
                    with pe.Else():
                        for sem, n in ((s_up_ps, 8), (s_heT_ps, 8), (s_y_ps, 8), (s_slotT_ps, 4),
                                       (s_gu_used, EPG), (s_dn_used, EPG)):
                            pe.drain().then_inc(sem, n)

            pe.wait_ge(s_const, 16 * N_CONST)
            pe.wait_ge(s_cpad, 2)
            pe.wait_ge(s_ones, 1)
            for l in range(DEPTH):
                modulation(l, 0)
                if l:
                    for c in range(2):
                        pe.wait_ge(s_y[c], groups_before(l))
                transpose_h(l, 0, NT)
                project_conv(l)
                project(l, (QK_U, V_U))
                transpose_qk(l)
                project(l, (LAT_U, GF_U, GB_U))
                transpose_latents(l)
                retention(l, 0)
                conv_mean(l)
                pe.wait_ge(s_small, 16 * N_SMALL * (l + 1))
                for i in range(10):
                    mla_job(l, i)
                conv_var(l)
                if RET_PASSES[l] == 2:
                    retention(l, 1)
                for t in range(NQ[l]):
                    mla_job(l, 10 + 2 * t)
                    mla_job(l, 11 + 2 * t)
                    if t:
                        transpose_q(l, t - 1)
                transpose_q(l, NQ[l] - 1)
                attention(l)
                pe.wait_ge(s_mla_out, before(l + 1, NQ))
                project_out(l)
                modulation(l, 1)
                pe.wait_ge(s_x1, 2 * before(l + 1, NQ))
                transpose_h(l, 1, NQ[l])
                route(l)
                experts(l)

        @block.scalar
        def _(act):
            S = nc.scalar
            steps = [0]

            def chain(ins):
                steps[0] += 1
                ins.then_inc(s_act, 1)
                act.wait_ge(s_act, steps[0])

            for dst, src in (
                (x[:, 0:2, :], dram["x"][0].rearrange("(t p) n -> p t n", p=P)),
                (x[:, 2:4, :], dram["ctx"][0].rearrange("(t p) n -> p t n", p=P)),
                (c_raw[:, 0, :], dram["c"][0].rearrange("(p k) -> p k", k=KD)),
                (c_raw[:, 1, :], dram["c_ctx"].rearrange("(p k) -> p k", k=KD)),
                (ident[:, :], dram["const_ident"]),
                (sel[:, :, :], dram["const_sel"]),
                (rope[:, :, :, :], dram["const_rope"]),
                (decay[:, 0, :, :], dram["const_decay"][:, 0, :, :]),
                (decay[:, 1, :, :], dram["const_decay"][:, 1, :, :]),
                (rank16[:, :], dram["const_rank"]),
                (tri[:, :], dram["const_tri"]),
                (router_w[:, :, :], dram["router_w"].rearrange("(p k) n -> p k n", k=KD)),
                (r_bias[:, :], dram["router_bias"].rearrange("(a n) -> a n", a=1).to_broadcast([P, N_EXPERTS])),
            ):
                act.dma_start(dst, src).then_inc(s_const, 16)

            def square_sums(l, a, tiles):
                for t in range(tiles):
                    i = norm_base(l, a) + t
                    if i:
                        act.wait_ge(s_sumsq, i)
                    S.activation(square_junk, x[:, t, :], ACT.Square, accum_out=rstd[:, t:t + 1]).then_inc(s_sumsq, 1)

            def copy_hT(l, a, tiles):
                for t in range(tiles):
                    i = norm_base(l, a) + t
                    for b in range(2):
                        act.wait_ge(s_hT_ps, 2 * i + b + 1)
                        S.activation(hT[:, 4 * b:4 * b + 4, tok(t)], ps[:, 6 + b, :].rearrange("p (k n) -> p k n", k=4),
                                     ACT.Copy).then_inc(s_hT, 1)

            def project(l, us):
                dst = {QK_U: qk_tok, V_U: v_ret, LAT_U: lat_tok}
                for i, (u, t) in enumerate(PROJ_JOBS[l]):
                    if u not in us:
                        continue
                    j = before(l, per_proj) + i
                    act.wait_ge(s_proj_ps, j + 1)
                    if l == 0 and u == V_U and t == 0:
                        act.wait_ge(s_filled, 16 * (SLOTS // P))
                    got = ps[:, 4 + j % 2, 0:UNIT_COLS[u][1]]
                    if u in dst:
                        S.activation(dst[u][:, t, :], got, ACT.Copy).then_inc(s_proj, 1)
                    else:
                        S.activation(gate_act[:, u - GF_U, t, :], got, ACT.Silu).then_inc(s_proj, 1)
                    if u == LAT_U:
                        act.wait_ge(s_proj, j + 1)
                        if NT * l + t:
                            act.wait_ge(s_lat_sq, NT * l + t)
                        if t < NQ[l]:
                            chain(S.activation(junk, lat_tok[:, t, 0:Q_RANK], ACT.Square,
                                               accum_out=lat_sumsq[:, t, 0:1]))
                        S.activation(junk[:, 0:KV_RANK], lat_tok[:, t, Q_RANK:Q_RANK + KV_RANK], ACT.Square,
                                     accum_out=lat_sumsq[:, t, 1:2]).then_inc(s_lat_sq, 1)

            def copy_qkT(l):
                for t in range(NT):
                    act.wait_ge(s_qkT_ps, NT * l + t + 1)
                    f0 = 0 if t < NQ[l] else 2
                    got = ps[:, 6 + t % 2, :].rearrange("p (f n) -> p f n", f=4)
                    S.activation(qkT[:, f0::2, tok(t)], got[:, f0::2, :], ACT.Copy).then_inc(s_qkT, 1)
                    S.activation(qkT[0:64, f0 + 1::2, tok(t)], got[0:64, f0 + 1::2, :], ACT.Copy).then_inc(s_qkT, 1)

            def copy_latT(l):
                act.wait_ge(s_small, 16 * N_SMALL * (l + 1))
                for t in range(NT):
                    act.wait_ge(s_latT_ps, NT * l + t + 1)
                    bank = 6 + t % 2
                    if t < NQ[l]:
                        for k in range(2):
                            S.activation(cqT[0:96, k, tok(t)], ps[0:96, bank, k * P:(k + 1) * P], ACT.Copy,
                                         scale=q_norm[0:96, k:k + 1]).then_inc(s_latT, 1)
                    S.activation(ckvT[:, tok(t)], ps[:, bank, 2 * P:3 * P], ACT.Copy,
                                 scale=kv_norm[:, 0:1]).then_inc(s_latT, 1)
                    S.activation(KT[D_NOPE:D_QK, 0, tok(t)], ps[0:D_ROPE, bank, 3 * P:4 * P], ACT.Copy).then_inc(s_latT, 1)

            def groupnorm_in(l, s):
                g = before(l, RET_PASSES) + s
                for f in range(2):
                    act.wait_ge(s_ret_pv[f], HEADS * (g + 1))
                for i in range(2):
                    if g:
                        act.wait_ge(s_ret_out, 2 * (g - 1) + i + 1)
                    for f in range(2):
                        S.activation(gn_y[:, i, 6 * f:6 * f + 6, :],
                                     ps[:, 4 + 2 * i + f, 0:VW].rearrange("p (h n) -> p h n", h=HEADS),
                                     ACT.Copy).then_inc(s_gn_y, 1)

            def groupnorm_sq(l, s):
                for i in range(2):
                    g = 2 * (before(l, RET_PASSES) + s) + i
                    act.wait_ge(s_gn_cent, g + 1)
                    if g:
                        act.wait_ge(s_gn_var, g)
                    S.activation(tmp[:, :].rearrange("p (g n) -> p g n", g=12), gn_y[:, i, :, :],
                                 ACT.Square).then_inc(s_gn_sq, 1)

            def conv_sq_act(l):
                for c in range(2):
                    act.wait_ge(s_ccent, 2 * l + c + 1)
                    S.activation(conv_sq[:, c, 0:NQ[l] * P], acc[:, c, 0:NQ[l] * P], ACT.Square).then_inc(s_csq, 1)

            def conv_std_act(l):
                act.wait_ge(s_cvar_ps, l + 1)
                S.activation(conv_std[:, 0:NQ[l] * P], ps[:, 1, 0:NQ[l] * P], ACT.Sqrt, bias=eps_col[:, 0:1]).then_inc(s_cstd, 1)

            def conv_out(l):
                for c in range(2):
                    act.wait_ge(s_cnorm, 2 * l + c + 1)
                    S.activation(convT[:, c, 0:NQ[l] * P], acc[:, c, 0:NQ[l] * P], ACT.Silu,
                                 scale=conv_vec[:, c, CONV_K + 1:CONV_K + 2], bias=conv_vec[:, c, CONV_K + 2:CONV_K + 3]).then_inc(s_convT, 1)

            def mla_copy(l, i):
                job = MLA_JOBS[l][i]
                j = before(l, per_mla) + i
                bank = 2 + j % 2
                act.wait_ge(s_mla_ps, j + 1)
                if job[0] == "k":
                    S.activation(KT[0:D_NOPE, job[1], :], ps[0:D_NOPE, bank, :], ACT.Copy).then_inc(s_mla_sb, 1)
                elif job[0] == "v":
                    S.activation(v_mla[:, job[1], :], ps[:, bank, 0:HEADS * D_V], ACT.Copy).then_inc(s_mla_sb, 1)
                else:
                    _, t, half = job
                    if t >= 2:
                        act.wait_ge(s_qT_ps, before(l, NQ) + t - 1)
                    if t == 0:
                        act.wait_ge(s_cnorm, 2 * (l + 1))
                    S.activation(q_stage[:, t % 2, half * 288:(half + 1) * 288], ps[:, bank, 0:288],
                                 ACT.Copy).then_inc(s_mla_sb, 1)

            def copy_qT(l, t):
                act.wait_ge(s_qT_ps, before(l, NQ) + t + 1)
                for b, n in ((0, 4), (1, 2)):
                    S.activation(qT[:, 4 * b:4 * b + n, tok(t)],
                                 ps[0:D_QK, 6 + b, 0:n * P].rearrange("p (h n) -> p h n", h=n),
                                 ACT.Copy, scale=MLA_SCALE).then_inc(s_qT, 1)

            def softmax(l):
                n0 = before(l, per_attn)
                for i, (t, h) in enumerate(ATTN[l]):
                    n = n0 + i
                    w = 512 if t < 2 else SEQ
                    act.wait_ge(s_max, n + 1)
                    if i >= 2:
                        act.wait_ge(s_pT_ps, n - 1)
                    S.activation(probs[:, n % 2, 0:w], ps[:, n % 2, 0:w], ACT.Exp, bias=neg_max[:, n % 2:n % 2 + 1],
                                 accum_out=prob_sum[:, t, h:h + 1]).then_inc(s_exp, 1)

            def copy_oT(l):
                for t in range(NQ[l]):
                    for b in range(2):
                        i = 2 * (before(l, NQ) + t) + b
                        act.wait_ge(s_oT_ps, i + 1)
                        S.activation(oT[:, 3 * b:3 * b + 3, tok(t)],
                                     ps[:, 2 + b, 0:3 * P].rearrange("p (k n) -> p k n", k=3), ACT.Copy).then_inc(s_oT, 1)

            def experts(l):
                def slot_copy(g, r):
                    c, b = r // 2, r % 2
                    act.wait_ge(s_slotT_ps, 4 * (groups_before(l) + g) + r + 1)
                    S.activation(slot_hT[:, g % 2, c, 4 * b:4 * b + 4, :], ps[:, 3, :].rearrange("p (k n) -> p k n", k=4),
                                 ACT.Copy).then_inc(s_slotT, 1)

                def silu(g, items, k):
                    gg = groups_before(l) + g
                    i = 8 * gg + k
                    if items is SHORT and k == 6:
                        act.drain().then_inc(s_silu, 4)
                    act.wait_ge(s_up_ps, i + 1)
                    if ended(gg, items, k, 2) > 0:
                        act.wait_ge(s_he, ended(gg, items, k, 2))
                    S.activation(silu_buf[:, i % 2, :], ps[:, i % 2, 0:D_EXPERT], ACT.Silu).then_inc(s_silu, 1)

                def copy_heT(g, items, k):
                    gg = groups_before(l) + g
                    i = 8 * gg + k
                    if items is SHORT and k == 6:
                        act.drain().then_inc(s_heT, 4)
                    act.wait_ge(s_heT_ps, i + 1)
                    if ended(gg, items, k, 2) > 0:
                        act.wait_ge(s_y_ps, ended(gg, items, k, 2))
                    S.activation(heT_buf[:, i % 2, :], ps[:, 2, 0:D_EXPERT], ACT.Copy).then_inc(s_heT, 1)

                def body(g, items):
                    order = list(items)
                    for p in range(1, len(order)):
                        silu(g, items, order[p])
                        if p < 4 and g < N_GROUPS - 1:
                            slot_copy(g + 1, p)
                        copy_heT(g, items, order[p - 1])

                act.wait_ge(s_flags, l + 1)
                for r in range(4):
                    slot_copy(0, r)
                for g in range(N_GROUPS):
                    silu(g, WHOLE, 0)
                    if g < N_GROUPS - 1:
                        slot_copy(g + 1, 0)
                    if g:
                        copy_heT(g - 1, WHOLE, 7)
                    second = act.value_load(flags[0:1, g:g + 1], min_val=0, max_val=1)
                    with act.If(second > 0):
                        body(g, WHOLE)
                    with act.Else():
                        body(g, SHORT)
                copy_heT(N_GROUPS - 1, WHOLE, 7)
                if group_passes[l] > N_GROUPS:
                    over = act.value_load(flags[0:1, 4:5], min_val=0, max_val=1)
                    with act.If(over > 0):
                        for r in range(4):
                            slot_copy(N_GROUPS, r)
                        silu(N_GROUPS, WHOLE, 0)
                        body(N_GROUPS, WHOLE)
                        copy_heT(N_GROUPS, WHOLE, 7)
                    with act.Else():
                        for sem, n in ((s_silu, 8), (s_heT, 8), (s_slotT, 4)):
                            act.drain().then_inc(sem, n)

            act.wait_ge(s_const, 16 * N_CONST)
            act.wait_ge(s_ones, 1)
            for s in range(2):
                S.activation(c_pad[:, :, s], c_raw[:, s, :], ACT.Silu).then_inc(s_cpad, 1)
            for l in range(DEPTH):
                if l:
                    act.wait_ge(s_x2, before(l, NQ))
                square_sums(l, 0, NT)
                copy_hT(l, 0, NT)
                for j in range(2):
                    act.wait_ge(s_conv_ps, 4 * l + j + 1)
                    S.activation(conv_sig[:, j, 0:NQ[l] * P], ps[:, 2 + j, 0:NQ[l] * P], ACT.Sigmoid).then_inc(s_sig, 1)
                project(l, (QK_U, V_U))
                copy_qkT(l)
                project(l, (LAT_U, GF_U, GB_U))
                copy_latT(l)
                groupnorm_in(l, 0)
                conv_sq_act(l)
                for i in range(10):
                    mla_copy(l, i)
                conv_std_act(l)
                groupnorm_sq(l, 0)
                conv_out(l)
                if RET_PASSES[l] == 2:
                    groupnorm_in(l, 1)
                    groupnorm_sq(l, 1)
                for t in range(NQ[l]):
                    mla_copy(l, 10 + 2 * t)
                    mla_copy(l, 11 + 2 * t)
                    if t:
                        copy_qT(l, t - 1)
                copy_qT(l, NQ[l] - 1)
                softmax(l)
                copy_oT(l)
                act.wait_ge(s_x1, 2 * before(l + 1, NQ))
                square_sums(l, 1, NQ[l])
                copy_hT(l, 1, NQ[l])
                act.wait_ge(s_logit_ps, l + 1)
                S.activation(aff[:, 0:NQ[l], :], ps[:, 4, 0:NQ[l] * N_EXPERTS].rearrange("p (t n) -> p t n", n=N_EXPERTS),
                             ACT.Sigmoid).then_inc(s_aff, 1)
                experts(l)
            act.wait_ge(s_x2, before(DEPTH, NQ))
            square_sums(DEPTH, 0, 2)

        @block.vector
        def _(dve):
            V = nc.vector
            steps = [0]

            def chain(ins):
                steps[0] += 1
                ins.then_inc(s_dve, 1)
                dve.wait_ge(s_dve, steps[0])

            def modulation(l, a):
                def bcast(u):
                    q, half = MOD_UNITS[u]
                    for s in range(2):
                        if (l, a, u, s) not in mod_at:
                            continue
                        b = mod_at[(l, a, u, s)]
                        dve.wait_ge(s_ada_bc, b + 1)
                        dst = mod[:, q, s, half * 512:(half + 1) * 512]
                        if q == SCALE_Q:
                            dve.wait_ge(s_normw, 16 * (2 * l + a + 1))
                            V.scalar_tensor_tensor(out=dst, in0=ps[:, 2 + b % 2, :], scalar=1.0,
                                                   in1=norm_w[:, half * 512:(half + 1) * 512],
                                                   op0=ALU.add, op1=ALU.mult).then_inc(s_mod, 1)
                        else:
                            V.tensor_copy(dst, ps[:, 2 + b % 2, :]).then_inc(s_mod, 1)

                for u in range(6):
                    n = l * ada_per_layer + a * 6 + u
                    dve.wait_ge(s_ada_part, n + 1)
                    dve.wait_ge(s_bias[n % 2], 16 * (n // 2 + 1))
                    if u >= 2:
                        dve.wait_ge(s_ada_bc, mod_at[(l, a, u - 1, 0)])
                    V.tensor_tensor(mod_rows[:, n % 2, :], ps[:, n % 2, :], ada_bias[:, n % 2, :],
                                    ALU.add).then_inc(s_ada_rows, 1)
                    if u >= 1:
                        bcast(u - 1)
                bcast(5)

            def scale_tiles(l, a, tiles):
                dve.wait_ge(s_mod, mod_at[(l, a, 4, 0)])
                for t in range(tiles):
                    i = norm_base(l, a) + t
                    dve.wait_ge(s_rstd, i + 1)
                    if i >= 2 and not a:
                        dve.wait_ge(s_hT_ps, 2 * (i - 1))
                    V.scalar_tensor_tensor(out=h2[:, t, 0:D] if a else h_tok[:, i % 2, :], in0=x[:, t, :],
                                           scalar=rstd[:, t:t + 1], in1=mod[:, SCALE_Q, t // 2, :], op0=ALU.mult, op1=ALU.mult).then_inc(s_scaled, 1)

            def glu(l):
                dve.wait_ge(s_pad, l + 1)
                dve.wait_ge(s_conv_ps, 4 * (l + 1))
                dve.wait_ge(s_sig, 2 * (l + 1))
                n = NQ[l] // 2
                for c in range(2):
                    V.tensor_tensor(conv_in[:, c, 0:n, CONV_K // 2:CONV_K // 2 + SEQ],
                                    ps[:, c, 0:n * SEQ].rearrange("p (s n) -> p s n", s=n),
                                    conv_sig[:, c, 0:n * SEQ].rearrange("p (s n) -> p s n", s=n),
                                    ALU.mult).then_inc(s_glu, 1)

            def rotate(view, t, heads, done, value):
                n = heads * D_ROPE
                straight = tmp[:, 0:n].rearrange("p (h r) -> p h r", h=heads)
                swapped = tmp[:, 384:384 + n].rearrange("p (h g b r) -> p h g b r", h=heads, g=2, b=2)
                src = view.rearrange("p h (g b r) -> p h g b r", g=2, b=2)
                sin = rope[:, t, 1, :].rearrange("p (h g b r) -> p h g b r", h=1, g=2, b=2)
                cos = rope[:, t, 0, :].rearrange("p (h r) -> p h r", h=1)
                V.tensor_tensor(straight, view, cos.to_broadcast([P, heads, D_ROPE]), ALU.mult)
                for b in range(2):
                    last = V.tensor_tensor(swapped[:, :, :, b, :], src[:, :, :, 1 - b, :],
                                           sin[:, :, :, b, :].to_broadcast([P, heads, 2, 8]), ALU.mult)
                chain(last)
                V.tensor_tensor(view, straight, tmp[:, 384:384 + n].rearrange("p (h r) -> p h r", h=heads),
                                ALU.add).then_inc(done, 1)
                dve.wait_ge(done, value)

            def rope_qk(l):
                for t in range(2):
                    dve.wait_ge(s_proj, before(l, per_proj) + t + 1)
                    rotate(qk_tok[:, t, :].rearrange("p (h r) -> p h r", h=12), t, 12, s_qk_rope, 2 * l + t + 1)

            def norm_latents(l):
                for t in range(NT):
                    dve.wait_ge(s_lat_rstd, NT * l + t + 1)
                    if t < NQ[l]:
                        V.tensor_scalar(lat_tok[:, t, 0:Q_RANK], lat_tok[:, t, 0:Q_RANK], lat_rstd[:, t, 0:1], None, ALU.mult)
                    ckv = lat_tok[:, t, Q_RANK:Q_RANK + KV_RANK]
                    last = V.tensor_scalar(ckv, ckv, lat_rstd[:, t, 1:2], None, ALU.mult)
                    if t < 2:
                        rotate(lat_tok[:, t, Q_RANK + KV_RANK:LATW].rearrange("p (h r) -> p h r", h=1), t, 1,
                               s_lat_norm, NT * l + t + 1)
                    else:
                        last.then_inc(s_lat_norm, 1)

            def taps(l):
                n = NQ[l] // 2
                dve.wait_ge(s_glu, 2 * (l + 1))
                dve.wait_ge(s_small, 16 * N_SMALL * (l + 1))
                for k in range(CONV_K):
                    for c in range(2):
                        i = 2 * (CONV_K * l + k) + c
                        src = conv_in[:, c, 0:n, k:k + SEQ]
                        dst = acc[:, c, 0:n * SEQ].rearrange("p (s n) -> p s n", s=n)
                        if k == 0:
                            V.tensor_scalar(dst, src, dw[:, c, 0:1], conv_vec[:, c, CONV_K:CONV_K + 1], ALU.mult, ALU.add).then_inc(s_taps, 1)
                        else:
                            dve.wait_ge(s_taps, i - 1)
                            V.scalar_tensor_tensor(out=dst, in0=src, scalar=dw[:, c, k:k + 1], in1=dst,
                                                   op0=ALU.mult, op1=ALU.add).then_inc(s_taps, 1)

            def masks(l, s):
                k = RET_DK ** -0.5
                for h in range(HEADS):
                    r = before(l, per_ret) + s * HEADS + h
                    dve.wait_ge(s_ret_ps, r + 1)
                    far = [gamma(h) ** P, gamma(HEADS - 1 - h) ** P]

                    def own(slot):
                        bank = 2 * (h % 2) + slot // 2 if s == 0 else h % 2
                        return ps[:, bank, slot % 2 * SEQ:(slot % 2 + 1) * SEQ]

                    def decayed(f, slot, cols, t0, scale):
                        n = cols.stop - cols.start
                        return V.scalar_tensor_tensor(out=masked[:, f, slot, cols], in0=own(slot)[:, cols],
                                                      scalar=float(scale * k), in1=decay[:, f, h, t0:t0 + n],
                                                      op0=ALU.mult, op1=ALU.mult)

                    whole = slice(0, SEQ)
                    if r:
                        dve.wait_ge(s_ret_pv[0], r)
                    if s == 0:
                        decayed(0, 0, whole, P, far[0])
                        decayed(0, 1, whole, P, 1.0)
                    decayed(0, 2, whole, 0, 1.0)
                    decayed(0, 3, slice(P, SEQ), 0, 1.0).then_inc(s_mask[0], 1)
                    if r:
                        dve.wait_ge(s_ret_pv[1], r)
                    if s == 0:
                        decayed(1, 0, whole, 0, 1.0)
                        decayed(1, 1, whole, 0, far[1])
                    decayed(1, 3, whole, P, 1.0)
                    decayed(1, 2, slice(0, P), SEQ, 1.0).then_inc(s_mask[1], 1)

            def groupnorm(l, s):
                g0 = 2 * (before(l, RET_PASSES) + s)
                for i in range(2):
                    dve.wait_ge(s_gn_y, 2 * (g0 + i + 1))
                    chain(V.tensor_reduce(gn_mean[:, i, :], gn_y[:, i, :, :], AX_X, ALU.add))
                    chain(V.tensor_scalar(gn_mean[:, i, :], gn_mean[:, i, :], 1.0 / RET_DV, None, ALU.mult))
                    V.tensor_tensor(gn_y[:, i, :, :], gn_y[:, i, :, :],
                                    gn_mean[:, i, :].rearrange("p (g n) -> p g n", n=1).to_broadcast([P, 12, RET_DV]),
                                    ALU.subtract).then_inc(s_gn_cent, 1)
                for i in range(2):
                    dve.wait_ge(s_gn_sq, g0 + i + 1)
                    V.tensor_reduce(gn_rstd[:, i, :], tmp[:, :].rearrange("p (g n) -> p g n", g=12), AX_X,
                                    ALU.add).then_inc(s_gn_var, 1)
                for i in range(2):
                    dve.wait_ge(s_gn_rstd, g0 + i + 1)
                    V.tensor_tensor(gn_y[:, i, :, :], gn_y[:, i, :, :],
                                    gn_rstd[:, i, :].rearrange("p (g n) -> p g n", n=1).to_broadcast([P, 12, RET_DV]),
                                    ALU.mult).then_inc(s_gn_norm, 1)

            def conv_centre(l):
                n = NQ[l] * P
                dve.wait_ge(s_cmean_ps, l + 1)
                for c in range(2):
                    V.tensor_tensor(acc[:, c, 0:n], acc[:, c, 0:n], ps[:, 0, 0:n], ALU.subtract).then_inc(s_ccent, 1)

            def conv_scale(l):
                n = NQ[l] * P
                dve.wait_ge(s_cstd, l + 1)
                chain(V.reciprocal(conv_std[:, 0:n], conv_std[:, 0:n]))
                for c in range(2):
                    V.tensor_tensor(acc[:, c, 0:n], acc[:, c, 0:n], conv_std[:, 0:n], ALU.mult).then_inc(s_cnorm, 1)

            def rope_q(l, t):
                dve.wait_ge(s_mla_sb, before(l, per_mla) + 10 + 2 * (t + 1))
                rotate(q_stage[:, t, :].rearrange("p (h r) -> p h r", h=HEADS)[:, :, D_NOPE:], t, HEADS,
                       s_q_rope, 2 * l + t + 1)

            def attention(l):
                n0 = before(l, per_attn)
                items = ATTN[l]

                def row_max(i):
                    t, h = items[i]
                    n = n0 + i
                    dve.wait_ge(s_score_ps, n + 1)
                    V.tensor_reduce(neg_max[:, n % 2:n % 2 + 1], ps[:, n % 2, 0:512 if t < 2 else SEQ], AX_X, ALU.max,
                                    negate=True).then_inc(s_max, 1)

                def copy_pT(i):
                    t, h = items[i]
                    n = n0 + i
                    w = 512 if t < 2 else SEQ
                    dve.wait_ge(s_pT_ps, n + 1)
                    if i >= 2:
                        dve.wait_ge(s_pv, n - 1)
                    V.tensor_copy(probsT[:, n % 2, 0:w], ps[:, 2 + n % 2, 0:w]).then_inc(s_pT, 1)

                def finish(i):
                    t, h = items[i]
                    if h < HEADS - 1:
                        return
                    dve.wait_ge(s_pv, n0 + i + 1)
                    chain(V.reciprocal(prob_sum[:, t, :], prob_sum[:, t, :]))
                    V.tensor_tensor(o_mla[:, t, :].rearrange("p (h n) -> p h n", h=HEADS),
                                    ps[:, 4 + t, 0:HEADS * D_V].rearrange("p (h n) -> p h n", h=HEADS),
                                    prob_sum[:, t, :].rearrange("p (h n) -> p h n", n=1).to_broadcast([P, HEADS, D_V]),
                                    ALU.mult).then_inc(s_mla_out, 1)

                row_max(0)
                for i in range(len(items)):
                    if i + 1 < len(items):
                        row_max(i + 1)
                    copy_pT(i)
                    if i:
                        finish(i - 1)
                finish(len(items) - 1)

            def residual(l):
                for c in range(2):
                    for t in range(NQ[l]):
                        i = c * NQ[l] + t
                        j = 2 * before(l, NQ) + i
                        cols = slice(c * 512, (c + 1) * 512)
                        dve.wait_ge(s_out_ps, j + 1)
                        if j:
                            dve.wait_ge(s_x1, j)
                        chain(V.tensor_tensor(tmp[:, 0:512], ps[:, 4 + i % 4, :], mod[:, GATE_Q, t // 2, cols], ALU.mult))
                        V.tensor_tensor(x[:, t, cols], x[:, t, cols], tmp[:, 0:512], ALU.add).then_inc(s_x1, 1)

            def route(l):
                n = NQ[l]
                scr = tmp[:, :]
                at = [0]

                def take(shape):
                    size = 1
                    for d in shape:
                        size *= d
                    v = scr[:, at[0]:at[0] + size]
                    at[0] += size
                    names = "abcd"[:len(shape)]
                    kw = dict(zip(names, shape))
                    return v.rearrange(f"p ({' '.join(names)}) -> p {' '.join(names)}", **kw)

                grp = n * N_GROUPS
                dve.wait_ge(s_aff, l + 1)
                choice = take([n, N_EXPERTS])
                c4 = choice.rearrange("p t (g e) -> p (t g) e", g=N_GROUPS)
                chain(V.tensor_tensor(choice, aff[:, 0:n, :],
                                      r_bias[:, :].rearrange("p (t n) -> p t n", t=1).to_broadcast([P, n, N_EXPERTS]), ALU.add))
                pairs = take([grp, 6])
                V.tensor_tensor(pairs[:, :, 0:3], c4[:, :, 0:3], c4[:, :, 1:4], ALU.add)
                V.tensor_tensor(pairs[:, :, 3:5], c4[:, :, 0:2], c4[:, :, 2:4], ALU.add)
                chain(V.tensor_tensor(pairs[:, :, 5:6], c4[:, :, 0:1], c4[:, :, 3:4], ALU.add))
                score = take([grp])
                chain(V.tensor_reduce(score, pairs, AX_X, ALU.max))
                s4 = score.rearrange("p (t g) -> p t g", g=N_GROUPS)
                best = take([n])
                chain(V.tensor_reduce(best, s4, AX_X, ALU.max))

                def spread(v, k):
                    return v.rearrange("p (t n) -> p t n", n=1).to_broadcast([P, n, k])

                ranks = rank16[:, :].rearrange("p (t n) -> p t n", t=1)

                def first_best(values, top, k, out_mask):
                    chain(V.tensor_tensor(out_mask, values, spread(top, k), ALU.is_ge))
                    chain(V.tensor_tensor(out_mask, out_mask, ranks[:, :, 0:k].to_broadcast([P, n, k]), ALU.mult))
                    chain(V.tensor_reduce(top, out_mask, AX_X, ALU.max))
                    chain(V.tensor_tensor(out_mask, out_mask, spread(top, k), ALU.is_equal))

                chosen_group = in_group(n)
                first_best(s4, best, N_GROUPS, chosen_group)
                outside = take([n, N_GROUPS])
                V.tensor_scalar(outside, chosen_group, BIG, -BIG, ALU.mult, ALU.add).then_inc(s_group, 1)
                dve.wait_ge(s_group, l + 1)
                ig = chosen_group.rearrange("p t g -> p (t g)").rearrange("p (g e) -> p g e", e=1).to_broadcast([P, grp, EPG])
                og = outside.rearrange("p t g -> p (t g)").rearrange("p (g e) -> p g e", e=1).to_broadcast([P, grp, EPG])
                chain(V.tensor_tensor(c4, c4, ig, ALU.mult))
                chain(V.tensor_tensor(c4, c4, og, ALU.add))
                chosen = []
                for j in range(2):
                    mask = take([n, N_EXPERTS])
                    chain(V.tensor_reduce(best, choice, AX_X, ALU.max))
                    first_best(choice, best, N_EXPERTS, mask)
                    chosen.append(mask)
                    if j == 0:
                        chain(V.scalar_tensor_tensor(out=choice, in0=mask, scalar=-4.0 * BIG, in1=choice,
                                                     op0=ALU.mult, op1=ALU.add))
                chain(V.tensor_tensor(chosen[0], chosen[0], chosen[1], ALU.add))
                chain(V.tensor_tensor(chosen[0], chosen[0], aff[:, 0:n, :], ALU.mult))
                chain(V.tensor_reduce(best, chosen[0], AX_X, ALU.add))
                chain(V.reciprocal(best, best))
                V.tensor_tensor(h2[:, 0:n, D:SLOT_W], chosen[0], spread(best, N_EXPERTS), ALU.mult)

                dve.wait_ge(s_rank_ps, l + 1)
                rank, over = take([n, N_GROUPS]), take([n, N_GROUPS])
                own = [group_slot[:, j:j + 1, :].to_broadcast([P, n, N_GROUPS]) for j in range(2)]
                got = ps[:, 4, 64:64 + 4 * n].rearrange("p (t g) -> p t g", t=n)
                V.tensor_scalar(rank, got, float(CONV_W), None, ALU.mult)
                chain(V.tensor_scalar(over, got, GROUP_SLOTS / CONV_W, None, ALU.is_ge))
                V.tensor_tensor(rank, rank, own[0], ALU.add)
                chain(V.tensor_tensor(over, over, own[1], ALU.mult))
                chain(V.tensor_tensor(rank, rank, over, ALU.add))
                chain(V.tensor_tensor(rank, rank, chosen_group, ALU.mult))
                chain(V.tensor_reduce(best, rank, AX_X, ALU.add))
                V.tensor_copy(slot_of[:, 0:n], best).then_inc(s_gates, 1)

                counts = ps[0:1, 4, 96:100]
                many = scr[0:1, at[0]:at[0] + 4]
                total = scr[0:1, at[0] + 4:at[0] + 8]
                V.tensor_scalar(flags[0:1, 0:4], counts, P / CONV_W, None, ALU.is_gt)
                chain(V.tensor_scalar(many, counts, GROUP_SLOTS / CONV_W, None, ALU.is_gt))
                chain(V.tensor_reduce(total[:, 0:1], many, AX_X, ALU.add))
                chain(V.tensor_tensor(many, many, group_slot[0:1, 0, :], ALU.mult))
                chain(V.tensor_reduce(total[:, 1:2], many, AX_X, ALU.add))
                V.tensor_copy(flags[0:1, 4:5], total[:, 0:1])
                V.tensor_scalar(flags[0:1, 5:6], total[:, 1:2], 1.0 / GROUP_SLOTS, None, ALU.mult).then_inc(s_flags, 1)

            def experts(l):
                over_gate = tmp[:, 0:2 * EPG].rearrange("p (c e) -> p c e", c=2)

                def hidden(g, items, k):
                    e, c = items[k]
                    gg = groups_before(l) + g
                    i = 8 * gg + k
                    if items is SHORT and k == 6:
                        dve.drain().then_inc(s_he, 4)
                    dve.wait_ge(s_silu, i + 1)
                    if ended(gg, items, k, 2) > 0:
                        dve.wait_ge(s_heT_ps, ended(gg, items, k, 2))
                    col = D + EPG * g + e
                    gate = over_gate[:, c, e:e + 1] if g == N_GROUPS else slot_tok[:, g % 2, c, col:col + 1]
                    V.scalar_tensor_tensor(out=he_buf[:, i % 2, :], in0=silu_buf[:, i % 2, :], scalar=gate,
                                           in1=ps[:, i % 2, D_EXPERT:2 * D_EXPERT], op0=ALU.mult, op1=ALU.mult).then_inc(s_he, 1)

                def rows_out(g, c):
                    gg = groups_before(l) + g
                    dve.wait_ge(s_y_ps, 8 * gg + 8 - c)
                    if gg:
                        dve.wait_ge(s_y_out[c], 16 * gg)
                    V.tensor_copy(y_moe[:, c, :], ps[:, 4 + 2 * c:6 + 2 * c, :].rearrange("p b n -> p (b n)")).then_inc(s_y[c], 1)

                def body(g, items):
                    for k in list(items)[1:]:
                        hidden(g, items, k)
                    if items is WHOLE:
                        rows_out(g, 1)
                    else:
                        dve.drain().then_inc(s_y[1], 1)

                dve.wait_ge(s_flags, l + 1)
                for g in range(N_GROUPS):
                    dve.wait_ge(s_slot[g % 2], 32 * (2 * l + g // 2 + 1))
                    hidden(g, WHOLE, 0)
                    if g:
                        rows_out(g - 1, 0)
                    second = dve.value_load(flags[0:1, g:g + 1], min_val=0, max_val=1)
                    with dve.If(second > 0):
                        body(g, WHOLE)
                    with dve.Else():
                        body(g, SHORT)
                rows_out(N_GROUPS - 1, 0)
                if group_passes[l] > N_GROUPS:
                    over = dve.value_load(flags[0:1, 4:5], min_val=0, max_val=1)
                    with dve.If(over > 0):
                        dve.wait_ge(s_over_slot, 32)
                        cols = slot_tok[:, 0, :, D:SLOT_W].rearrange("p c (g e) -> p c e g", g=N_GROUPS)
                        V.tensor_reduce(over_gate, cols, AX_X, ALU.add).then_inc(s_over_gate, 1)
                        dve.wait_ge(s_over_gate, 1)
                        hidden(N_GROUPS, WHOLE, 0)
                        body(N_GROUPS, WHOLE)
                        rows_out(N_GROUPS, 0)
                    with dve.Else():
                        dve.drain().then_inc(s_he, 8)
                        for c in range(2):
                            dve.drain().then_inc(s_y[c], 1)
                for t in range(NQ[l]):
                    dve.wait_ge(s_back[t], 16 * (l + 1))
                    chain(V.tensor_tensor(y_back[:, t, :], y_back[:, t, :], mod[:, GATE_Q, t // 2, :], ALU.mult))
                    V.tensor_tensor(x[:, t, :], x[:, t, :], y_back[:, t, :], ALU.add).then_inc(s_x2, 1)

            dve.wait_ge(s_const, 16 * N_CONST)
            for l in range(DEPTH):
                modulation(l, 0)
                scale_tiles(l, 0, NT)
                glu(l)
                rope_qk(l)
                norm_latents(l)
                taps(l)
                masks(l, 0)
                conv_centre(l)
                groupnorm(l, 0)
                conv_scale(l)
                if RET_PASSES[l] == 2:
                    masks(l, 1)
                    groupnorm(l, 1)
                for t in range(2):
                    rope_q(l, t)
                attention(l)
                residual(l)
                modulation(l, 1)
                scale_tiles(l, 1, NQ[l])
                route(l)
                experts(l)
            dve.wait_ge(s_normw, 16 * (2 * DEPTH + 1))
            for t in range(2):
                i = norm_base(DEPTH, 0) + t
                dve.wait_ge(s_rstd, i + 1)
                V.scalar_tensor_tensor(out=h_tok[:, i % 2, :], in0=x[:, t, :], scalar=rstd[:, t:t + 1],
                                       in1=norm_w, op0=ALU.mult, op1=ALU.mult).then_inc(s_final, 1)

        @block.gpsimd
        def _(pool):
            G = nc.gpsimd
            steps = [0]

            def chain(ins):
                steps[0] += 1
                ins.then_inc(s_pool, 1)
                pool.wait_ge(s_pool, steps[0])

            def inverse_root(v, n, eps):
                w = v.shape[-1]
                chain(G.tensor_scalar(v, v, 1.0 / n, eps, ALU.mult, ALU.add))
                return G.tensor_tensor(v, v, half_neg[:, 0:w], ALU.pow)

            def zero_bias(l, a):
                G.memset(ada_bias, 0.0).then_inc(s_bias_zero, 1)

            def norm(l, a, tiles, shift=True):
                for t in range(tiles):
                    i = norm_base(l, a) + t
                    pool.wait_ge(s_sumsq, i + 1)
                    inverse_root(rstd[:, t:t + 1], D, EPS).then_inc(s_rstd, 1)
                if shift:
                    for t in range(tiles):
                        i = norm_base(l, a) + t
                        pool.wait_ge(s_scaled, i + 1)
                        h = h2[:, t, 0:D] if a else h_tok[:, i % 2, :]
                        G.tensor_tensor(h, h, mod[:, SHIFT_Q, t // 2, :], ALU.add).then_inc(s_h, 1)

            def dispatch(l):
                pool.wait_ge(s_gates, l + 1)
                pool.wait_ge(s_filled, 16 * (SLOTS // P))
                for t in range(NQ[l]):
                    pool.indirect_dma_start(out=slots, out_offset=bass.IndirectOffsetOnAxis(ap=slot_of[:, t:t + 1], axis=0),
                                            in_=h2[:, t, :], in_offset=None).then_inc(s_scattered, 16)

                def store(g, c):
                    gg = groups_before(l) + g
                    pool.wait_ge(s_y[c], gg + 1)
                    r0 = (2 * g + c) * P
                    pool.dma_start(y_slots[r0:r0 + P, :], y_moe[:, c, :]).then_inc(s_y_out[c], 16)

                for g in range(group_passes[l]):
                    store(g, 1)
                    store(g, 0)
                for c in range(2):
                    pool.wait_ge(s_y_out[c], 16 * groups_before(l + 1))
                for t in range(NQ[l]):
                    pool.indirect_dma_start(out=y_back[:, t, :], out_offset=None, in_=y_slots,
                                            in_offset=bass.IndirectOffsetOnAxis(ap=slot_of[:, t:t + 1], axis=0)
                                            ).then_inc(s_back[t], 16)

            G.memset(zero_rows, 0.0).then_inc(s_fill, 1)
            for g in range(N_GROUPS):
                G.memset(group_slot[:, 0, g:g + 1], float(g * GROUP_SLOTS))
                G.memset(group_slot[:, 1, g:g + 1], float((N_GROUPS - 1 - g) * GROUP_SLOTS))
            G.memset(ones_mean[:, :], 1.0 / CONV_W)
            G.memset(eps_col[:, :], EPS)
            G.memset(half_neg[:, :], -0.5)
            G.memset(c_pad[:, :, :], 0.0).then_inc(s_ones, 1)
            pool.wait_ge(s_ones, 1)
            pool.wait_ge(s_const, 16 * N_CONST)
            for l in range(DEPTH):
                if l:
                    pool.wait_ge(s_ada_rows, l * ada_per_layer)
                    pool.wait_ge(s_x2, before(l, NQ))
                zero_bias(l, 0)
                for e0 in (0, CONV_K // 2 + SEQ):
                    last = G.memset(conv_in[:, :, :, e0:e0 + CONV_K // 2], 0.0)
                last.then_inc(s_pad, 1)
                norm(l, 0, NT)
                for t in range(NT):
                    pool.wait_ge(s_lat_sq, NT * l + t + 1)
                    if t < NQ[l]:
                        chain(G.tensor_scalar(lat_rstd[:, t, 0:1], lat_sumsq[:, t, 0:1], 1.0 / Q_RANK, EPS, ALU.mult, ALU.add))
                    chain(G.tensor_scalar(lat_rstd[:, t, 1:2], lat_sumsq[:, t, 1:2], 1.0 / KV_RANK, EPS, ALU.mult, ALU.add))
                    v = lat_rstd[:, t, 0 if t < NQ[l] else 1:2]
                    G.tensor_tensor(v, v, half_neg[:, 0:v.shape[-1]], ALU.pow).then_inc(s_lat_rstd, 1)
                pool.wait_ge(s_latT, lat_evacs(l, NT))
                for h in range(1, HEADS):
                    last = G.tensor_copy(KT[D_NOPE:D_QK, h, :], KT[D_NOPE:D_QK, 0, :])
                last.then_inc(s_kr, 1)
                pool.wait_ge(s_kr, l + 1)
                for s in range(RET_PASSES[l]):
                    g0 = 2 * (before(l, RET_PASSES) + s)
                    for i in range(2):
                        pool.wait_ge(s_gn_var, g0 + i + 1)
                        inverse_root(gn_rstd[:, i, :], RET_DV, GN_EPS).then_inc(s_gn_rstd, 1)
                    for i in range(2):
                        t = 2 * s + i
                        pool.wait_ge(s_gn_norm, g0 + i + 1)
                        for f in range(2):
                            last = G.tensor_tensor(gate_act[:, f, t, :], gate_act[:, f, t, :],
                                                   gn_y[:, i, 6 * f:6 * f + 6, :].rearrange("p h n -> p (h n)"), ALU.mult)
                        chain(last)
                        G.tensor_tensor(gate_act[:, 0, t, :], gate_act[:, 0, t, :], gate_act[:, 1, t, :],
                                        ALU.add).then_inc(s_ret_out, 1)
                zero_bias(l, 1)
                norm(l, 1, NQ[l])
                dispatch(l)
            norm(DEPTH, 0, 2, shift=False)


def _constants():
    import numpy as np

    ident = np.eye(P, dtype=np.float32)
    sel = np.zeros((P, 2, P), np.float32)
    for s in range(2):
        sel[s::32, s, :] = 1.0
    p = np.arange(P)[:, None, None].astype(np.float64)
    n = np.arange(384)[None, None, :]
    g = gamma(np.arange(HEADS, dtype=np.float64))[None, :, None]
    fwd, bwd = n - p, p + SEQ - n
    decay = np.stack([np.where(fwd >= 0, g ** np.maximum(fwd, 0), 0.0),
                      np.where(bwd >= 0, g[:, ::-1] ** np.maximum(bwd, 0), 0.0)], axis=1).astype(np.float32)
    t = np.arange(SEQ).reshape(2, P)
    inv = 10000.0 ** (-np.arange(8, dtype=np.float64) / 8)
    rope = np.zeros((P, 2, 2, D_ROPE), np.float32)
    for i in range(2):
        for g2, pos in enumerate((t[i] // 64, t[i] % 64)):
            ang = pos[:, None] * inv
            for b in range(2):
                cols = slice(16 * g2 + 8 * b, 16 * g2 + 8 * b + 8)
                rope[:, i, 0, cols] = np.cos(ang)
                rope[:, i, 1, cols] = np.sin(ang) * (1 if b else -1)
    rank = np.broadcast_to(np.arange(N_EXPERTS, 0, -1, dtype=np.float32), (P, N_EXPERTS)).copy()
    tri = np.triu(np.ones((P, P), np.float32), 1) / CONV_W
    return {"const_ident": ident, "const_tri": tri, "const_sel": sel, "const_decay": decay, "const_rope": rope, "const_rank": rank}


_INS = ["x", "c", "ctx", "c_ctx", "ada_w", "ada_b", "norm1_w", "norm2_w", "w_in", 
        "mla_w_uq", "mla_kv_norm_w", "mla_w_ukv", "w_out", "router_w", "router_bias", "moe_w_gate",
        "moe_w_up", "moe_w_down", "final_norm_w"]


def kernel(**inputs):
    import numpy as np
    import concourse.bacc as bacc
    from concourse.bass_utils import run_bass_kernel_spmd

    nc = bacc.Bacc("TRN2", target_bir_lowering=False, num_devices=1, dynamic_dma_scratch_size=2048)
    arrays = {name: np.ascontiguousarray(inputs[name]) for name in _INS}
    cols = np.concatenate([np.asarray(inputs["conv_dw"])] +
                          [np.asarray(inputs[name])[:, None] for name in ("conv_b", "conv_ln_w", "conv_ln_b")], axis=1)
    arrays["conv_cols"] = np.ascontiguousarray(cols.reshape(DEPTH, CONV_K + 3, 2, P).transpose(0, 3, 2, 1))
    arrays["q_norm_cols"] = np.ascontiguousarray(np.asarray(inputs["mla_q_norm_w"]).reshape(DEPTH, 2, 96).transpose(0, 2, 1))
    arrays.update(_constants())
    dram = {name: nc.dram_tensor(f"in_{name}", a.shape, mybir.dt.from_np(a.dtype), kind="ExternalInput").ap()
            for name, a in arrays.items()}
    out = nc.dram_tensor("out_0", (1, SEQ, D), F32, kind="ExternalOutput").ap()
    build(nc, dram, out)
    r = run_bass_kernel_spmd(nc, [{f"in_{name}": a for name, a in arrays.items()}], core_ids=[0])
    return r.results[0]["out_0"]
```

```python
from contextlib import ExitStack

import concourse.bass as bass
from concourse import mybir

P = 128
D = 1024
DEPTH = 2
SEQ = 256
NT = 4
KD = D // P
CONV_W, CONV_K = 256, 31
HEADS, RET_DK, RET_DV = 6, 32, 64
CHUNK_PAD = SEQ + CONV_K - 1
Q_RANK, KV_RANK, D_NOPE, D_ROPE, D_V = 192, 128, 64, 32, 64
D_QK = D_NOPE + D_ROPE
MLA_SCALE = float(D_QK) ** -0.5
N_EXPERTS, EPG, D_EXPERT = 16, 4, 256
N_GROUPS = N_EXPERTS // EPG
EPS, GN_EPS = 1e-6, 1e-5
QKW, VW = 2 * HEADS * RET_DK, HEADS * RET_DV
LATW = Q_RANK + KV_RANK + D_ROPE
BIG = 1e30
GROUP_SLOTS = 2 * P
SLOTS = (N_GROUPS + 1) * GROUP_SLOTS
SLOT_W = D + N_EXPERTS
F32 = mybir.dt.float32
BF16 = mybir.dt.bfloat16
ACT = mybir.ActivationFunctionType
ALU = mybir.AluOpType
AX_X = mybir.AxisListType.X

NQ = [4, 2]
QK_U, CONV_U, V_U, LAT_U, GF_U, GB_U = range(6)
UNIT_COLS = [(512, QKW), (0, 512), (896, VW), (2048, LATW), (1280, VW), (1664, VW)]
N_WSLOT = 3
SCALE_Q, SHIFT_Q, GATE_Q = 0, 1, 2
MOD_UNITS = [(SHIFT_Q, 0), (SHIFT_Q, 1), (SCALE_Q, 0), (SCALE_Q, 1), (GATE_Q, 0), (GATE_Q, 1)]


def gamma(h):
    return 1.0 - 2.0 ** (-5.0 - h)


def plan():
    units, mods, ends = [], [], []
    in_slot = [[] for _ in range(N_WSLOT)]
    for l in range(DEPTH):
        turning = []
        if l == 0:
            turning += [("ada", 0, 0, u) for u in range(4)]
        turning += [("in", l, u) for u in (QK_U, CONV_U, V_U)]
        if l == 0:
            turning += [("ada", 0, 0, u) for u in (4, 5)]
        turning += [("in", l, LAT_U), ("ada", l, 1, 4), ("in", l, GF_U), ("ada", l, 1, 5), ("in", l, GB_U)]
        turning += [("ada", l, 1, u) for u in range(4)]
        for i, unit in enumerate(turning):
            in_slot[i % N_WSLOT].append(len(units))
            units.append(unit)
        for slot, unit in [(c, ("out", l, c)) for c in range(2)] + \
                          [(2, ("ada", l + 1, 0, u)) for u in range(6) if l + 1 < DEPTH]:
            in_slot[slot].append(len(units))
            units.append(unit)
        ends.append(len(units))
        for a in range(2):
            for u, (q, half) in enumerate(MOD_UNITS):
                both = l == 0 or (a == 0 and q != GATE_Q)
                mods += [(l, a, u, s) for s in range(2 if both else 1)]
    return units, in_slot, ends, mods


def build(nc, dram, out):
    units, in_slot, layer_ends, mods = plan()
    unit_at = {u: n for n, u in enumerate(units)}
    mod_at = {m: n for n, m in enumerate(mods)}
    slot_at = {n: (j, ns.index(n)) for j, ns in enumerate(in_slot) for n in ns}
    ada_per_layer = 12

    def ada_at(l, a, u):
        return l * ada_per_layer + a * 6 + ((u + 2) % 6 if a else u)

    ada_by_experts = [min(ada_per_layer * (l + 1) + 6, ada_per_layer * DEPTH) for l in range(DEPTH)]
    group_passes = [N_GROUPS + (NQ[l] * P > 2 * GROUP_SLOTS - 1) for l in range(DEPTH)]

    def before(l, per):
        return sum(per[:l])

    with ExitStack() as ctx:
        def sb(name, shape, dt=F32):
            return ctx.enter_context(nc.sbuf_tensor(name, shape, dt))

        def sem(name):
            return ctx.enter_context(nc.semaphore(name))

        ps = ctx.enter_context(nc.psum_tensor("ps", [P, 8, 512], F32))

        wring = sb("wring", [P, N_WSLOT, 4096])
        x = sb("x", [P, NT, D])
        hT_buf = sb("hT_buf", [P, 4096])
        mod = sb("mod", [P, 3, 2, D])
        work1 = sb("work1", [P, 4096])
        decay = sb("decay", [P, 2, HEADS, SEQ])
        q_decay = sb("q_decay", [P, 2, 2, SEQ])
        k_decay = sb("k_decay", [P, 2, 2, HEADS])
        work2 = sb("work2", [P, 2176])
        convT = sb("convT", [P, 2, 512])
        tokens = sb("tokens", [P, 3 * NT * VW])
        v_mla = sb("v_mla", [P, NT, HEADS * D_V])
        o_mla = sb("o_mla", [P, NT, HEADS * D_V])
        stage = sb("stage", [P, 1536])
        tmp = sb("tmp", [P, 768])
        w_uq = sb("w_uq", [P, 2, HEADS * D_QK])
        w_ukv = sb("w_ukv", [P, HEADS * P])
        cqT = sb("cqT", [P, 2, 512])
        ckvT = sb("ckvT", [P, 512])
        sel = sb("sel", [P, 2, P])
        ident = sb("ident", [P, P])
        ones_mean = sb("ones_mean", [P, P])
        rope = sb("rope", [P, 2, 2, D_ROPE])
        router_w = sb("router_w", [P, KD, N_EXPERTS])
        c_raw = sb("c_raw", [P, 2, KD])
        c_pad = sb("c_pad", [P, KD, 32])
        conv_vec = sb("conv_vec", [P, 2, CONV_K + 3])
        dw = conv_vec[:, :, 0:CONV_K]
        q_norm = sb("q_norm", [P, 2])
        kv_norm = sb("kv_norm", [P, 1])
        eps_col = sb("eps_col", [P, 1])
        half_neg = sb("half_neg", [P, 12])
        rstd = sb("rstd", [P, NT])
        lat_sumsq = sb("lat_sumsq", [P, NT, 2])
        lat_rstd = sb("lat_rstd", [P, NT, 2])
        gn_mean = sb("gn_mean", [P, 2, 12])
        gn_rstd = sb("gn_rstd", [P, 2, 12])
        neg_max = sb("neg_max", [P, 2])
        prob_sum = sb("prob_sum", [P, NT, HEADS])
        aff = sb("aff", [P, NT, N_EXPERTS])
        r_bias = sb("r_bias", [P, N_EXPERTS])
        rank16 = sb("rank16", [P, N_EXPERTS])
        tri = sb("tri", [P, P])
        group_slot = sb("group_slot", [P, 2, N_GROUPS])
        slot_of = sb("slot_of", [P, NT], mybir.dt.uint32)
        ada_bias = sb("ada_bias", [P, 2, 512])
        gate_rows = sb("gate_rows", [P, 2, 512])
        flags = sb("flags", [1, 8], mybir.dt.int32)

        hT = hT_buf[:, :].rearrange("p (k n) -> p k n", k=KD)
        retT = hT_buf[:, 0:HEADS * SEQ].rearrange("p (h n) -> p h n", h=HEADS)
        oT = hT_buf[:, 0:6 * 512].rearrange("p (k n) -> p k n", k=6)
        norm_w = work1[:, D:2 * D]
        v_ret = tokens[:, 0:NT * VW].rearrange("p (t n) -> p t n", t=NT)
        gate_act = tokens[:, NT * VW:3 * NT * VW].rearrange("p (f t n) -> p f t n", f=2, t=NT)
        h2 = tokens[:, 0:NT * SLOT_W].rearrange("p (t n) -> p t n", t=NT)
        slot_tok = tokens[:, 0:4 * SLOT_W].rearrange("p (b c n) -> p b c n", b=2, c=2)
        y_back = tokens[:, 0:NT * D].rearrange("p (t n) -> p t n", t=NT)
        zero_rows = w_uq[:, :, :].rearrange("p k n -> p (k n)")[:, 0:SLOT_W]
        slot_hT = hT_buf[:, :].rearrange("p (b c k n) -> p b c k n", b=2, c=2, k=KD)
        h_tok = work1[:, 2 * D:4 * D].rearrange("p (b n) -> p b n", b=2)
        conv_sig = h_tok[:, :, 0:512]
        qkT = work1[:, 0:2048].rearrange("p (f n) -> p f n", f=4)
        masked = [half.rearrange("p (f j n) -> p f j n", f=2, j=2) for half in (work1[:, 2048:3072], hT_buf[:, 2048:3072])]
        qT = work1[0:D_QK, 0:HEADS * 512].rearrange("p (h n) -> p h n", h=HEADS)
        KT = mod[0:D_QK, 0:2, :, :].rearrange("p a b n -> p (a b n)")[:, 0:HEADS * 512].rearrange(
            "p (h n) -> p h n", h=HEADS)
        conv_in = work2[:, 0:2 * 2 * CHUNK_PAD].rearrange("p (c s n) -> p c s n", c=2, s=2)
        conv_sq = work2[:, 0:1024].rearrange("p (c n) -> p c n", c=2)
        conv_std = work2[:, 0:512]
        acc = work2[:, 1144:2168].rearrange("p (c n) -> p c n", c=2)
        q_stage = work2[:, 0:1152].rearrange("p (b n) -> p b n", b=2)
        probs = work2[:, 0:1024].rearrange("p (b n) -> p b n", b=2)
        probsT = work2[:, 1024:2048].rearrange("p (b n) -> p b n", b=2)
        y_moe = work2[:, 0:2048].rearrange("p (c n) -> p c n", c=2)
        qk_tok = stage[:, 0:NT * QKW].rearrange("p (t n) -> p t n", t=NT)
        lat_tok = stage[:, 0:NT * LATW].rearrange("p (t n) -> p t n", t=NT)
        gn_y = stage[:, 0:1536].rearrange("p (i g n) -> p i g n", i=2, g=12)
        gn_squares = [v.rearrange("p (g n) -> p g n", g=12)
                      for v in (tmp[:, :], cqT[:, :, :].rearrange("p k n -> p (k n)")[:, 0:768])]
        junk = o_mla[:, 0, 0:Q_RANK]
        square_junk = tmp[:, 0:512].bitcast(BF16)
        silu_buf = work1[:, 0:512].rearrange("p (b n) -> p b n", b=2)
        he_buf = work1[:, 512:1024].rearrange("p (b n) -> p b n", b=2)
        heT_buf = work1[:, 2 * D:2 * D + 512].rearrange("p (b n) -> p b n", b=2)
        h2T = work2[:, 0:2 * D].rearrange("p (b k n) -> p b k n", b=2, k=KD)
        gu = [wring[:, j, :].rearrange("p (k n) -> p k n", k=KD) for j in range(2)]
        dn = [wring[:, 2, j * 2048:(j + 1) * 2048].rearrange("p (f n) -> p f n", f=2) for j in range(2)]

        def unit_view(n):
            kind = units[n][0]
            cols = UNIT_COLS[units[n][2]][1] if kind == "in" else 512
            return wring[:, slot_at[n][0], 0:KD * cols].rearrange("p (k n) -> p k n", k=KD)

        def mod_rows(l, a, u):
            if a == 0:
                held = (v_mla, o_mla)[u // 3][:, :, :].rearrange("p t n -> p (t n)")
                return held[:, u % 3 * 512:u % 3 * 512 + 512]
            if u >= 4:
                return gate_rows[:, u - 4, :]
            c0 = u * 512 if u < 3 else 2 * NT * VW
            return tokens[:, c0:c0 + 512]

        k_state = v_mla[:, 0:2, :].rearrange("p a b -> p (a b)")[:, 0:768].rearrange("p (f j n) -> p f j n", f=2, j=2)
        state = v_mla[:, 2:4, :].rearrange("p a b -> p (a b)").rearrange("p (h f n) -> p h f n", h=HEADS, f=2)
        q_state = o_mla[:, :, :].rearrange("p t n -> p (t n)")[:, 512:1536].rearrange("p (a f n) -> p a f n", a=2, f=2)

        s_cond = sem("s_cond")
        s_x = sem("s_x")
        s_ctx = sem("s_ctx")
        s_const = sem("s_const")
        s_small = sem("s_small")
        s_uq = sem("s_uq")
        s_wslot = [sem(f"s_wslot{j}") for j in range(N_WSLOT)]
        s_bias = [sem(f"s_bias{j}") for j in range(2)]
        s_normw = sem("s_normw")
        s_gu = [[sem(f"s_gu{j}_{b}") for b in range(2)] for j in range(2)]
        s_dn = [sem(f"s_dn{j}") for j in range(2)]
        s_ones = sem("s_ones")
        s_cpad = sem("s_cpad")
        s_bias_zero = sem("s_bias_zero")
        s_ada_part = sem("s_ada_part")
        s_ada_rows = sem("s_ada_rows")
        s_ada_bc = sem("s_ada_bc")
        s_mod = sem("s_mod")
        s_sumsq = sem("s_sumsq")
        s_rstd = sem("s_rstd")
        s_scaled = sem("s_scaled")
        s_h = sem("s_h")
        s_hT_ps = sem("s_hT_ps")
        s_hT = sem("s_hT")
        s_conv_ps = sem("s_conv_ps")
        s_sig = sem("s_sig")
        s_glu = sem("s_glu")
        s_pad = sem("s_pad")
        s_proj_ps = sem("s_proj_ps")
        s_proj = sem("s_proj")
        s_qk_rope = sem("s_qk_rope")
        s_qkT_ps = sem("s_qkT_ps")
        s_qkT = sem("s_qkT")
        s_lat_sq = sem("s_lat_sq")
        s_lat_rstd = sem("s_lat_rstd")
        s_lat_norm = sem("s_lat_norm")
        s_latT_ps = sem("s_latT_ps")
        s_latT = sem("s_latT")
        s_kr = sem("s_kr")
        s_taps = sem("s_taps")
        s_cmean_ps = sem("s_cmean_ps")
        s_ccent = sem("s_ccent")
        s_csq = sem("s_csq")
        s_cvar_ps = sem("s_cvar_ps")
        s_cstd = sem("s_cstd")
        s_cnorm = sem("s_cnorm")
        s_convT = sem("s_convT")
        s_k_state = sem("s_k_state")
        s_q_state = sem("s_q_state")
        s_state_ps = sem("s_state_ps")
        s_state = sem("s_state")
        s_state_zero = sem("s_state_zero")
        s_ret_ps = sem("s_ret_ps")
        s_mask = [sem("s_mask_f"), sem("s_mask_b")]
        s_ret_pv = [sem("s_ret_pv_f"), sem("s_ret_pv_b")]
        s_retT = sem("s_retT")
        s_retT_ps = sem("s_retT_ps")
        s_gn_y = sem("s_gn_y")
        s_gn_cent = sem("s_gn_cent")
        s_gn_sq = sem("s_gn_sq")
        s_gn_var = sem("s_gn_var")
        s_gn_rstd = sem("s_gn_rstd")
        s_gn_norm = sem("s_gn_norm")
        s_ret_out = sem("s_ret_out")
        s_mla_ps = sem("s_mla_ps")
        s_mla_sb = sem("s_mla_sb")
        s_q_rope = sem("s_q_rope")
        s_qT_ps = sem("s_qT_ps")
        s_qT = sem("s_qT")
        s_score_ps = sem("s_score_ps")
        s_max = sem("s_max")
        s_exp = sem("s_exp")
        s_pT_ps = sem("s_pT_ps")
        s_pT = sem("s_pT")
        s_pv = sem("s_pv")
        s_mla_out = sem("s_mla_out")
        s_oT_ps = sem("s_oT_ps")
        s_oT = sem("s_oT")
        s_out_ps = sem("s_out_ps")
        s_x1 = sem("s_x1")
        s_logit_ps = sem("s_logit_ps")
        s_aff = sem("s_aff")
        s_gates = sem("s_gates")
        s_over_gate = sem("s_over_gate")
        s_group = sem("s_group")
        s_rank_ps = sem("s_rank_ps")
        s_count_ps = sem("s_count_ps")
        s_flags = sem("s_flags")
        s_fill = sem("s_fill")
        s_filled = sem("s_filled")
        s_scattered = sem("s_scattered")
        s_slot = [[sem(f"s_slot{j}_{c}") for c in range(2)] for j in range(2)]
        s_slotT_ps = sem("s_slotT_ps")
        s_slotT = sem("s_slotT")
        s_over_slot = sem("s_over_slot")
        s_over_gu = [[sem(f"s_over_gu{j}_{b}") for b in range(2)] for j in range(2)]
        s_over_dn = [sem(f"s_over_dn{j}") for j in range(2)]
        s_gu_used = [sem(f"s_gu_used{b}") for b in range(2)]
        s_dn_used = sem("s_dn_used")
        s_y_out = [sem(f"s_y_out{c}") for c in range(2)]
        s_back = [sem(f"s_back{t}") for t in range(NT)]
        s_up_ps = sem("s_up_ps")
        s_silu = sem("s_silu")
        s_he = sem("s_he")
        s_heT_ps = sem("s_heT_ps")
        s_heT = sem("s_heT")
        s_y_ps = sem("s_y_ps")
        s_y = [sem(f"s_y{c}") for c in range(2)]
        s_x2 = sem("s_x2")
        s_final = sem("s_final")
        s_out = sem("s_out")
        s_dve = sem("s_dve")
        s_pool = sem("s_pool")
        s_act = sem("s_act")

        slots = nc.dram_tensor("slots", (SLOTS, SLOT_W), F32, kind="Internal").ap()
        y_slots = nc.dram_tensor("y_slots", (SLOTS, D), F32, kind="Internal").ap()

        RET_BANKS = [((7, 0), (5, 0)), ((6, 0), (5, SEQ))]
        MODULATE_AT = [(5, 7, 9, 14), (2, 4, 6, 8)]
        NORM_AT = [[(1, 0, 3), (4, 1, 0), (5, 1, 1), (7, 1, 2), (10, 1, 3)],
                   [(1, 0, 0), (2, 0, 1), (4, 0, 2), (5, 0, 3)]]
        N_COND, N_X, N_CONST = 3, 2, 8
        N_SMALL = 4
        NORM_TILES = [4 + NQ[0], 4 + NQ[1]]

        def norm_base(l, a):
            return sum(NORM_TILES[:l]) + (0, 4, 4 + NQ[l])[a] if l < DEPTH else sum(NORM_TILES)

        PROJ_JOBS = [[(u, t) for u in (QK_U, V_U, LAT_U, GF_U, GB_U) for t in range(NT if u < GF_U else NQ[l])]
                     for l in range(DEPTH)]
        per_proj = [len(j) for j in PROJ_JOBS]

        def job_cols(l, u, t):
            unneeded = {QK_U: HEADS * RET_DK, LAT_U: Q_RANK}
            return slice(unneeded.get(u, 0) if t >= NQ[l] else 0, UNIT_COLS[u][1])

        MLA_JOBS = [[("k", h) for h in range(HEADS)] + [("v", t) for t in range(NT)] +
                    [("q", t, half) for t in range(NQ[l]) for half in range(2)] for l in range(DEPTH)]
        per_mla = [len(j) for j in MLA_JOBS]
        ATTN = [[(t, h) for t in range(NQ[l]) for h in range(HEADS)] for l in range(DEPTH)]
        per_attn = [len(j) for j in ATTN]
        RET_PASSES = [NQ[l] // 2 for l in range(DEPTH)]
        per_ret = [HEADS * r for r in RET_PASSES]

        def groups_before(l):
            return sum(group_passes[:l])

        WHOLE = {0: (0, 0), 1: (0, 1), 2: (1, 0), 3: (1, 1), 4: (2, 0), 5: (2, 1), 6: (3, 1), 7: (3, 0)}
        SHORT = {0: (0, 0), 1: (1, 0), 6: (2, 0), 7: (3, 0)}

        def ended(gg, items, k, back):
            place = list(items).index(k) - back
            return 8 * gg + (list(items)[place] + 1 if place >= 0 else place + 1)

        def w_wait(eng, n):
            slot, turn = slot_at[n]
            eng.wait_ge(s_wslot[slot], 16 * (turn + 1))

        block = ctx.enter_context(nc.Block())

        def freed(n):
            kind, l = units[n][:2]
            if kind == "ada":
                return s_ada_part, ada_at(*units[n][1:]) + 1
            if kind == "out":
                return s_out_ps, 2 * before(l + 1, NQ)
            if units[n][2] == CONV_U:
                return s_conv_ps, 4 * (l + 1)
            done = [i for i, (u, t) in enumerate(PROJ_JOBS[l]) if u == units[n][2]][-1] + 1
            return s_proj_ps, before(l, per_proj) + done

        @block.sync
        def _(sp):
            def load_unit(n):
                u = units[n]
                l = u[1]
                slot, turn = slot_at[n]
                if turn:
                    last = in_slot[slot][turn - 1]
                    if last < layer_ends[0] <= n:
                        sp.wait_ge((s_gu_used[1], s_gu_used[1], s_dn_used)[slot], EPG * groups_before(1))
                    else:
                        sp.wait_ge(*freed(last))
                if u[0] == "ada":
                    a, j = u[2], u[3]
                    q, half = MOD_UNITS[j]
                    col = (a * 3 + (1, 0, 2)[q]) * D + half * 512
                    src = dram["ada_w"][l].rearrange("(p k) n -> p k n", k=KD)[:, :, col:col + 512]
                    b = ada_at(l, a, j)
                    if b >= 2:
                        sp.wait_ge(s_ada_rows, b - 1)
                    elif b == 0:
                        sp.wait_ge(s_bias_zero, 1)
                    sp.dma_start(ada_bias[0:2, b % 2, :],
                                 dram["ada_b"][l:l + 1, col:col + 512].to_broadcast([2, 512])).then_inc(s_bias[b % 2], 16)
                elif u[0] == "in":
                    c0, w = UNIT_COLS[u[2]]
                    src = dram["w_in"][l].rearrange("(p k) n -> p k n", k=KD)[:, :, c0:c0 + w]
                else:
                    src = dram["w_out"][l].rearrange("(k p) n -> p k n", p=P)[:, :, u[2] * 512:u[2] * 512 + 512]
                sp.dma_start(unit_view(n), src).then_inc(s_wslot[slot], 16)

            def load_norm_w(l, a):
                if a:
                    sp.wait_ge(s_score_ps, before(l + 1, per_attn))
                if l or a:
                    sp.wait_ge(s_mod, mod_at[(l if a else l - 1, 1 - a, 4, 0)])
                sp.dma_start(norm_w, dram[("norm1_w", "norm2_w")[a]][l:l + 1, :].to_broadcast([P, D])).then_inc(s_normw, 16)

            def load_expert(l, g, e, gu_sem, dn_sem, which):
                m = EPG * groups_before(l) + e if gu_sem is s_over_gu else EPG * (groups_before(l) + g) + e
                if gu_sem is s_over_gu:
                    m += EPG * N_GROUPS
                j = m % 2
                first = m - EPG * groups_before(l) < 2
                if first:
                    if which == 0:
                        sp.wait_ge(s_out_ps, 2 * before(l + 1, NQ))
                    else:
                        sp.wait_ge(s_ada_part, ada_by_experts[l])

                def weights(name):
                    w = dram[name][l].rearrange("(g e) k n -> g e k n", e=EPG)
                    return w[bass.ds(g, 1), e].rearrange("g k n -> (g k) n")

                if which == 0:
                    for b in range(2):
                        ks = slice(4 * b, 4 * b + 4)
                        if not first:
                            sp.wait_ge(s_gu_used[b], m - 1)
                        for i, name in enumerate(("moe_w_gate", "moe_w_up")):
                            sp.dma_start(gu[j][:, ks, i * D_EXPERT:(i + 1) * D_EXPERT],
                                         weights(name).rearrange("(p k) n -> p k n", k=KD)[:, ks, :]).then_inc(gu_sem[j][b], 16)
                else:
                    if not first:
                        sp.wait_ge(s_dn_used, m - 1)
                    sp.dma_start(dn[j], weights("moe_w_down").rearrange("(p f) n -> p f n", f=2)).then_inc(dn_sem[j], 16)

            def load_slots(l, g):
                if g >= 2:
                    sp.wait_ge(s_he, 8 * (groups_before(l) + g - 1))
                for c in range(2):
                    r0 = (2 * g + c) * P
                    sp.dma_start(slot_tok[:, g % 2, c, :], slots[r0:r0 + P, :]).then_inc(
                        s_over_slot if g == N_GROUPS else s_slot[g % 2][c], 16)

            def load_experts(l):
                for e in range(2):
                    load_expert(l, 0, e, s_gu, s_dn, 0)
                load_expert(l, 0, 0, s_gu, s_dn, 1)
                sp.wait_ge(s_scattered, 16 * before(l + 1, NQ))
                load_slots(l, 0)
                load_slots(l, 1)
                for m in range(2, N_EXPERTS):
                    load_expert(l, m // EPG, m % EPG, s_gu, s_dn, 0)
                    load_expert(l, (m - 1) // EPG, (m - 1) % EPG, s_gu, s_dn, 1)
                    if m % EPG == 0 and m // EPG + 1 < N_GROUPS:
                        load_slots(l, m // EPG + 1)
                load_expert(l, N_GROUPS - 1, EPG - 1, s_gu, s_dn, 1)
                if group_passes[l] > N_GROUPS:
                    over = sp.value_load(flags[0:1, 4:5], min_val=0, max_val=1)
                    group = sp.value_load(flags[0:1, 5:6], min_val=0, max_val=N_GROUPS - 1)
                    with sp.If(over > 0):
                        load_slots(l, N_GROUPS)
                        for e in range(EPG):
                            load_expert(l, group, e, s_over_gu, s_over_dn, 0)
                            if e:
                                load_expert(l, group, e - 1, s_over_gu, s_over_dn, 1)
                        load_expert(l, group, EPG - 1, s_over_gu, s_over_dn, 1)

            def load_small(l):
                for dst, src in (
                    (w_ukv[:, :], dram["mla_w_ukv"][l]),
                    (conv_vec[:, :, :], dram["conv_cols"][l]),
                    (q_norm[0:96, :], dram["q_norm_cols"][l]),
                    (kv_norm[:, :], dram["mla_kv_norm_w"][l].rearrange("(p k) -> p k", k=1)),
                ):
                    sp.dma_start(dst, src).then_inc(s_small, 16)

            def load_uq(l):
                sp.dma_start(w_uq[0:96, :, :], dram["mla_w_uq"][l].rearrange("(k p) n -> p k n", p=96)).then_inc(s_uq, 16)

            for l in range(DEPTH):
                if l:
                    sp.wait_ge(s_convT, 2 * l)
                    sp.wait_ge(s_mla_ps, before(l, per_mla))
                    load_small(l)
                    load_uq(l)
                    sp.wait_ge(s_back[NQ[l - 1] - 1], 16 * l)
                for n in range(layer_ends[l - 1] if l else 0, layer_ends[l]):
                    load_unit(n)
                    if n == 1:
                        load_norm_w(0, 0)
                    if n == 3:
                        for dst, src in ((ident[:, :], dram["const_ident"]),
                                         (x[:, 0:2, :], dram["x"][0].rearrange("(t p) n -> p t n", p=P))):
                            sp.dma_start(dst, src).then_inc(s_x, 16)
                        sp.dma_start(x[:, 2:4, :], dram["ctx"][0].rearrange("(t p) n -> p t n", p=P)).then_inc(s_ctx, 16)
                    if units[n] == ("ada", l + 1, 0, 0) or (l == DEPTH - 1 and units[n] == ("out", l, 1)):
                        load_norm_w(l, 1)
                    if units[n] == ("ada", l + 1, 0, 1):
                        load_norm_w(l + 1, 0)
                    if n == 5:
                        for dst, src in (
                            (rope[:, :, :, :], dram["const_rope"]),
                            (k_decay[:, :, :, :], dram["const_k_decay"]),
                            (q_decay[:, :, :, :], dram["const_q_decay"]),
                            (decay[:, :, :, :], dram["const_decay"]),
                            (rank16[:, :], dram["const_rank"]),
                            (tri[:, :], dram["const_tri"]),
                            (router_w[:, :, :], dram["router_w"].rearrange("(p k) n -> p k n", k=KD)),
                            (r_bias[:, :], dram["router_bias"].rearrange("(a n) -> a n", a=1).to_broadcast([P, N_EXPERTS])),
                        ):
                            sp.dma_start(dst, src).then_inc(s_const, 16)
                        load_small(l)
                    if units[n] == ("in", 0, GB_U):
                        sp.wait_ge(s_fill, 1)
                        for j in range(SLOTS // P):
                            sp.dma_start(slots[j * P:(j + 1) * P, :], zero_rows).then_inc(s_filled, 16)
                        for j in range(SLOTS // P - 2, SLOTS // P):
                            sp.dma_start(y_slots[j * P:(j + 1) * P, :], zero_rows[:, 0:D]).then_inc(s_filled, 16)
                    if units[n] == ("ada", 0, 1, 1):
                        sp.wait_ge(s_filled, 16 * (SLOTS // P + 2))
                        load_uq(0)
                load_experts(l)
            sp.wait_ge(s_mod, len(mods))
            sp.dma_start(norm_w, dram["final_norm_w"].rearrange("(a n) -> a n", a=1).to_broadcast([P, D])).then_inc(s_normw, 16)
            for t in range(2):
                sp.wait_ge(s_final, t + 1)
                sp.dma_start(out[0, t * P:(t + 1) * P, :], h_tok[:, (norm_base(DEPTH, 0) + t) % 2, :]).then_inc(s_out, 16)
            sp.wait_ge(s_out, 32)

        def tok(t):
            return slice(t * P, (t + 1) * P)

        def in_group(n):
            return tmp[:, 700:700 + 4 * n].rearrange("p (t g) -> p t g", t=n)

        def lat_evacs(l, t):
            per = lambda a, b: sum(4 if i < NQ[a] else 2 for i in range(b))
            return sum(per(a, NT) for a in range(l)) + per(l, t)

        @block.tensor
        def _(pe):
            T = nc.tensor

            def modulate(l, a, u):
                n = ada_at(l, a, u)
                w_wait(pe, unit_at[("ada", l, a, u)])
                w = unit_view(unit_at[("ada", l, a, u)])
                if n >= 2:
                    pe.wait_ge(s_ada_rows, n - 1)
                for step in range(2):
                    for strip in range(4):
                        k = 2 * strip + step
                        last = T.matmul(ps[32 * strip:32 * strip + 32, (6 if a and u < 4 else 0) + n % 2, :], c_pad[:, k, :], w[:, k, :],
                                        start=(step == 0), stop=(step == 1),
                                        tile_position=(0, 32 * strip))
                last.then_inc(s_ada_part, 1)

            def broadcast(l, a, u):
                pe.wait_ge(s_ada_rows, ada_at(l, a, u) + 1)
                for s in range(2):
                    if (l, a, u, s) in mod_at:
                        b = mod_at[(l, a, u, s)]
                        if b >= 2:
                            pe.wait_ge(s_mod, b - 1)
                        T.matmul(ps[:, 2 + b % 2, :], sel[:, s, :], mod_rows(l, a, u),
                                 start=True, stop=True).then_inc(s_ada_bc, 1)

            def transpose_h(l, a, tiles):
                for t in tiles:
                    i = norm_base(l, a) + t
                    pe.wait_ge(s_h, i + 1)
                    h = (h2[:, t, 0:D] if a else h_tok[:, i % 2, :]).rearrange("q (p k) -> q k p", k=KD)
                    for b in range(2):
                        if i >= 1:
                            pe.wait_ge(s_hT, 2 * (i - 1) + b + 1)
                        for j in range(4):
                            last = T.transpose(ps[:, 6 + b, j * P:(j + 1) * P], h[:, 4 * b + j, :], ident[:, :])
                        last.then_inc(s_hT_ps, 1)

            def project_conv(l):
                n = unit_at[("in", l, CONV_U)]
                w_wait(pe, n)
                w = unit_view(n)
                pe.wait_ge(s_hT, 2 * (norm_base(l, 0) + 4))
                pe.wait_ge(s_ada_rows, l * ada_per_layer + (6 if l else 4))
                pe.wait_ge(s_mod, mod_at[(l, 0, 4, 0)])
                width = NQ[l] * P
                for m in (2, 3, 0, 1):
                    for k in range(KD):
                        last = T.matmul(ps[:, m, 0:width], w[:, k, tok(m)], hT[:, k, 0:width],
                                        start=(k == 0), stop=(k == KD - 1))
                    last.then_inc(s_conv_ps, 1)

            def project(l, us, tiles=range(NT)):
                for i, (u, t) in enumerate(PROJ_JOBS[l]):
                    if u not in us or t not in tiles:
                        continue
                    j = before(l, per_proj) + i
                    cols = job_cols(l, u, t)
                    if u == QK_U:
                        pe.wait_ge(s_hT, 2 * (norm_base(l, 0) + t + 1))
                    n = unit_at[("in", l, u)]
                    if t == 0:
                        w_wait(pe, n)
                    w = unit_view(n)
                    if i >= 2:
                        pe.wait_ge(s_proj, j - 1)
                    for k in range(KD):
                        last = T.matmul(ps[:, 4 + j % 2, cols], hT[:, k, tok(t)], w[:, k, cols],
                                        start=(k == 0), stop=(k == KD - 1))
                    last.then_inc(s_proj_ps, 1)

            def transpose_qk(l):
                for t in range(NT):
                    if t < 2:
                        pe.wait_ge(s_qk_rope, 2 * l + t + 1)
                    else:
                        pe.wait_ge(s_proj, before(l, per_proj) + t + 1)
                        pe.wait_ge(s_qkT, 2 * (NT * l + t - 1))
                    for f, (c0, w) in enumerate(((0, 128), (128, 64), (192, 128), (320, 64))):
                        if f < 2 and t >= NQ[l]:
                            continue
                        last = T.transpose(ps[0:w, 6 + t % 2, f * P:(f + 1) * P], qk_tok[:, t, c0:c0 + w], ident[:, :])
                    last.then_inc(s_qkT_ps, 1)

            def transpose_latents(l):
                pe.wait_ge(s_qkT, 2 * NT * (l + 1))
                for t in range(NT):
                    pe.wait_ge(s_lat_norm, NT * l + t + 1)
                    if t >= 2:
                        pe.wait_ge(s_latT, lat_evacs(l, t - 1))
                    for f, (c0, w) in enumerate(((0, 96), (96, 96), (192, 128), (320, 32))):
                        if f < 2 and t >= NQ[l]:
                            continue
                        last = T.transpose(ps[0:w, 6 + t % 2, f * P:(f + 1) * P], lat_tok[:, t, c0:c0 + w], ident[:, :])
                    last.then_inc(s_latT_ps, 1)

            def retention(l, s):
                r0 = before(l, per_ret) + s * HEADS
                ahead = 4 if s == 0 else 2

                def scores(h0):
                    pair = (h0, h0 + 1)
                    for h in pair:
                        r = r0 + h
                        if s == 0 and h < 4:
                            pe.wait_ge(s_glu, 2 * (l + 1))
                            pe.wait_ge(s_sig, 2 * (l + 1))
                        elif s == 1 and h < 2:
                            pe.wait_ge((s_ccent, s_cstd)[h], (2 * (l + 1), l + 1)[h])
                        else:
                            pe.wait_ge(s_mask[0], r + 1 - ahead)
                            pe.wait_ge(s_mask[1], r + 1 - ahead)
                    for slot in range(2):
                        for h in pair:
                            q0, side = 32 * (h % 4), h // 4
                            last = T.matmul(ps[:, h % ahead, slot * SEQ:(slot + 1) * SEQ],
                                            qkT[q0:q0 + 32, 2 + side, tok(2 * s + slot)],
                                            qkT[q0:q0 + 32, side, s * SEQ:(s + 1) * SEQ], start=True, stop=True,
                                            tile_position=(q0, 0))
                            if slot == 1:
                                last.then_inc(s_ret_ps, 1)

                def sums(h):
                    r = r0 + h
                    at = h % 2 * SEQ
                    for f in range(2):
                        pe.wait_ge(s_mask[f], r + 1)
                    if s == 0:
                        side = h // 4
                        rows = (P, 64)[side]
                        for f in range(2):
                            T.matmul(ps[RET_DV * f:RET_DV * (f + 1), 4 + h // 2, at:at + SEQ],
                                     state[0:rows, h, f, :], q_state[0:rows, side, f, :],
                                     start=True, stop=False, tile_position=(0, RET_DV * f))
                    for n in range(2):
                        for f in range(2):
                            j = 1 - n if f else n
                            cols = tok(1 - f) if n else slice(0, SEQ)
                            last = T.matmul(ps[RET_DV * f:RET_DV * (f + 1), 4 + h // 2, at + cols.start:at + cols.stop],
                                            v_ret[:, 2 * s + j, h * RET_DV:(h + 1) * RET_DV], masked[r % 2][:, f, j, cols],
                                            start=(s == 1 and n == 0), stop=(n == 1), tile_position=(0, RET_DV * f))
                            if n == 1:
                                last.then_inc(s_ret_pv[f], 1)

                if s == 0:
                    pe.wait_ge(s_ada_rows, l * ada_per_layer + 8)
                    pe.wait_ge(s_mod, mod_at[(l, 1, 0, 0)])
                scores(0)
                if s == 0:
                    pe.wait_ge(s_state, HEADS * (l + 1))
                    pe.wait_ge(s_q_state, 2 * (l + 1))
                    scores(2)
                if s == 0:
                    pe.wait_ge(s_proj, before(l + 1, per_proj))
                    pe.wait_ge(s_latT, lat_evacs(l, NT))
                else:
                    pe.wait_ge(s_gn_y, 4 * (before(l, RET_PASSES) + s))
                for h in range(0, HEADS, 2):
                    if h + ahead < HEADS:
                        scores(h + ahead)
                    sums(h)
                    sums(h + 1)

            def context_state(l):
                pe.wait_ge(s_latT, lat_evacs(l, NT))
                pe.wait_ge(s_proj, before(l, per_proj) + 2 * NT)
                pe.wait_ge(s_k_state, 2 * (l + 1))
                for side, heads in enumerate((range(4), range(4, HEADS))):
                    for f in range(2):
                        for j in range(2):
                            for h in heads:
                                q0 = 32 * (h % 4)
                                last = T.matmul(ps[q0:q0 + 32, 7, (2 * side + f) * RET_DV:(2 * side + f + 1) * RET_DV],
                                                k_state[:, f, j, 32 * h:32 * h + 32], v_ret[:, 2 + j, h * RET_DV:(h + 1) * RET_DV],
                                                start=(j == 0), stop=(j == 1), tile_position=(0, q0))
                last.then_inc(s_state_ps, 1)

            def turn_retention(l, s):
                g = before(l, RET_PASSES) + s
                pe.wait_ge(s_retT, 3 * (g + 1))
                for i in range(2):
                    for h in range(HEADS):
                        bank, c0 = RET_BANKS[i][h // 4]
                        c0 += h % 4 * P
                        last = T.transpose(ps[:, bank, c0:c0 + P], retT[:, h, tok(i)], ident[:, :])
                    last.then_inc(s_retT_ps, 1)

            def conv_mean(l):
                for f in range(2):
                    pe.wait_ge(s_mask[f], before(l, per_ret) + HEADS)
                pe.wait_ge(s_taps, 2 * CONV_K * (l + 1))
                for c in range(2):
                    last = T.matmul(ps[:, 0, 0:NQ[l] * P], ones_mean[:, :], acc[:, c, 0:NQ[l] * P],
                                    start=(c == 0), stop=(c == 1))
                last.then_inc(s_cmean_ps, 1)

            def conv_var(l):
                pe.wait_ge(s_csq, 2 * (l + 1))
                for c in range(2):
                    last = T.matmul(ps[:, 1, 0:NQ[l] * P], ones_mean[:, :], conv_sq[:, c, 0:NQ[l] * P],
                                    start=(c == 0), stop=(c == 1))
                last.then_inc(s_cvar_ps, 1)

            def mla_job(l, i):
                job = MLA_JOBS[l][i]
                j = before(l, per_mla) + i
                bank = 2 + j % 2
                if i >= 2:
                    pe.wait_ge(s_mla_sb, j - 1)
                if job[0] == "k":
                    h = job[1]
                    last = T.matmul(ps[0:D_NOPE, bank, :], w_ukv[:, h * P:h * P + D_NOPE], ckvT[:, :],
                                    start=True, stop=True)
                elif job[0] == "v":
                    vs = w_ukv[:, :].rearrange("p (h n) -> p h n", h=HEADS)[:, :, D_NOPE:]
                    last = T.matmul(ps[:, bank, 0:HEADS * D_V], ckvT[:, tok(job[1])], vs, start=True, stop=True)
                else:
                    _, t, half = job
                    for k in range(2):
                        last = T.matmul(ps[:, bank, 0:288], cqT[0:96, k, tok(t)],
                                        w_uq[0:96, k, half * 288:(half + 1) * 288], start=(k == 0), stop=(k == 1))
                last.then_inc(s_mla_ps, 1)

            def transpose_q(l, t):
                i = before(l, NQ) + t
                if t < 2:
                    pe.wait_ge(s_q_rope, 2 * l + t + 1)
                else:
                    pe.wait_ge(s_mla_sb, before(l, per_mla) + 10 + 2 * (t + 1))
                if t == 0:
                    pe.wait_ge(s_cstd, l + 1)
                    for f in range(2):
                        pe.wait_ge(s_mask[f], before(l + 1, per_ret))
                else:
                    pe.wait_ge(s_qT, 2 * i)
                for h in range(HEADS):
                    last = T.transpose(ps[0:D_QK, h // 4, h % 4 * P:(h % 4 + 1) * P],
                                       q_stage[:, t % 2, h * D_QK:(h + 1) * D_QK], ident[:, :])
                last.then_inc(s_qT_ps, 1)

            def attention(l):
                items = ATTN[l]
                n0 = before(l, per_attn)
                pe.wait_ge(s_kr, l + 1)
                pe.wait_ge(s_mla_sb, before(l + 1, per_mla))
                pe.wait_ge(s_cstd, l + 1)
                for f in range(2):
                    pe.wait_ge(s_mask[f], before(l + 1, per_ret))
                pe.wait_ge(s_qT, 2 * before(l + 1, NQ))

                def scores(i):
                    t, h = items[i]
                    if i >= 2:
                        pe.wait_ge(s_exp, n0 + i - 1)
                    keys = slice(0, 512) if t < 2 else slice(SEQ, 512)
                    T.matmul(ps[:, (n0 + i) % 2, 0:keys.stop - keys.start], qT[:, h, tok(t)], KT[:, h, keys],
                             start=True, stop=True).then_inc(s_score_ps, 1)

                def turn(i):
                    t, h = items[i]
                    n = n0 + i
                    pe.wait_ge(s_exp, n + 1)
                    if i >= 2:
                        pe.wait_ge(s_pT, n - 1)
                    for j in range(4 if t < 2 else 2):
                        last = T.transpose(ps[:, 2 + n % 2, tok(j)], probs[:, n % 2, tok(j)], ident[:, :])
                    last.then_inc(s_pT_ps, 1)

                def values(i):
                    t, h = items[i]
                    n = n0 + i
                    pe.wait_ge(s_pT, n + 1)
                    tiles = range(4) if t < 2 else range(2, 4)
                    if i == HEADS:
                        pe.wait_ge(s_gn_y, 4 * before(l + 1, RET_PASSES))
                    if t >= 2 and h == 0:
                        pe.wait_ge(s_ada_rows, ada_per_layer * (l + 1) - (3 - t))
                    for j, kt in enumerate(tiles):
                        last = T.matmul(ps[:, 4 + t, h * D_V:(h + 1) * D_V], probsT[:, n % 2, tok(j)],
                                        v_mla[:, kt, h * D_V:(h + 1) * D_V], start=(j == 0), stop=(kt == 3))
                    last.then_inc(s_pv, 1)

                scores(0)
                for i in range(len(items)):
                    if i + 1 < len(items):
                        scores(i + 1)
                    turn(i)
                    if i:
                        values(i - 1)
                    if i in MODULATE_AT[l]:
                        if i == MODULATE_AT[l][0]:
                            pe.wait_ge(s_gn_y, 4 * before(l + 1, RET_PASSES))
                        modulate(l, 1, MODULATE_AT[l].index(i))
                values(len(items) - 1)

            def project_out(l):
                i0 = before(l, NQ)
                pe.wait_ge(s_mod, mod_at[(l, 1, 4, 0)])
                for t in range(NQ[l]):
                    for b in range(2):
                        if b == 0:
                            pe.wait_ge(s_ret_out, i0 + t + 1)
                        else:
                            pe.wait_ge(s_mla_out, i0 + t + 1)
                        if t:
                            pe.wait_ge(s_oT, 2 * (i0 + t - 1) + b + 1)
                        o = o_mla[:, t, :] if b else gate_act[:, 0, t, :]
                        for j in range(3):
                            last = T.transpose(ps[:, 2 + b, tok(j)], o[:, tok(j)], ident[:, :])
                        last.then_inc(s_oT_ps, 1)
                pe.wait_ge(s_convT, 2 * (l + 1))
                pe.wait_ge(s_exp, before(l + 1, per_attn))
                pe.wait_ge(s_mla_out, before(l + 1, NQ))
                for t in range(NQ[l]):
                    pe.wait_ge(s_oT, 2 * (i0 + t + 1))
                    for c in range(2):
                        i = 2 * t + c
                        if t == 0:
                            w_wait(pe, unit_at[("out", l, c)])
                        w = unit_view(unit_at[("out", l, c)])
                        if i >= 2:
                            pe.wait_ge(s_x1, 2 * i0 + i - 1)
                        for k in range(KD):
                            lhs = convT[:, k, tok(t)] if k < 2 else oT[:, k - 2, tok(t)]
                            last = T.matmul(ps[:, 4 + c, :], lhs, w[:, k, :], start=(k == 0), stop=(k == KD - 1))
                        last.then_inc(s_out_ps, 1)
                        if l + 1 < DEPTH and 1 <= i <= 6:
                            modulate(l + 1, 0, i - 1)
                    if t:
                        transpose_h(l, 1, [t - 1])
                    if t >= 2:
                        logits(l, t - 2)
                logits(l, NQ[l] - 2)
                transpose_h(l, 1, [NQ[l] - 1])
                logits(l, NQ[l] - 1)

            def logits(l, t):
                pe.wait_ge(s_hT, 2 * (norm_base(l, 1) + t + 1))
                for k in range(KD):
                    last = T.matmul(ps[:, 2, t * N_EXPERTS:(t + 1) * N_EXPERTS], h2T[:, t % 2, k, :], router_w[:, k, :],
                                    start=(k == 0), stop=(k == KD - 1))
                last.then_inc(s_logit_ps, 1)

            def route(l):
                pe.wait_ge(s_group, l + 1)
                n = NQ[l]
                chosen = in_group(n)
                flat = chosen.rearrange("p t g -> p (t g)")
                T.matmul(ps[:, 4, 64:64 + 4 * n], tri[:, :], flat, start=True, stop=False)
                for back in range(1, n):
                    last = T.matmul(ps[:, 4, 64 + 4 * back:64 + 4 * n], ones_mean[:, :], flat[:, 0:4 * (n - back)],
                                    start=False, stop=(back == n - 1))
                last.then_inc(s_rank_ps, 1)
                for u in range(n):
                    last = T.matmul(ps[:, 5, 96:100], ones_mean[:, :], chosen[:, u, :], start=(u == 0), stop=(u == n - 1))
                last.then_inc(s_count_ps, 1)

            def experts(l):
                waiting = {"gu0": 0, "gu1": 0, "dn": 0}

                def release(which, ins):
                    if waiting[which]:
                        ins.then_inc({"gu0": s_gu_used[0], "gu1": s_gu_used[1], "dn": s_dn_used}[which], waiting[which])
                        waiting[which] = 0

                def slot_round(g, r):
                    c, b = r // 2, r % 2
                    n = 4 * (groups_before(l) + g) + r
                    if g == N_GROUPS:
                        pe.wait_ge(s_over_slot, 32)
                    else:
                        pe.wait_ge(s_slot[g % 2][c], 16 * (2 * l + g // 2 + 1))
                    if n:
                        pe.wait_ge(s_slotT, n)
                    h = slot_tok[:, g % 2, c, 0:D].rearrange("q (p k) -> q k p", k=KD)
                    for j in range(4):
                        last = T.transpose(ps[:, 3, tok(j)], h[:, 4 * b + j, :], ident[:, :])
                        if j == 0:
                            release("gu1", last)
                    last.then_inc(s_slotT_ps, 1)

                def landed(g, e, sems, over_sems, each):
                    if g == N_GROUPS:
                        pe.wait_ge(over_sems[e % 2], each * (e // 2 + 1))
                    else:
                        pe.wait_ge(sems[e % 2], each * (2 * (N_GROUPS * l + g) + e // 2 + 1))

                def up(g, items, k):
                    e, c = items[k]
                    gg = groups_before(l) + g
                    i = 8 * gg + k
                    if items is SHORT and k == 6:
                        pe.drain().then_inc(s_up_ps, 4)
                    pe.wait_ge(s_slotT, 4 * gg + (4 if c else 2))
                    if ended(gg, items, k, 2) > 0:
                        pe.wait_ge(s_he, ended(gg, items, k, 2))
                    leaves = k > 0 and c == (0 if items is SHORT or e == EPG - 1 else 1)
                    for q in range(KD):
                        if q % 4 == 0:
                            landed(g, e, [pair[q // 4] for pair in s_gu], [pair[q // 4] for pair in s_over_gu], 32)
                        last = T.matmul(ps[:, i % 2, :], slot_hT[:, g % 2, c, q, :], gu[e % 2][:, q, :],
                                        start=(q == 0), stop=(q == KD - 1))
                        if q == 0:
                            release("dn", last)
                        elif q == 1:
                            release("gu1", last)
                        elif q == 2:
                            release("gu0", last)
                        elif q == 4 and leaves:
                            last.then_inc(s_gu_used[0], 1)
                    last.then_inc(s_up_ps, 1)
                    if leaves:
                        waiting["gu1"] += 1

                def turn(g, items, k):
                    gg = groups_before(l) + g
                    i = 8 * gg + k
                    if items is SHORT and k == 6:
                        pe.drain().then_inc(s_heT_ps, 4)
                    pe.wait_ge(s_he, i + 1)
                    if ended(gg, items, k, 1) > 0:
                        pe.wait_ge(s_heT, ended(gg, items, k, 1))
                    he = he_buf[:, i % 2, :].rearrange("q (p f) -> q f p", f=2)
                    for f in range(2):
                        last = T.transpose(ps[:, 2, tok(f)], he[:, f, :], ident[:, :])
                        if f == 0:
                            release("gu1", last)
                    last.then_inc(s_heT_ps, 1)

                def down(g, items, k):
                    e, c = items[k]
                    gg = groups_before(l) + g
                    i = 8 * gg + k
                    if items is SHORT and k == 6:
                        pe.drain().then_inc(s_y_ps, 4)
                    pe.wait_ge(s_heT, i + 1)
                    landed(g, e, s_dn, s_over_dn, 16)
                    if e == 0 and gg:
                        pe.wait_ge(s_y[c], gg)
                    for half in range(2):
                        for f in range(2):
                            last = T.matmul(ps[:, 4 + 2 * c + half, :], heT_buf[:, i % 2, tok(f)],
                                            dn[e % 2][:, f, half * 512:(half + 1) * 512],
                                            start=(e == 0 and f == 0), stop=(e == EPG - 1 and f == 1))
                            if half == 0 and f == 0:
                                release("dn", last)
                    last.then_inc(s_y_ps, 1)
                    if items is SHORT or k in (1, 3, 5, 7):
                        waiting["dn"] += 1

                def body(g, items):
                    order = list(items)
                    if items is SHORT:
                        waiting["gu0"] += 1
                        waiting["gu1"] += 1
                    for p in range(1, len(order)):
                        up(g, items, order[p])
                        if p < 4 and g < N_GROUPS - 1:
                            slot_round(g + 1, p)
                        turn(g, items, order[p - 1])
                        if p >= 2:
                            down(g, items, order[p - 2])
                    down(g, items, order[-2])
                    if waiting["dn"]:
                        pe.drain().then_inc(s_dn_used, waiting["dn"])
                        waiting["dn"] = 0
                    assert not waiting["gu0"] and not waiting["gu1"]

                def finish(g):
                    turn(g, WHOLE, 7)
                    down(g, WHOLE, 7)

                def settle():
                    pe.drain().then_inc(s_dn_used, waiting["dn"])
                    waiting["dn"] = 0

                pe.wait_ge(s_mod, mod_at[(l + 1, 0, 4, 0)] if l + 1 < DEPTH else len(mods))
                pe.wait_ge(s_flags, l + 1)
                for r in range(4):
                    slot_round(0, r)
                for g in range(N_GROUPS):
                    up(g, WHOLE, 0)
                    if g < N_GROUPS - 1:
                        slot_round(g + 1, 0)
                    if g:
                        finish(g - 1)
                    second = pe.value_load(flags[0:1, g:g + 1], min_val=0, max_val=1)
                    carried = dict(waiting)
                    with pe.If(second > 0):
                        body(g, WHOLE)
                    waiting.update(carried)
                    with pe.Else():
                        body(g, SHORT)
                finish(N_GROUPS - 1)
                settle()
                if group_passes[l] > N_GROUPS:
                    over = pe.value_load(flags[0:1, 4:5], min_val=0, max_val=1)
                    with pe.If(over > 0):
                        for r in range(4):
                            slot_round(N_GROUPS, r)
                        up(N_GROUPS, WHOLE, 0)
                        body(N_GROUPS, WHOLE)
                        finish(N_GROUPS)
                        settle()
                    with pe.Else():
                        for sem, n in ((s_up_ps, 8), (s_heT_ps, 8), (s_y_ps, 8), (s_slotT_ps, 4),
                                       (s_gu_used[0], EPG), (s_gu_used[1], EPG), (s_dn_used, EPG)):
                            pe.drain().then_inc(sem, n)

            pe.wait_ge(s_cond, 16 * N_COND)
            pe.wait_ge(s_cpad, 2)
            pe.wait_ge(s_ones, 1)
            for u in range(4):
                modulate(0, 0, u)
                if u:
                    broadcast(0, 0, u - 1)
            broadcast(0, 0, 3)
            pe.wait_ge(s_x, 16 * N_X)
            for l in range(DEPTH):
                if l:
                    for c in range(2):
                        pe.wait_ge(s_y[c], groups_before(l))
                transpose_h(l, 0, [0])
                for t in range(NT):
                    if t + 1 < NT:
                        transpose_h(l, 0, [t + 1])
                    project(l, (QK_U,), [t])
                project_conv(l)
                project(l, (V_U,))
                pe.wait_ge(s_glu, 2 * (l + 1))
                pe.wait_ge(s_sig, 2 * (l + 1))
                if l == 0:
                    modulate(l, 0, 4)
                    modulate(l, 0, 5)
                transpose_qk(l)
                broadcast(l, 0, 4)
                broadcast(l, 0, 5)
                project(l, (LAT_U,))
                modulate(l, 1, 4)
                project(l, (GF_U,))
                modulate(l, 1, 5)
                project(l, (GB_U,))
                transpose_latents(l)
                pe.wait_ge(s_const, 16 * N_CONST)
                context_state(l)
                retention(l, 0)
                conv_mean(l)
                turn_retention(l, 0)
                pe.wait_ge(s_small, 16 * N_SMALL * (l + 1))
                pe.wait_ge(s_uq, 16 * (l + 1))
                for i in range(10):
                    mla_job(l, i)
                conv_var(l)
                if RET_PASSES[l] == 2:
                    retention(l, 1)
                    turn_retention(l, 1)
                for i in range(4):
                    mla_job(l, 10 + i)
                for t in range(NQ[l]):
                    transpose_q(l, t)
                    if t + 2 < NQ[l]:
                        mla_job(l, 14 + 2 * t)
                        mla_job(l, 15 + 2 * t)
                attention(l)
                pe.wait_ge(s_pT, before(l + 1, per_attn))
                for u in range(4):
                    broadcast(l, 1, u)
                project_out(l)
                route(l)
                for u in (4, 5):
                    broadcast(l, 1, u)
                if l + 1 < DEPTH:
                    for u in range(4):
                        broadcast(l + 1, 0, u)
                experts(l)

        @block.scalar
        def _(act):
            S = nc.scalar
            steps = [0]

            def chain(ins):
                steps[0] += 1
                ins.then_inc(s_act, 1)
                act.wait_ge(s_act, steps[0])

            for dst, src in (
                (c_raw[:, 0, :], dram["c"][0].rearrange("(p k) -> p k", k=KD)),
                (c_raw[:, 1, :], dram["c_ctx"].rearrange("(p k) -> p k", k=KD)),
                (sel[:, :, :], dram["const_sel"]),
            ):
                act.dma_start(dst, src).then_inc(s_cond, 16)

            def square_sums(l, a, tiles):
                for t in tiles:
                    i = norm_base(l, a) + t
                    if not (l or a):
                        act.wait_ge(*((s_ctx, 16) if t >= 2 else (s_x, 16 * N_X)))
                    if a:
                        act.wait_ge(s_x1, 2 * (before(l, NQ) + t + 1))
                    elif l:
                        act.wait_ge(s_x2, before(l - 1, NQ) + t + 1)
                    if i:
                        act.wait_ge(s_sumsq, i)
                    S.activation(square_junk, x[:, t, :], ACT.Square, accum_out=rstd[:, t:t + 1]).then_inc(s_sumsq, 1)

            def copy_hT(l, a, tiles):
                for t in tiles:
                    i = norm_base(l, a) + t
                    for b in range(2):
                        act.wait_ge(s_hT_ps, 2 * i + b + 1)
                        if a and t >= 2:
                            act.wait_ge(s_logit_ps, before(l, NQ) + t - 1)
                        dst = h2T[:, t % 2, 4 * b:4 * b + 4, :] if a else hT[:, 4 * b:4 * b + 4, tok(t)]
                        S.activation(dst, ps[:, 6 + b, :].rearrange("p (k n) -> p k n", k=4),
                                     ACT.Copy).then_inc(s_hT, 1)

            def project(l, us, tiles=range(NT)):
                dst = {QK_U: qk_tok, V_U: v_ret, LAT_U: lat_tok}
                for i, (u, t) in enumerate(PROJ_JOBS[l]):
                    if u not in us or t not in tiles:
                        continue
                    j = before(l, per_proj) + i
                    cols = job_cols(l, u, t)
                    act.wait_ge(s_proj_ps, j + 1)
                    if u == LAT_U and t == 0:
                        act.wait_ge(s_k_state, 2 * (l + 1))
                    got = ps[:, 4 + j % 2, cols]
                    if u in dst:
                        S.activation(dst[u][:, t, cols], got, ACT.Copy).then_inc(s_proj, 1)
                    else:
                        S.activation(gate_act[:, u - GF_U, t, :], got, ACT.Silu).then_inc(s_proj, 1)
                    if u == LAT_U:
                        act.wait_ge(s_proj, j + 1)
                        if NT * l + t:
                            act.wait_ge(s_lat_sq, NT * l + t)
                        if t < NQ[l]:
                            chain(S.activation(junk, lat_tok[:, t, 0:Q_RANK], ACT.Square,
                                               accum_out=lat_sumsq[:, t, 0:1]))
                        S.activation(junk[:, 0:KV_RANK], lat_tok[:, t, Q_RANK:Q_RANK + KV_RANK], ACT.Square,
                                     accum_out=lat_sumsq[:, t, 1:2]).then_inc(s_lat_sq, 1)

            def copy_qkT(l):
                for t in range(NT):
                    act.wait_ge(s_qkT_ps, NT * l + t + 1)
                    f0 = 0 if t < NQ[l] else 2
                    got = ps[:, 6 + t % 2, :].rearrange("p (f n) -> p f n", f=4)
                    S.activation(qkT[:, f0::2, tok(t)], got[:, f0::2, :], ACT.Copy).then_inc(s_qkT, 1)
                    S.activation(qkT[0:64, f0 + 1::2, tok(t)], got[0:64, f0 + 1::2, :], ACT.Copy).then_inc(s_qkT, 1)

            def copy_latT(l):
                act.wait_ge(s_small, 16 * N_SMALL * (l + 1))
                for t in range(NT):
                    act.wait_ge(s_latT_ps, NT * l + t + 1)
                    bank = 6 + t % 2
                    if t < NQ[l]:
                        for k in range(2):
                            S.activation(cqT[0:96, k, tok(t)], ps[0:96, bank, k * P:(k + 1) * P], ACT.Copy,
                                         scale=q_norm[0:96, k:k + 1]).then_inc(s_latT, 1)
                    S.activation(ckvT[:, tok(t)], ps[:, bank, 2 * P:3 * P], ACT.Copy,
                                 scale=kv_norm[:, 0:1]).then_inc(s_latT, 1)
                    S.activation(KT[D_NOPE:D_QK, 0, tok(t)], ps[0:D_ROPE, bank, 3 * P:4 * P], ACT.Copy).then_inc(s_latT, 1)

            def copy_state(l):
                act.wait_ge(s_state_ps, l + 1)
                act.wait_ge(s_state_zero, l + 1)
                for h in range(HEADS):
                    own, c0 = slice(32 * (h % 4), 32 * (h % 4) + 32), h // 4 * P
                    S.activation(state[own, h, :, :], ps[own, 7, c0:c0 + P].rearrange("p (f n) -> p f n", f=2),
                                 ACT.Copy).then_inc(s_state, 1)

            def groupnorm_in(l, s):
                g = before(l, RET_PASSES) + s
                for i in range(2):
                    act.wait_ge(s_retT_ps, 2 * g + 2)
                    if g:
                        act.wait_ge(s_ret_out, 2 * (g - 1) + i + 1)
                    y = gn_y[:, i, :, :].rearrange("p (f h) n -> p h f n", f=2)
                    for b, (h0, h1) in enumerate(((0, 4), (4, 6))):
                        bank, c0 = RET_BANKS[i][b]
                        S.activation(y[:, h0:h1, :, :],
                                     ps[:, bank, c0:c0 + (h1 - h0) * P].rearrange("p (h f n) -> p h f n", f=2, n=RET_DV),
                                     ACT.Copy).then_inc(s_gn_y, 1)

            def copy_retention(l, s):
                for b in range(3):
                    for f in range(2):
                        act.wait_ge(s_ret_pv[f], before(l, per_ret) + HEADS * s + 2 * (b + 1))
                    S.activation(retT[:, 2 * b:2 * b + 2, :], ps[:, 4 + b, :].rearrange("p (h n) -> p h n", h=2),
                                 ACT.Copy).then_inc(s_retT, 1)

            def groupnorm_sq(l, s, tiles=range(2)):
                for i in tiles:
                    g = 2 * (before(l, RET_PASSES) + s) + i
                    act.wait_ge(s_gn_cent, g + 1)
                    if g >= 2:
                        act.wait_ge(s_gn_var, g - 1)
                    S.activation(gn_squares[i], gn_y[:, i, :, :],
                                 ACT.Square).then_inc(s_gn_sq, 1)

            def conv_sq_act(l):
                for c in range(2):
                    act.wait_ge(s_ccent, 2 * l + c + 1)
                    S.activation(conv_sq[:, c, 0:NQ[l] * P], acc[:, c, 0:NQ[l] * P], ACT.Square).then_inc(s_csq, 1)

            def conv_std_act(l):
                act.wait_ge(s_cvar_ps, l + 1)
                S.activation(conv_std[:, 0:NQ[l] * P], ps[:, 1, 0:NQ[l] * P], ACT.Sqrt, bias=eps_col[:, 0:1]).then_inc(s_cstd, 1)

            def conv_out(l):
                for c in range(2):
                    act.wait_ge(s_cnorm, 2 * l + c + 1)
                    S.activation(convT[:, c, 0:NQ[l] * P], acc[:, c, 0:NQ[l] * P], ACT.Silu,
                                 scale=conv_vec[:, c, CONV_K + 1:CONV_K + 2], bias=conv_vec[:, c, CONV_K + 2:CONV_K + 3]).then_inc(s_convT, 1)

            def mla_copy(l, i):
                job = MLA_JOBS[l][i]
                j = before(l, per_mla) + i
                bank = 2 + j % 2
                act.wait_ge(s_mla_ps, j + 1)
                if job[0] == "k":
                    S.activation(KT[0:D_NOPE, job[1], :], ps[0:D_NOPE, bank, :], ACT.Copy).then_inc(s_mla_sb, 1)
                elif job[0] == "v":
                    S.activation(v_mla[:, job[1], :], ps[:, bank, 0:HEADS * D_V], ACT.Copy).then_inc(s_mla_sb, 1)
                else:
                    _, t, half = job
                    if t >= 2:
                        act.wait_ge(s_qT_ps, before(l, NQ) + t - 1)
                    if t == 0:
                        act.wait_ge(s_cnorm, 2 * (l + 1))
                    S.activation(q_stage[:, t % 2, half * 288:(half + 1) * 288], ps[:, bank, 0:288],
                                 ACT.Copy).then_inc(s_mla_sb, 1)

            def copy_qT(l, t):
                act.wait_ge(s_qT_ps, before(l, NQ) + t + 1)
                for b, n in ((0, 4), (1, 2)):
                    S.activation(qT[:, 4 * b:4 * b + n, tok(t)],
                                 ps[0:D_QK, b, 0:n * P].rearrange("p (h n) -> p h n", h=n),
                                 ACT.Copy, scale=MLA_SCALE).then_inc(s_qT, 1)

            def softmax(l):
                n0 = before(l, per_attn)
                for i, (t, h) in enumerate(ATTN[l]):
                    n = n0 + i
                    w = 512 if t < 2 else SEQ
                    act.wait_ge(s_max, n + 1)
                    if i >= 2:
                        act.wait_ge(s_pT_ps, n - 1)
                    S.activation(probs[:, n % 2, 0:w], ps[:, n % 2, 0:w], ACT.Exp, bias=neg_max[:, n % 2:n % 2 + 1],
                                 accum_out=prob_sum[:, t, h:h + 1]).then_inc(s_exp, 1)
                    if (i, 1, 0) in NORM_AT[l]:
                        groupnorm_in(l, 1)
                    for tile in range(2):
                        if (i, RET_PASSES[l] - 1, tile) in NORM_AT[l]:
                            groupnorm_sq(l, RET_PASSES[l] - 1, [tile])

            def copy_oT(l):
                for t in range(NQ[l]):
                    for b in range(2):
                        i = 2 * (before(l, NQ) + t) + b
                        act.wait_ge(s_oT_ps, i + 1)
                        S.activation(oT[:, 3 * b:3 * b + 3, tok(t)],
                                     ps[:, 2 + b, 0:3 * P].rearrange("p (k n) -> p k n", k=3), ACT.Copy).then_inc(s_oT, 1)

            def experts(l):
                def slot_copy(g, r):
                    c, b = r // 2, r % 2
                    act.wait_ge(s_slotT_ps, 4 * (groups_before(l) + g) + r + 1)
                    S.activation(slot_hT[:, g % 2, c, 4 * b:4 * b + 4, :], ps[:, 3, :].rearrange("p (k n) -> p k n", k=4),
                                 ACT.Copy).then_inc(s_slotT, 1)

                def silu(g, items, k):
                    gg = groups_before(l) + g
                    i = 8 * gg + k
                    if items is SHORT and k == 6:
                        act.drain().then_inc(s_silu, 4)
                    act.wait_ge(s_up_ps, i + 1)
                    if ended(gg, items, k, 2) > 0:
                        act.wait_ge(s_he, ended(gg, items, k, 2))
                    S.activation(silu_buf[:, i % 2, :], ps[:, i % 2, 0:D_EXPERT], ACT.Silu).then_inc(s_silu, 1)

                def copy_heT(g, items, k):
                    gg = groups_before(l) + g
                    i = 8 * gg + k
                    if items is SHORT and k == 6:
                        act.drain().then_inc(s_heT, 4)
                    act.wait_ge(s_heT_ps, i + 1)
                    if ended(gg, items, k, 2) > 0:
                        act.wait_ge(s_y_ps, ended(gg, items, k, 2))
                    S.activation(heT_buf[:, i % 2, :], ps[:, 2, 0:D_EXPERT], ACT.Copy).then_inc(s_heT, 1)

                def body(g, items):
                    order = list(items)
                    for p in range(1, len(order)):
                        silu(g, items, order[p])
                        if p < 4 and g < N_GROUPS - 1:
                            slot_copy(g + 1, p)
                        copy_heT(g, items, order[p - 1])

                act.wait_ge(s_flags, l + 1)
                for r in range(4):
                    slot_copy(0, r)
                for g in range(N_GROUPS):
                    silu(g, WHOLE, 0)
                    if g < N_GROUPS - 1:
                        slot_copy(g + 1, 0)
                    if g:
                        copy_heT(g - 1, WHOLE, 7)
                    second = act.value_load(flags[0:1, g:g + 1], min_val=0, max_val=1)
                    with act.If(second > 0):
                        body(g, WHOLE)
                    with act.Else():
                        body(g, SHORT)
                copy_heT(N_GROUPS - 1, WHOLE, 7)
                if group_passes[l] > N_GROUPS:
                    over = act.value_load(flags[0:1, 4:5], min_val=0, max_val=1)
                    with act.If(over > 0):
                        for r in range(4):
                            slot_copy(N_GROUPS, r)
                        silu(N_GROUPS, WHOLE, 0)
                        body(N_GROUPS, WHOLE)
                        copy_heT(N_GROUPS, WHOLE, 7)
                    with act.Else():
                        for sem, n in ((s_silu, 8), (s_heT, 8), (s_slotT, 4)):
                            act.drain().then_inc(sem, n)

            act.wait_ge(s_cond, 16 * N_COND)
            act.wait_ge(s_ones, 1)
            for s in range(2):
                S.activation(c_pad[:, :, s], c_raw[:, s, :], ACT.Silu).then_inc(s_cpad, 1)
            for l in range(DEPTH):
                square_sums(l, 0, range(NT))
                copy_hT(l, 0, [0])
                for t in range(NT):
                    if t + 1 < NT:
                        copy_hT(l, 0, [t + 1])
                    project(l, (QK_U,), [t])
                for j in range(2):
                    act.wait_ge(s_conv_ps, 4 * l + j + 1)
                    S.activation(conv_sig[:, j, 0:NQ[l] * P], ps[:, 2 + j, 0:NQ[l] * P], ACT.Sigmoid).then_inc(s_sig, 1)
                project(l, (V_U,))
                copy_qkT(l)
                project(l, (LAT_U, GF_U, GB_U))
                copy_latT(l)
                copy_state(l)
                copy_retention(l, 0)
                groupnorm_in(l, 0)
                conv_sq_act(l)
                for i in range(10):
                    mla_copy(l, i)
                conv_std_act(l)
                if RET_PASSES[l] == 2:
                    copy_retention(l, 1)
                conv_out(l)
                for i in range(4):
                    mla_copy(l, 10 + i)
                for t in range(NQ[l]):
                    copy_qT(l, t)
                    if t + 2 < NQ[l]:
                        mla_copy(l, 14 + 2 * t)
                        mla_copy(l, 15 + 2 * t)
                if RET_PASSES[l] == 2:
                    groupnorm_sq(l, 0)
                softmax(l)
                copy_oT(l)
                for t in range(NQ[l]):
                    square_sums(l, 1, [t])
                    if t:
                        copy_hT(l, 1, [t - 1])
                copy_hT(l, 1, [NQ[l] - 1])
                act.wait_ge(s_logit_ps, before(l + 1, NQ))
                S.activation(aff[:, 0:NQ[l], :], ps[:, 2, 0:NQ[l] * N_EXPERTS].rearrange("p (t n) -> p t n", n=N_EXPERTS),
                             ACT.Sigmoid).then_inc(s_aff, 1)
                experts(l)
            square_sums(DEPTH, 0, range(2))

        @block.vector
        def _(dve):
            V = nc.vector
            steps = [0]

            def chain(ins):
                steps[0] += 1
                ins.then_inc(s_dve, 1)
                dve.wait_ge(s_dve, steps[0])

            def rows(l, a, u):
                n = ada_at(l, a, u)
                dve.wait_ge(s_ada_part, n + 1)
                dve.wait_ge(s_bias[n % 2], 16 * (n // 2 + 1))
                V.tensor_tensor(mod_rows(l, a, u), ps[:, (6 if a and u < 4 else 0) + n % 2, :], ada_bias[:, n % 2, :],
                                ALU.add).then_inc(s_ada_rows, 1)

            def bcast(l, a, u):
                q, half = MOD_UNITS[u]
                for s in range(2):
                    if (l, a, u, s) not in mod_at:
                        continue
                    b = mod_at[(l, a, u, s)]
                    dve.wait_ge(s_ada_bc, b + 1)
                    dst = mod[:, q, s, half * 512:(half + 1) * 512]
                    if q == SCALE_Q:
                        dve.wait_ge(s_normw, 16 * (2 * l + a + 1))
                        V.scalar_tensor_tensor(out=dst, in0=ps[:, 2 + b % 2, :], scalar=1.0,
                                               in1=norm_w[:, half * 512:(half + 1) * 512],
                                               op0=ALU.add, op1=ALU.mult).then_inc(s_mod, 1)
                    else:
                        V.tensor_copy(dst, ps[:, 2 + b % 2, :]).then_inc(s_mod, 1)

            def scale_tiles(l, a, tiles):
                dve.wait_ge(s_mod, mod_at[(l, a, 4, 0)])
                for t in tiles:
                    i = norm_base(l, a) + t
                    dve.wait_ge(s_rstd, i + 1)
                    if i >= 2 and not a:
                        dve.wait_ge(s_hT_ps, 2 * (i - 1))
                    V.scalar_tensor_tensor(out=h2[:, t, 0:D] if a else h_tok[:, i % 2, :], in0=x[:, t, :],
                                           scalar=rstd[:, t:t + 1], in1=mod[:, SCALE_Q, t // 2, :], op0=ALU.mult, op1=ALU.mult).then_inc(s_scaled, 1)
                    if a:
                        dve.wait_ge(s_scaled, i + 1)
                        V.tensor_tensor(h2[:, t, 0:D], h2[:, t, 0:D], mod[:, SHIFT_Q, t // 2, :], ALU.add).then_inc(s_h, 1)

            def glu(l):
                dve.wait_ge(s_pad, l + 1)
                dve.wait_ge(s_conv_ps, 4 * (l + 1))
                dve.wait_ge(s_sig, 2 * (l + 1))
                n = NQ[l] // 2
                for c in range(2):
                    V.tensor_tensor(conv_in[:, c, 0:n, CONV_K // 2:CONV_K // 2 + SEQ],
                                    ps[:, c, 0:n * SEQ].rearrange("p (s n) -> p s n", s=n),
                                    conv_sig[:, c, 0:n * SEQ].rearrange("p (s n) -> p s n", s=n),
                                    ALU.mult).then_inc(s_glu, 1)

            def rotate(view, t, heads, done, value):
                n = heads * D_ROPE
                straight = tmp[:, 0:n].rearrange("p (h r) -> p h r", h=heads)
                swapped = tmp[:, 384:384 + n].rearrange("p (h g b r) -> p h g b r", h=heads, g=2, b=2)
                src = view.rearrange("p h (g b r) -> p h g b r", g=2, b=2)
                sin = rope[:, t, 1, :].rearrange("p (h g b r) -> p h g b r", h=1, g=2, b=2)
                cos = rope[:, t, 0, :].rearrange("p (h r) -> p h r", h=1)
                V.tensor_tensor(straight, view, cos.to_broadcast([P, heads, D_ROPE]), ALU.mult)
                for b in range(2):
                    last = V.tensor_tensor(swapped[:, :, :, b, :], src[:, :, :, 1 - b, :],
                                           sin[:, :, :, b, :].to_broadcast([P, heads, 2, 8]), ALU.mult)
                chain(last)
                V.tensor_tensor(view, straight, tmp[:, 384:384 + n].rearrange("p (h r) -> p h r", h=heads),
                                ALU.add).then_inc(done, 1)
                dve.wait_ge(done, value)

            def rope_qk(l):
                for t in range(2):
                    dve.wait_ge(s_proj, before(l, per_proj) + t + 1)
                    rotate(qk_tok[:, t, :].rearrange("p (h r) -> p h r", h=12), t, 12, s_qk_rope, 2 * l + t + 1)

            def norm_latents(l):
                for t in range(NT):
                    dve.wait_ge(s_lat_rstd, NT * l + t + 1)
                    if t < NQ[l]:
                        V.tensor_scalar(lat_tok[:, t, 0:Q_RANK], lat_tok[:, t, 0:Q_RANK], lat_rstd[:, t, 0:1], None, ALU.mult)
                    ckv = lat_tok[:, t, Q_RANK:Q_RANK + KV_RANK]
                    last = V.tensor_scalar(ckv, ckv, lat_rstd[:, t, 1:2], None, ALU.mult)
                    if t < 2:
                        rotate(lat_tok[:, t, Q_RANK + KV_RANK:LATW].rearrange("p (h r) -> p h r", h=1), t, 1,
                               s_lat_norm, NT * l + t + 1)
                    else:
                        last.then_inc(s_lat_norm, 1)

            def taps(l):
                n = NQ[l] // 2
                dve.wait_ge(s_glu, 2 * (l + 1))
                dve.wait_ge(s_small, 16 * N_SMALL * (l + 1))
                for k in range(CONV_K):
                    if k == 3 * CONV_K // 4:
                        rows(l, 1, 5)
                    for c in range(2):
                        i = 2 * (CONV_K * l + k) + c
                        src = conv_in[:, c, 0:n, k:k + SEQ]
                        dst = acc[:, c, 0:n * SEQ].rearrange("p (s n) -> p s n", s=n)
                        if k == 0:
                            V.tensor_scalar(dst, src, dw[:, c, 0:1], conv_vec[:, c, CONV_K:CONV_K + 1], ALU.mult, ALU.add).then_inc(s_taps, 1)
                        else:
                            dve.wait_ge(s_taps, i - 1)
                            V.scalar_tensor_tensor(out=dst, in0=src, scalar=dw[:, c, k:k + 1], in1=dst,
                                                   op0=ALU.mult, op1=ALU.add).then_inc(s_taps, 1)

            def masks(l, s):
                ahead = 4 if s == 0 else 2
                for h in range(HEADS):
                    r = before(l, per_ret) + s * HEADS + h
                    dve.wait_ge(s_ret_ps, r + 1)

                    def decayed(f, slot, cols, t0):
                        n = cols.stop - cols.start
                        c0 = slot * SEQ + cols.start
                        return V.scalar_tensor_tensor(out=masked[r % 2][:, f, slot, cols], in0=ps[:, h % ahead, c0:c0 + n],
                                                      scalar=float(RET_DK ** -0.5), in1=decay[:, f, h, t0:t0 + n],
                                                      op0=ALU.mult, op1=ALU.mult)

                    whole = slice(0, SEQ)
                    if r >= 2:
                        dve.wait_ge(s_ret_pv[0], r - 1)
                    decayed(0, 0, whole, 0)
                    decayed(0, 1, slice(P, SEQ), 0).then_inc(s_mask[0], 1)
                    if r >= 2:
                        dve.wait_ge(s_ret_pv[1], r - 1)
                    decayed(1, 1, whole, 0)
                    decayed(1, 0, slice(0, P), P).then_inc(s_mask[1], 1)

            def keys_for_state(l):
                dve.wait_ge(s_proj, before(l, per_proj) + NT)
                for f in range(2):
                    V.tensor_tensor(k_state[:, f, :, :].rearrange("p j (h n) -> p j h n", h=HEADS),
                                    qk_tok[:, 2:4, VW // 2:VW].rearrange("p j (h n) -> p j h n", h=HEADS),
                                    k_decay[:, f, :, :].rearrange("p j (h n) -> p j h n", n=1).to_broadcast([P, 2, HEADS, RET_DK]),
                                    ALU.mult).then_inc(s_k_state, 1)

            def queries_for_state(l):
                dve.wait_ge(s_qkT, 2 * NT * (l + 1))
                for side, n in ((0, P), (1, 64)):
                    V.tensor_tensor(q_state[0:n, side, :, :],
                                    qkT[0:n, side, 0:SEQ].rearrange("p (f n) -> p f n", f=1).to_broadcast([n, 2, SEQ]),
                                    q_decay[0:n, side, :, :], ALU.mult).then_inc(s_q_state, 1)

            def groupnorm(l, s, stage):
                g0 = 2 * (before(l, RET_PASSES) + s)
                for i in [stage] if stage < 2 else []:
                    dve.wait_ge(s_gn_y, 2 * (g0 + i + 1))
                    chain(V.tensor_reduce(gn_mean[:, i, :], gn_y[:, i, :, :], AX_X, ALU.add))
                    chain(V.tensor_scalar(gn_mean[:, i, :], gn_mean[:, i, :], 1.0 / RET_DV, None, ALU.mult))
                    V.tensor_tensor(gn_y[:, i, :, :], gn_y[:, i, :, :],
                                    gn_mean[:, i, :].rearrange("p (g n) -> p g n", n=1).to_broadcast([P, 12, RET_DV]),
                                    ALU.subtract).then_inc(s_gn_cent, 1)
                for i in range(2 if stage == 2 else 0):
                    dve.wait_ge(s_gn_sq, g0 + i + 1)
                    V.tensor_reduce(gn_rstd[:, i, :], gn_squares[i], AX_X,
                                    ALU.add).then_inc(s_gn_var, 1)
                for i in range(2 if stage == 3 else 0):
                    dve.wait_ge(s_gn_rstd, g0 + i + 1)
                    V.tensor_tensor(gn_y[:, i, :, :], gn_y[:, i, :, :],
                                    gn_rstd[:, i, :].rearrange("p (g n) -> p g n", n=1).to_broadcast([P, 12, RET_DV]),
                                    ALU.mult).then_inc(s_gn_norm, 1)

            def conv_centre(l):
                n = NQ[l] * P
                dve.wait_ge(s_cmean_ps, l + 1)
                for c in range(2):
                    V.tensor_tensor(acc[:, c, 0:n], acc[:, c, 0:n], ps[:, 0, 0:n], ALU.subtract).then_inc(s_ccent, 1)

            def conv_scale(l):
                n = NQ[l] * P
                dve.wait_ge(s_cstd, l + 1)
                chain(V.reciprocal(conv_std[:, 0:n], conv_std[:, 0:n]))
                for c in range(2):
                    V.tensor_tensor(acc[:, c, 0:n], acc[:, c, 0:n], conv_std[:, 0:n], ALU.mult).then_inc(s_cnorm, 1)

            def rope_q(l, t):
                dve.wait_ge(s_mla_sb, before(l, per_mla) + 10 + 2 * (t + 1))
                rotate(q_stage[:, t, :].rearrange("p (h r) -> p h r", h=HEADS)[:, :, D_NOPE:], t, HEADS,
                       s_q_rope, 2 * l + t + 1)

            def attention(l):
                n0 = before(l, per_attn)
                items = ATTN[l]

                def row_max(i):
                    t, h = items[i]
                    n = n0 + i
                    dve.wait_ge(s_score_ps, n + 1)
                    V.tensor_reduce(neg_max[:, n % 2:n % 2 + 1], ps[:, n % 2, 0:512 if t < 2 else SEQ], AX_X, ALU.max,
                                    negate=True).then_inc(s_max, 1)

                def copy_pT(i):
                    t, h = items[i]
                    n = n0 + i
                    w = 512 if t < 2 else SEQ
                    dve.wait_ge(s_pT_ps, n + 1)
                    if i >= 2:
                        dve.wait_ge(s_pv, n - 1)
                    V.tensor_copy(probsT[:, n % 2, 0:w], ps[:, 2 + n % 2, 0:w]).then_inc(s_pT, 1)

                def finish(i):
                    t, h = items[i]
                    if h < HEADS - 1:
                        return
                    dve.wait_ge(s_pv, n0 + i + 1)
                    chain(V.reciprocal(prob_sum[:, t, :], prob_sum[:, t, :]))
                    V.tensor_tensor(o_mla[:, t, :].rearrange("p (h n) -> p h n", h=HEADS),
                                    ps[:, 4 + t, 0:HEADS * D_V].rearrange("p (h n) -> p h n", h=HEADS),
                                    prob_sum[:, t, :].rearrange("p (h n) -> p h n", n=1).to_broadcast([P, HEADS, D_V]),
                                    ALU.mult).then_inc(s_mla_out, 1)

                row_max(0)
                for i in range(len(items)):
                    if i + 1 < len(items):
                        row_max(i + 1)
                    copy_pT(i)
                    if i:
                        finish(i - 1)
                    for item, s, stage in NORM_AT[l]:
                        if item == i:
                            groupnorm(l, s, stage)
                    if i in MODULATE_AT[l]:
                        u = MODULATE_AT[l].index(i)
                        if u == 0:
                            for f in range(2):
                                dve.wait_ge(s_ret_pv[f], before(l + 1, per_ret))
                        elif u == 3:
                            dve.wait_ge(s_ret_out, 2 * before(l + 1, RET_PASSES))
                        rows(l, 1, u)
                finish(len(items) - 1)

            def residual(l):
                dve.wait_ge(s_oT_ps, 2 * before(l + 1, NQ))
                for t in range(NQ[l]):
                    for c in range(2):
                        i = 2 * t + c
                        j = 2 * before(l, NQ) + i
                        cols = slice(c * 512, (c + 1) * 512)
                        dve.wait_ge(s_out_ps, j + 1)
                        if j:
                            dve.wait_ge(s_x1, j)
                        chain(V.tensor_tensor(tmp[:, 0:512], ps[:, 4 + c, :], mod[:, GATE_Q, t // 2, cols], ALU.mult))
                        V.tensor_tensor(x[:, t, cols], x[:, t, cols], tmp[:, 0:512], ALU.add).then_inc(s_x1, 1)
                        if l + 1 < DEPTH and 1 <= i <= 6:
                            rows(l + 1, 0, i - 1)
                    scale_tiles(l, 1, [t])

            def route(l):
                n = NQ[l]
                scr = tmp[:, :]
                at = [0]

                def take(shape):
                    size = 1
                    for d in shape:
                        size *= d
                    v = scr[:, at[0]:at[0] + size]
                    at[0] += size
                    names = "abcd"[:len(shape)]
                    kw = dict(zip(names, shape))
                    return v.rearrange(f"p ({' '.join(names)}) -> p {' '.join(names)}", **kw)

                grp = n * N_GROUPS
                dve.wait_ge(s_aff, l + 1)
                choice = take([n, N_EXPERTS])
                c4 = choice.rearrange("p t (g e) -> p (t g) e", g=N_GROUPS)
                chain(V.tensor_tensor(choice, aff[:, 0:n, :],
                                      r_bias[:, :].rearrange("p (t n) -> p t n", t=1).to_broadcast([P, n, N_EXPERTS]), ALU.add))
                pairs = take([grp, 6])
                V.tensor_tensor(pairs[:, :, 0:3], c4[:, :, 0:3], c4[:, :, 1:4], ALU.add)
                V.tensor_tensor(pairs[:, :, 3:5], c4[:, :, 0:2], c4[:, :, 2:4], ALU.add)
                chain(V.tensor_tensor(pairs[:, :, 5:6], c4[:, :, 0:1], c4[:, :, 3:4], ALU.add))
                score = take([grp])
                chain(V.tensor_reduce(score, pairs, AX_X, ALU.max))
                s4 = score.rearrange("p (t g) -> p t g", g=N_GROUPS)
                best = take([n])
                chain(V.tensor_reduce(best, s4, AX_X, ALU.max))

                def spread(v, k):
                    return v.rearrange("p (t n) -> p t n", n=1).to_broadcast([P, n, k])

                ranks = rank16[:, :].rearrange("p (t n) -> p t n", t=1)

                def first_best(values, top, k, out_mask):
                    chain(V.tensor_tensor(out_mask, values, spread(top, k), ALU.is_ge))
                    chain(V.tensor_tensor(out_mask, out_mask, ranks[:, :, 0:k].to_broadcast([P, n, k]), ALU.mult))
                    chain(V.tensor_reduce(top, out_mask, AX_X, ALU.max))
                    chain(V.tensor_tensor(out_mask, out_mask, spread(top, k), ALU.is_equal))

                chosen_group = in_group(n)
                first_best(s4, best, N_GROUPS, chosen_group)
                outside = take([n, N_GROUPS])
                V.tensor_scalar(outside, chosen_group, BIG, -BIG, ALU.mult, ALU.add).then_inc(s_group, 1)
                dve.wait_ge(s_group, l + 1)
                ig = chosen_group.rearrange("p t g -> p (t g)").rearrange("p (g e) -> p g e", e=1).to_broadcast([P, grp, EPG])
                og = outside.rearrange("p t g -> p (t g)").rearrange("p (g e) -> p g e", e=1).to_broadcast([P, grp, EPG])
                chain(V.tensor_tensor(c4, c4, ig, ALU.mult))
                chain(V.tensor_tensor(c4, c4, og, ALU.add))
                chosen = []
                for j in range(2):
                    mask = take([n, N_EXPERTS])
                    chain(V.tensor_reduce(best, choice, AX_X, ALU.max))
                    first_best(choice, best, N_EXPERTS, mask)
                    chosen.append(mask)
                    if j == 0:
                        chain(V.scalar_tensor_tensor(out=choice, in0=mask, scalar=-4.0 * BIG, in1=choice,
                                                     op0=ALU.mult, op1=ALU.add))
                chain(V.tensor_tensor(chosen[0], chosen[0], chosen[1], ALU.add))
                chain(V.tensor_tensor(chosen[0], chosen[0], aff[:, 0:n, :], ALU.mult))
                chain(V.tensor_reduce(best, chosen[0], AX_X, ALU.add))
                chain(V.reciprocal(best, best))
                V.tensor_tensor(h2[:, 0:n, D:SLOT_W], chosen[0], spread(best, N_EXPERTS), ALU.mult)

                dve.wait_ge(s_rank_ps, l + 1)
                rank, over = take([n, N_GROUPS]), take([n, N_GROUPS])
                own = [group_slot[:, j:j + 1, :].to_broadcast([P, n, N_GROUPS]) for j in range(2)]
                got = ps[:, 4, 64:64 + 4 * n].rearrange("p (t g) -> p t g", t=n)
                V.tensor_scalar(rank, got, float(CONV_W), None, ALU.mult)
                chain(V.tensor_scalar(over, got, GROUP_SLOTS / CONV_W, None, ALU.is_ge))
                V.tensor_tensor(rank, rank, own[0], ALU.add)
                chain(V.tensor_tensor(over, over, own[1], ALU.mult))
                chain(V.tensor_tensor(rank, rank, over, ALU.add))
                chain(V.tensor_tensor(rank, rank, chosen_group, ALU.mult))
                chain(V.tensor_reduce(best, rank, AX_X, ALU.add))
                V.tensor_copy(slot_of[:, 0:n], best).then_inc(s_gates, 1)

                dve.wait_ge(s_count_ps, l + 1)
                counts = ps[0:1, 5, 96:100]
                many = scr[0:1, at[0]:at[0] + 4]
                total = scr[0:1, at[0] + 4:at[0] + 8]
                V.tensor_scalar(flags[0:1, 0:4], counts, P / CONV_W, None, ALU.is_gt)
                chain(V.tensor_scalar(many, counts, GROUP_SLOTS / CONV_W, None, ALU.is_gt))
                chain(V.tensor_reduce(total[:, 0:1], many, AX_X, ALU.add))
                chain(V.tensor_tensor(many, many, group_slot[0:1, 0, :], ALU.mult))
                chain(V.tensor_reduce(total[:, 1:2], many, AX_X, ALU.add))
                V.tensor_copy(flags[0:1, 4:5], total[:, 0:1])
                V.tensor_scalar(flags[0:1, 5:6], total[:, 1:2], 1.0 / GROUP_SLOTS, None, ALU.mult).then_inc(s_flags, 1)

            def experts(l):
                over_gate = tmp[:, 0:2 * EPG].rearrange("p (c e) -> p c e", c=2)

                def hidden(g, items, k):
                    e, c = items[k]
                    gg = groups_before(l) + g
                    i = 8 * gg + k
                    if items is SHORT and k == 6:
                        dve.drain().then_inc(s_he, 4)
                    dve.wait_ge(s_silu, i + 1)
                    if ended(gg, items, k, 2) > 0:
                        dve.wait_ge(s_heT_ps, ended(gg, items, k, 2))
                    col = D + EPG * g + e
                    gate = over_gate[:, c, e:e + 1] if g == N_GROUPS else slot_tok[:, g % 2, c, col:col + 1]
                    V.scalar_tensor_tensor(out=he_buf[:, i % 2, :], in0=silu_buf[:, i % 2, :], scalar=gate,
                                           in1=ps[:, i % 2, D_EXPERT:2 * D_EXPERT], op0=ALU.mult, op1=ALU.mult).then_inc(s_he, 1)

                def rows_out(g, c):
                    gg = groups_before(l) + g
                    dve.wait_ge(s_y_ps, 8 * gg + 8 - c)
                    if gg:
                        dve.wait_ge(s_y_out[c], 16 * gg)
                    V.tensor_copy(y_moe[:, c, :], ps[:, 4 + 2 * c:6 + 2 * c, :].rearrange("p b n -> p (b n)")).then_inc(s_y[c], 1)

                def body(g, items):
                    for k in list(items)[1:]:
                        hidden(g, items, k)
                    if items is WHOLE:
                        rows_out(g, 1)
                    else:
                        dve.drain().then_inc(s_y[1], 1)

                dve.wait_ge(s_flags, l + 1)
                for g in range(N_GROUPS):
                    for c in range(2):
                        dve.wait_ge(s_slot[g % 2][c], 16 * (2 * l + g // 2 + 1))
                    hidden(g, WHOLE, 0)
                    if g:
                        rows_out(g - 1, 0)
                    second = dve.value_load(flags[0:1, g:g + 1], min_val=0, max_val=1)
                    with dve.If(second > 0):
                        body(g, WHOLE)
                    with dve.Else():
                        body(g, SHORT)
                rows_out(N_GROUPS - 1, 0)
                if group_passes[l] > N_GROUPS:
                    over = dve.value_load(flags[0:1, 4:5], min_val=0, max_val=1)
                    with dve.If(over > 0):
                        dve.wait_ge(s_over_slot, 32)
                        cols = slot_tok[:, 0, :, D:SLOT_W].rearrange("p c (g e) -> p c e g", g=N_GROUPS)
                        V.tensor_reduce(over_gate, cols, AX_X, ALU.add).then_inc(s_over_gate, 1)
                        dve.wait_ge(s_over_gate, 1)
                        hidden(N_GROUPS, WHOLE, 0)
                        body(N_GROUPS, WHOLE)
                        rows_out(N_GROUPS, 0)
                    with dve.Else():
                        dve.drain().then_inc(s_he, 8)
                        for c in range(2):
                            dve.drain().then_inc(s_y[c], 1)

            def combine(l):
                for t in range(NQ[l]):
                    dve.wait_ge(s_back[t], 16 * (l + 1))
                    chain(V.tensor_tensor(y_back[:, t, :], y_back[:, t, :], mod[:, GATE_Q, t // 2, :], ALU.mult))
                    V.tensor_tensor(x[:, t, :], x[:, t, :], y_back[:, t, :], ALU.add).then_inc(s_x2, 1)
                    if t and l + 1 < DEPTH:
                        scale_tiles(l + 1, 0, [t - 1])
                if l + 1 < DEPTH:
                    scale_tiles(l + 1, 0, [NT - 1])

            for u in range(4):
                rows(0, 0, u)
                if u:
                    bcast(0, 0, u - 1)
            bcast(0, 0, 3)
            dve.wait_ge(s_x, 16 * N_X)
            scale_tiles(0, 0, range(NT))
            for l in range(DEPTH):
                dve.wait_ge(s_const, 16 * N_CONST)
                rope_qk(l)
                keys_for_state(l)
                glu(l)
                if l:
                    dve.wait_ge(s_x2, before(l, NQ))
                if l == 0:
                    for u in (4, 5):
                        rows(l, 0, u)
                for u in (4, 5):
                    bcast(l, 0, u)
                queries_for_state(l)
                rows(l, 1, 4)
                norm_latents(l)
                taps(l)
                masks(l, 0)
                conv_centre(l)
                if RET_PASSES[l] == 2:
                    masks(l, 1)
                conv_scale(l)
                for t in range(2):
                    rope_q(l, t)
                if RET_PASSES[l] == 2:
                    for stage in range(3):
                        groupnorm(l, 0, stage)
                attention(l)
                for u in range(4):
                    bcast(l, 1, u)
                residual(l)
                route(l)
                dve.wait_ge(s_x1, 2 * before(l + 1, NQ))
                for u in (4, 5):
                    bcast(l, 1, u)
                if l + 1 < DEPTH:
                    dve.wait_ge(s_h, norm_base(l, 1) + NQ[l])
                    for u in range(4):
                        bcast(l + 1, 0, u)
                experts(l)
                combine(l)
            dve.wait_ge(s_normw, 16 * (2 * DEPTH + 1))
            for t in range(2):
                i = norm_base(DEPTH, 0) + t
                dve.wait_ge(s_rstd, i + 1)
                V.scalar_tensor_tensor(out=h_tok[:, i % 2, :], in0=x[:, t, :], scalar=rstd[:, t:t + 1],
                                       in1=norm_w, op0=ALU.mult, op1=ALU.mult).then_inc(s_final, 1)

        @block.gpsimd
        def _(pool):
            G = nc.gpsimd
            steps = [0]

            def chain(ins):
                steps[0] += 1
                ins.then_inc(s_pool, 1)
                pool.wait_ge(s_pool, steps[0])

            def inverse_root(v, n, eps):
                w = v.shape[-1]
                chain(G.tensor_scalar(v, v, 1.0 / n, eps, ALU.mult, ALU.add))
                return G.tensor_tensor(v, v, half_neg[:, 0:w], ALU.pow)

            def norm(l, a, tiles, shift=True):
                for t in range(tiles + (1 if shift else 0)):
                    if t < tiles:
                        pool.wait_ge(s_sumsq, norm_base(l, a) + t + 1)
                        inverse_root(rstd[:, t:t + 1], D, EPS).then_inc(s_rstd, 1)
                    if shift and t:
                        i = norm_base(l, a) + t - 1
                        pool.wait_ge(s_scaled, i + 1)
                        h = h_tok[:, i % 2, :]
                        G.tensor_tensor(h, h, mod[:, SHIFT_Q, (t - 1) // 2, :], ALU.add).then_inc(s_h, 1)

            def dispatch(l):
                pool.wait_ge(s_gates, l + 1)
                pool.wait_ge(s_filled, 16 * (SLOTS // P + 2))
                for t in range(NQ[l]):
                    pool.indirect_dma_start(out=slots, out_offset=bass.IndirectOffsetOnAxis(ap=slot_of[:, t:t + 1], axis=0),
                                            in_=h2[:, t, :], in_offset=None).then_inc(s_scattered, 16)

                def store(g, c):
                    gg = groups_before(l) + g
                    pool.wait_ge(s_y[c], gg + 1)
                    r0 = (2 * g + c) * P
                    pool.dma_start(y_slots[r0:r0 + P, :], y_moe[:, c, :]).then_inc(s_y_out[c], 16)

                def skip(g, c):
                    gg = groups_before(l) + g
                    pool.wait_ge(s_y[c], gg + 1)
                    r0 = (2 * g + c) * P
                    pool.dma_start(y_slots[r0:r0 + 1, 0:N_EXPERTS], y_moe[0:1, c, 0:N_EXPERTS]).then_inc(s_y_out[c], 16)

                pool.wait_ge(s_flags, l + 1)
                for g in range(N_GROUPS):
                    if l:
                        second = pool.value_load(flags[0:1, g:g + 1], min_val=0, max_val=1)
                        with pool.If(second > 0):
                            store(g, 1)
                        with pool.Else():
                            skip(g, 1)
                    else:
                        store(g, 1)
                    store(g, 0)
                if group_passes[l] > N_GROUPS:
                    over = pool.value_load(flags[0:1, 4:5], min_val=0, max_val=1)
                    with pool.If(over > 0):
                        for c in (1, 0):
                            store(N_GROUPS, c)
                    with pool.Else():
                        for c in (1, 0):
                            skip(N_GROUPS, c)
                for c in range(2):
                    pool.wait_ge(s_y_out[c], 16 * groups_before(l + 1))
                for t in range(NQ[l]):
                    pool.indirect_dma_start(out=y_back[:, t, :], out_offset=None, in_=y_slots,
                                            in_offset=bass.IndirectOffsetOnAxis(ap=slot_of[:, t:t + 1], axis=0)
                                            ).then_inc(s_back[t], 16)

            G.memset(ada_bias[:, :, :], 0.0).then_inc(s_bias_zero, 1)
            G.memset(c_pad[:, :, :], 0.0).then_inc(s_ones, 1)
            G.memset(zero_rows, 0.0).then_inc(s_fill, 1)
            for g in range(N_GROUPS):
                G.memset(group_slot[:, 0, g:g + 1], float(g * GROUP_SLOTS))
                G.memset(group_slot[:, 1, g:g + 1], float((N_GROUPS - 1 - g) * GROUP_SLOTS))
            G.memset(ones_mean[:, :], 1.0 / CONV_W)
            G.memset(eps_col[:, :], EPS)
            chain(G.memset(half_neg[:, :], -0.5))
            for l in range(DEPTH):
                norm(l, 0, NT)
                for e0 in (0, CONV_K // 2 + SEQ):
                    last = G.memset(conv_in[:, :, :, e0:e0 + CONV_K // 2], 0.0)
                last.then_inc(s_pad, 1)
                pool.wait_ge(s_mod, mod_at[(l, 0, 4, 0)])
                G.memset(state, 0.0).then_inc(s_state_zero, 1)
                for t in range(NT):
                    pool.wait_ge(s_lat_sq, NT * l + t + 1)
                    if t < NQ[l]:
                        chain(G.tensor_scalar(lat_rstd[:, t, 0:1], lat_sumsq[:, t, 0:1], 1.0 / Q_RANK, EPS, ALU.mult, ALU.add))
                    chain(G.tensor_scalar(lat_rstd[:, t, 1:2], lat_sumsq[:, t, 1:2], 1.0 / KV_RANK, EPS, ALU.mult, ALU.add))
                    v = lat_rstd[:, t, 0 if t < NQ[l] else 1:2]
                    G.tensor_tensor(v, v, half_neg[:, 0:v.shape[-1]], ALU.pow).then_inc(s_lat_rstd, 1)
                pool.wait_ge(s_latT, lat_evacs(l, NT))
                for h in range(1, HEADS):
                    last = G.tensor_copy(KT[D_NOPE:D_QK, h, :], KT[D_NOPE:D_QK, 0, :])
                last.then_inc(s_kr, 1)
                pool.wait_ge(s_kr, l + 1)
                for s in range(RET_PASSES[l]):
                    g0 = 2 * (before(l, RET_PASSES) + s)
                    for i in range(2):
                        pool.wait_ge(s_gn_var, g0 + i + 1)
                        inverse_root(gn_rstd[:, i, :], RET_DV, GN_EPS).then_inc(s_gn_rstd, 1)
                    for i in range(2):
                        t = 2 * s + i
                        pool.wait_ge(s_gn_norm, g0 + i + 1)
                        for f in range(2):
                            last = G.tensor_tensor(gate_act[:, f, t, :], gate_act[:, f, t, :],
                                                   gn_y[:, i, 6 * f:6 * f + 6, :].rearrange("p h n -> p (h n)"), ALU.mult)
                        chain(last)
                        G.tensor_tensor(gate_act[:, 0, t, :], gate_act[:, 0, t, :], gate_act[:, 1, t, :],
                                        ALU.add).then_inc(s_ret_out, 1)
                norm(l, 1, NQ[l], shift=False)
                dispatch(l)
            norm(DEPTH, 0, 2, shift=False)


def _constants():
    import numpy as np

    ident = np.eye(P, dtype=np.float32)
    sel = np.zeros((P, 2, P), np.float32)
    for s in range(2):
        sel[s::32, s, :] = 1.0
    p = np.arange(P)[:, None, None].astype(np.float64)
    n = np.arange(SEQ)[None, None, :]
    g = gamma(np.arange(HEADS, dtype=np.float64))[None, :, None]
    fwd, bwd = n - p, p + P - n
    decay = np.stack([np.where(fwd >= 0, g ** np.maximum(fwd, 0), 0.0),
                      np.where(bwd >= 0, g[:, ::-1] ** np.maximum(bwd, 0), 0.0)], axis=1).astype(np.float32)
    heads = np.arange(HEADS, dtype=np.float64)
    j = np.arange(SEQ).reshape(2, P).T[:, :, None].astype(np.float64)
    k_decay = np.stack([gamma(heads) ** (SEQ - j), gamma(heads[::-1]) ** j], axis=1) * RET_DK ** -0.5
    q_decay = np.zeros((P, 2, 2, SEQ))
    i = np.arange(SEQ, dtype=np.float64)
    for h in range(HEADS):
        rows = slice(32 * (h % 4), 32 * (h % 4) + 32)
        q_decay[rows, h // 4, 0] = gamma(h) ** i
        q_decay[rows, h // 4, 1] = gamma(HEADS - 1 - h) ** (SEQ - i)
    t = np.arange(SEQ).reshape(2, P)
    inv = 10000.0 ** (-np.arange(8, dtype=np.float64) / 8)
    rope = np.zeros((P, 2, 2, D_ROPE), np.float32)
    for i in range(2):
        for g2, pos in enumerate((t[i] // 64, t[i] % 64)):
            ang = pos[:, None] * inv
            for b in range(2):
                cols = slice(16 * g2 + 8 * b, 16 * g2 + 8 * b + 8)
                rope[:, i, 0, cols] = np.cos(ang)
                rope[:, i, 1, cols] = np.sin(ang) * (1 if b else -1)
    rank = np.broadcast_to(np.arange(N_EXPERTS, 0, -1, dtype=np.float32), (P, N_EXPERTS)).copy()
    tri = np.triu(np.ones((P, P), np.float32), 1) / CONV_W
    return {"const_ident": ident, "const_tri": tri, "const_sel": sel, "const_decay": decay,
            "const_k_decay": k_decay.astype(np.float32), "const_q_decay": q_decay.astype(np.float32),
            "const_rope": rope, "const_rank": rank}


_INS = ["x", "c", "ctx", "c_ctx", "ada_w", "ada_b", "norm1_w", "norm2_w", "w_in",
        "mla_w_uq", "mla_kv_norm_w", "mla_w_ukv", "w_out", "router_w", "router_bias", "moe_w_gate",
        "moe_w_up", "moe_w_down", "final_norm_w"]


def kernel(**inputs):
    import numpy as np
    import concourse.bacc as bacc
    from concourse.bass_utils import run_bass_kernel_spmd

    nc = bacc.Bacc("TRN2", target_bir_lowering=False, num_devices=1, dynamic_dma_scratch_size=2048)
    arrays = {name: np.ascontiguousarray(inputs[name]) for name in _INS}
    cols = np.concatenate([np.asarray(inputs["conv_dw"])] +
                          [np.asarray(inputs[name])[:, None] for name in ("conv_b", "conv_ln_w", "conv_ln_b")], axis=1)
    arrays["conv_cols"] = np.ascontiguousarray(cols.reshape(DEPTH, CONV_K + 3, 2, P).transpose(0, 3, 2, 1))
    arrays["q_norm_cols"] = np.ascontiguousarray(np.asarray(inputs["mla_q_norm_w"]).reshape(DEPTH, 2, 96).transpose(0, 2, 1))
    arrays.update(_constants())
    dram = {name: nc.dram_tensor(f"in_{name}", a.shape, mybir.dt.from_np(a.dtype), kind="ExternalInput").ap()
            for name, a in arrays.items()}
    out = nc.dram_tensor("out_0", (1, SEQ, D), F32, kind="ExternalOutput").ap()
    build(nc, dram, out)
    r = run_bass_kernel_spmd(nc, [{f"in_{name}": a for name, a in arrays.items()}], core_ids=[0])
    return r.results[0]["out_0"]
```
